# Optimizing a Trainium2 kernel written in Bass

```python
import jax, jax.numpy as jnp
from jax import lax
import numpy as np

D_MODEL = 1024
BATCH = 1
SEQ = 256
DEPTH = 2

D_MIX = D_MODEL
HG_HEADS = 4
HG_DK = 128
HG_DV = 128
HG_W = HG_HEADS * HG_DV
HG_CHUNK = 64
NSA_HEADS = 8
NSA_KV_HEADS = 2
NSA_DH = 64
NSA_G = NSA_HEADS // NSA_KV_HEADS
NSA_W = NSA_HEADS * NSA_DH
KV_W = NSA_KV_HEADS * NSA_DH
CMP_BLOCK = 32
CMP_STRIDE = 16
CMP_HIDDEN = 128
SLC_BLOCK = 64
SLC_TOPK = 16
SLC_Q_BLOCK = 64
WINDOW = 512
Q_BLOCK = 128
FORCE_SCORE = 1e4
ROPE_THETA = 500000.0
ROPE_DIM = NSA_DH // 4
PLE_DIM = 256
RMS_EPS = 1e-6
IN_SPLITS = (HG_W,) * 5 + (NSA_W,) + (KV_W,) * 6 + (3 * NSA_HEADS, NSA_W)
IN_COLS = 5 * HG_W + NSA_W + 6 * KV_W + 3 * NSA_HEADS + NSA_W


def rmsnorm(x, g):
    xf = x.astype(jnp.float32)
    var = jnp.mean(xf * xf, axis=-1, keepdims=True)
    return (xf * lax.rsqrt(var + RMS_EPS)).astype(x.dtype) * g

def masked_softmax(s, mask):
    s = jnp.where(mask, s.astype(jnp.float32), -jnp.inf)
    m = jnp.max(s, axis=-1, keepdims=True)
    m = jnp.where(jnp.isfinite(m), m, 0.0)
    e = jnp.where(mask, jnp.exp(s - m), 0.0)
    return e / jnp.maximum(jnp.sum(e, axis=-1, keepdims=True), 1e-30)

def rope_tables(seq):
    pos = jnp.arange(seq, dtype=jnp.float32)
    inv = ROPE_THETA ** (-jnp.arange(0, ROPE_DIM, 2, dtype=jnp.float32) / ROPE_DIM)
    ang = pos[:, None] * inv[None, :]
    return jnp.cos(ang), jnp.sin(ang)

def partial_rope(x, cos, sin):
    half = ROPE_DIM // 2
    x1, x2, xp = x[..., :half], x[..., half:ROPE_DIM], x[..., ROPE_DIM:]
    c = cos.astype(x.dtype)
    s = sin.astype(x.dtype)
    return jnp.concatenate([x1 * c - x2 * s, x1 * s + x2 * c, xp], axis=-1)

def heads(a, n):
    B, T, W = a.shape
    return a.reshape(B, T, n, W // n).transpose(0, 2, 1, 3)

def hgrn2_chunkwise(q, log_f, k, v):
    B, H, T, DK = q.shape
    DV = v.shape[-1]
    C = HG_CHUNK
    N = T // C

    def to_chunks(a):
        return jnp.moveaxis(a.reshape(B, H, N, C, a.shape[-1]), 2, 0)

    causal = jnp.tril(jnp.ones((C, C), dtype=bool))[:, :, None]

    def step(S, inp):
        qi, lfi, ki, vi = inp
        b = jnp.cumsum(lfi.astype(jnp.float32), axis=-2)
        diff = b[..., :, None, :] - b[..., None, :, :]
        decay = jnp.exp(jnp.where(causal, diff, -jnp.inf))
        A = jnp.einsum('bhtd,bhsd,bhtsd->bhts', qi, ki, decay)
        o = jnp.einsum('bhts,bhsv->bhtv', A, vi) + jnp.einsum('bhtd,bhdv->bhtv', qi * jnp.exp(b), S)
        b_last = b[..., -1:, :]
        S_new = jnp.exp(b_last[..., 0, :])[..., None] * S + jnp.einsum(
            'bhsd,bhsv->bhdv', ki * jnp.exp(b_last - b), vi)
        return S_new, o

    S0 = jnp.zeros((B, H, DK, DV), jnp.float32)
    _, o = lax.scan(step, S0, (to_chunks(q), to_chunks(log_f), to_chunks(k), to_chunks(v)))
    return jnp.moveaxis(o, 0, 2).reshape(B, H, T, DV).astype(v.dtype)

def compress(kv, pe, w1, w2):
    B, G, T, dh = kv.shape
    NC = (T - CMP_BLOCK) // CMP_STRIDE + 1
    idx = jnp.arange(NC)[:, None] * CMP_STRIDE + jnp.arange(CMP_BLOCK)[None, :]
    blocks = kv[:, :, idx, :] + pe
    flat = blocks.reshape(B, G, NC, CMP_BLOCK * dh)
    return jax.nn.silu(flat @ w1) @ w2

def window_attn(q, k, v, scale):
    B, KVH, G, T, dh = q.shape
    NB = T // Q_BLOCK
    NW = WINDOW // Q_BLOCK
    pad = ((0, 0), (0, 0), (WINDOW, 0), (0, 0))
    kb = jnp.pad(k, pad).reshape(B, KVH, NB + NW, Q_BLOCK, dh)
    vb = jnp.pad(v, pad).reshape(B, KVH, NB + NW, Q_BLOCK, dh)
    band_k = jnp.concatenate([kb[:, :, i:i + NB] for i in range(NW + 1)], axis=3)
    band_v = jnp.concatenate([vb[:, :, i:i + NB] for i in range(NW + 1)], axis=3)
    qb = q.reshape(B, KVH, G, NB, Q_BLOCK, dh)
    s = jnp.einsum('bgnxqd,bgxkd->bgnxqk', qb, band_k) * scale
    qpos = jnp.arange(NB)[:, None] * Q_BLOCK + jnp.arange(Q_BLOCK)[None, :]
    kpos = jnp.arange(NB)[:, None] * Q_BLOCK - WINDOW + jnp.arange((NW + 1) * Q_BLOCK)[None, :]
    d = qpos[:, :, None] - kpos[:, None, :]
    mask = (d >= 0) & (d < WINDOW) & (kpos[:, None, :] >= 0)
    p = masked_softmax(s, mask)
    o = jnp.einsum('bgnxqk,bgxkd->bgnxqd', p.astype(v.dtype), band_v)
    return o.reshape(B, KVH, G, T, dh)

def selected_attn(q, k, v, sel, scale):
    B, KVH, G, T, dh = q.shape
    K = sel.shape[-1]
    NB = T // SLC_Q_BLOCK
    qb = jnp.moveaxis(q.reshape(B, KVH, G, NB, SLC_Q_BLOCK, dh), 3, 0)
    sb = jnp.moveaxis(sel.reshape(B, KVH, NB, SLC_Q_BLOCK, K), 2, 0)
    t0 = jnp.arange(NB) * SLC_Q_BLOCK
    bi = jnp.arange(B)[:, None, None, None]
    gi = jnp.arange(KVH)[None, :, None, None]

    def one(args):
        qx, sx, s0 = args
        tok = (sx[..., None] * SLC_BLOCK + jnp.arange(SLC_BLOCK)).reshape(B, KVH, SLC_Q_BLOCK, K * SLC_BLOCK)
        kg = k[bi, gi, tok]
        vg = v[bi, gi, tok]
        s = jnp.einsum('bgnqd,bgqkd->bgnqk', qx, kg) * scale
        qpos = s0 + jnp.arange(SLC_Q_BLOCK)
        mask = (tok <= qpos[:, None])[:, :, None]
        p = masked_softmax(s, mask)
        return jnp.einsum('bgnqk,bgqkd->bgnqd', p.astype(vg.dtype), vg)

    o = lax.map(one, (qb, sb, t0))
    return jnp.moveaxis(o, 0, 3).reshape(B, KVH, G, T, dh)

def first_inputs(seed: int = 0) -> dict:
    key = jax.random.key(seed)
    ks = jax.random.split(key, 16)
    n = jax.random.normal
    f32 = jnp.float32
    return {
        "x": n(ks[0], (BATCH, SEQ, D_MODEL), f32),
        "p": n(ks[1], (DEPTH, BATCH, SEQ, PLE_DIM), f32),
        "norm_g": 1.0 + 0.05 * n(ks[2], (DEPTH, D_MODEL), f32),
        "w_in": n(ks[3], (DEPTH, D_MODEL, IN_COLS), f32) * D_MODEL ** -0.5,
        "hgrn_lb": 0.5 * n(ks[4], (DEPTH, HG_HEADS * HG_DK), f32),
        "hgrn_onorm_g": 1.0 + 0.05 * n(ks[5], (DEPTH, HG_DV), f32),
        "nsa_qnorm_g": 1.0 + 0.05 * n(ks[6], (DEPTH, NSA_DH), f32),
        "nsa_knorm_g": 1.0 + 0.05 * n(ks[7], (DEPTH, 3, NSA_DH), f32),
        "cmp_pe": 0.1 * n(ks[8], (DEPTH, 2, CMP_BLOCK, NSA_DH), f32),
        "cmp_w1": n(ks[9], (DEPTH, 2, CMP_BLOCK * NSA_DH, CMP_HIDDEN), f32) * (CMP_BLOCK * NSA_DH) ** -0.5,
        "cmp_w2": n(ks[10], (DEPTH, 2, CMP_HIDDEN, NSA_DH), f32) * CMP_HIDDEN ** -0.5,
        "w_out": n(ks[11], (DEPTH, D_MIX, D_MODEL), f32) * (0.5 * D_MIX ** -0.5),
        "ple_norm_g": 1.0 + 0.05 * n(ks[12], (DEPTH, D_MODEL), f32),
        "w_pg": n(ks[13], (DEPTH, D_MODEL, D_MODEL), f32) * D_MODEL ** -0.5,
        "w_pp": n(ks[14], (DEPTH, PLE_DIM, D_MODEL), f32) * (0.5 * PLE_DIM ** -0.5),
    }

def first_block(x, p, norm_g, w_in, hgrn_lb, hgrn_onorm_g, nsa_qnorm_g, nsa_knorm_g,
              cmp_pe, cmp_w1, cmp_w2, w_out, ple_norm_g, w_pg, w_pp):
    B, T, _ = x.shape
    KVH, G, dh = NSA_KV_HEADS, NSA_G, NSA_DH
    scale = dh ** -0.5
    split_points = np.cumsum(IN_SPLITS)[:-1].tolist()

    cos, sin = rope_tables(T)
    lb_all = jnp.cumsum(jax.nn.softmax(hgrn_lb.astype(jnp.float32), axis=0), axis=0)
    lb_all = lb_all - lb_all[0]

    NC = (T - CMP_BLOCK) // CMP_STRIDE + 1
    NSB = T // SLC_BLOCK
    top_k = min(SLC_TOPK, NSB)
    c_tok = jnp.arange(NC)[:, None] * CMP_STRIDE + jnp.arange(CMP_BLOCK)[None, :]
    overlap = jnp.mean((c_tok[..., None] // SLC_BLOCK == jnp.arange(NSB)).astype(jnp.float32), axis=1)
    c_end = jnp.arange(NC) * CMP_STRIDE + CMP_BLOCK - 1
    cmp_mask = c_end[None, :] <= jnp.arange(T)[:, None]
    cur = (jnp.arange(T) // SLC_BLOCK)[:, None]
    jb = jnp.arange(NSB)[None, :]
    forced = (jb == 0) | (jb == cur) | (jb == cur - 1)
    eligible = jb <= cur

    h = x
    for i in range(DEPTH):
        xn = rmsnorm(h, norm_g[i])
        proj = xn @ w_in[i]
        (hq, hf, hi, hgo, hz, nq, kcm, vcm, ksl, vsl, kwn, vwn, ngate, nz) = jnp.split(proj, split_points, axis=-1)

        lb = lb_all[i].reshape(HG_HEADS, 1, HG_DK)
        fl = heads(hf, HG_HEADS).astype(jnp.float32)
        log_f = jnp.logaddexp(jnp.log(lb), jnp.log1p(-lb) + jax.nn.log_sigmoid(fl))
        k_hg = (1.0 - lb) * jax.nn.sigmoid(-fl)
        o_hg = hgrn2_chunkwise(heads(hq, HG_HEADS), log_f, k_hg, heads(hi, HG_HEADS))
        o_hg = rmsnorm(o_hg, hgrn_onorm_g[i]).transpose(0, 2, 1, 3).reshape(B, T, HG_W)
        y_hg = o_hg * jax.nn.sigmoid(hgo) * jax.nn.silu(hz)

        qn = rmsnorm(heads(nq, NSA_HEADS), nsa_qnorm_g[i])
        q_nope = qn.reshape(B, KVH, G, T, dh)
        q_rope = partial_rope(qn, cos, sin).reshape(B, KVH, G, T, dh)

        kc = rmsnorm(compress(heads(kcm, KVH), cmp_pe[i, 0], cmp_w1[i, 0], cmp_w2[i, 0]), nsa_knorm_g[i, 0])
        vc = compress(heads(vcm, KVH), cmp_pe[i, 1], cmp_w1[i, 1], cmp_w2[i, 1])
        s_cmp = jnp.einsum('bgntd,bgcd->bgntc', q_nope, kc) * scale
        p_cmp = masked_softmax(s_cmp, cmp_mask)
        o_cmp = jnp.einsum('bgntc,bgcd->bgntd', p_cmp.astype(vc.dtype), vc)

        imp = jnp.einsum('bgntc,cj->bgtj', p_cmp, overlap)
        score = jnp.where(forced, FORCE_SCORE, jnp.where(eligible, imp, -1.0))
        _, sel = lax.top_k(score, top_k)
        k_sl = partial_rope(rmsnorm(heads(ksl, KVH), nsa_knorm_g[i, 1]), cos, sin)
        o_slc = selected_attn(q_rope, k_sl, heads(vsl, KVH), sel, scale)

        k_wn = partial_rope(rmsnorm(heads(kwn, KVH), nsa_knorm_g[i, 2]), cos, sin)
        o_win = window_attn(q_rope, k_wn, heads(vwn, KVH), scale)

        gates = jax.nn.sigmoid(ngate).reshape(B, T, 3, KVH, G).transpose(2, 0, 3, 4, 1)[..., None]
        o_nsa = gates[0] * o_cmp + gates[1] * o_slc + gates[2] * o_win
        o_nsa = o_nsa.reshape(B, NSA_HEADS, T, dh).transpose(0, 2, 1, 3).reshape(B, T, NSA_W)
        y_nsa = o_nsa * jax.nn.silu(nz)

        h = h + jnp.concatenate([y_hg, y_nsa], axis=-1) @ w_out[i]

        gate = jax.nn.sigmoid(rmsnorm(h, ple_norm_g[i]) @ w_pg[i])
        h = h + gate * (p[i] @ w_pp[i])
    return h


N_EVEN = (DEPTH + 1) // 2
N_ODD = DEPTH // 2

LRU_WIDTH = D_MODEL // 2
LRU_HEADS = 8
LRU_HEAD_DIM = LRU_WIDTH // LRU_HEADS
LRU_CONV = 4
LRU_C = 8.0
LRU_MIN_RAD = 0.9
LRU_MAX_RAD = 0.999
SC_WIDTH = D_MODEL // 2
SC_CONV = 3
EVEN_IN = 2 * LRU_WIDTH + 3 * SC_WIDTH

SGU_WIDTH = D_MODEL // 2
SGU_HEADS = 8
SGU_HEAD_DIM = SGU_WIDTH // SGU_HEADS
CHUNK = 128
FOX_HEADS = 8
FOX_HEAD_DIM = 64
FOX_WIDTH = FOX_HEADS * FOX_HEAD_DIM
ODD_IN = 2 * SGU_WIDTH + 3 * FOX_WIDTH + FOX_HEADS

D_FF = 2816
FFN_CONV = 3
EPS = 1e-6


def rmsnorm_2(x, g):
    xf = x.astype(jnp.float32)
    y = xf * lax.rsqrt(jnp.mean(xf * xf, axis=-1, keepdims=True) + EPS)
    return (y * g.astype(jnp.float32)).astype(x.dtype)

def causal_depthwise_conv(x, w, b):
    k_width, ch = w.shape
    out = lax.conv_general_dilated(
        x, w[:, None, :].astype(x.dtype), window_strides=(1,),
        padding=[(k_width - 1, 0)], dimension_numbers=('NWC', 'WIO', 'NWC'),
        feature_group_count=ch)
    return out + b.astype(x.dtype)

def rg_lru(x, w_a, b_a, w_x, b_x, lam):
    bsz, s, w = x.shape
    xh = x.reshape(bsz, s, LRU_HEADS, LRU_HEAD_DIM)
    r = jax.nn.sigmoid((jnp.einsum('bshi,hij->bshj', xh, w_a).reshape(bsz, s, w) + b_a).astype(jnp.float32))
    i = jax.nn.sigmoid((jnp.einsum('bshi,hij->bshj', xh, w_x).reshape(bsz, s, w) + b_x).astype(jnp.float32))
    log_a = -LRU_C * r * jax.nn.softplus(-lam.astype(jnp.float32))
    a = jnp.exp(log_a)
    u = jnp.sqrt(-jnp.expm1(2.0 * log_a)) * (i * x.astype(jnp.float32))

    def combine(left, right):
        a_l, h_l = left
        a_r, h_r = right
        return a_l * a_r, a_r * h_l + h_r

    _, h = lax.associative_scan(combine, (a, u), axis=1)
    return h.astype(x.dtype)

def even_mixer(x, w_in, lru_conv_w, lru_conv_b, lru_wa, lru_ba, lru_wx, lru_bx, lru_lambda,
               sconv_w, sconv_b, w_out):
    p = x @ w_in
    W, C = LRU_WIDTH, SC_WIDTH
    xa, ga, c_pre, b_post, vb = jnp.split(p, [W, 2 * W, 2 * W + C, 2 * W + 2 * C], axis=-1)
    xa = causal_depthwise_conv(xa, lru_conv_w, lru_conv_b)
    ya = rg_lru(xa, lru_wa, lru_ba, lru_wx, lru_bx, lru_lambda) * jax.nn.gelu(ga)
    yb = b_post * causal_depthwise_conv(c_pre * vb, sconv_w, sconv_b)
    return jnp.concatenate([ya, yb], axis=-1) @ w_out

def chunked_spatial_gating(u, g, g_norm, w_s, b_s):
    bsz, s, _ = u.shape
    n_chunks = s // CHUNK
    gv = rmsnorm_2(g.reshape(bsz, s, SGU_HEADS, SGU_HEAD_DIM), g_norm.reshape(SGU_HEADS, SGU_HEAD_DIM))
    gv = gv.reshape(bsz, n_chunks, CHUNK, SGU_HEADS, SGU_HEAD_DIM)
    w_causal = jnp.tril(w_s)
    mixed = jnp.einsum('gts,bnsgc->bntgc', w_causal, gv) + b_s.T[:, :, None]
    return u * mixed.reshape(bsz, s, SGU_WIDTH)

def forgetting_attention(q, k, v, f_logit, b_f):
    bsz, s, _ = q.shape
    nb = s // Q_BLOCK

    def heads(t):
        return t.reshape(bsz, s, FOX_HEADS, FOX_HEAD_DIM).transpose(0, 2, 1, 3)

    q, k, v = heads(q), heads(k), heads(v)
    log_f = jax.nn.log_sigmoid(f_logit.astype(jnp.float32) + b_f.astype(jnp.float32))
    c = jnp.cumsum(log_f, axis=1).transpose(0, 2, 1)
    q_blocks = q.reshape(bsz, FOX_HEADS, nb, Q_BLOCK, FOX_HEAD_DIM).transpose(2, 0, 1, 3, 4)
    c_blocks = c.reshape(bsz, FOX_HEADS, nb, Q_BLOCK).transpose(2, 0, 1, 3)
    starts = jnp.arange(nb) * Q_BLOCK
    key_pos = jnp.arange(s)
    scale = FOX_HEAD_DIM ** -0.5

    def block(args):
        qb, cb, start = args
        logits = (jnp.einsum('bhqd,bhkd->bhqk', qb, k).astype(jnp.float32) * scale
                  + cb[..., None] - c[:, :, None, :])
        q_pos = start + jnp.arange(Q_BLOCK)
        logits = jnp.where(key_pos[None, :] <= q_pos[:, None], logits, -jnp.inf)
        p = jax.nn.softmax(logits, axis=-1)
        return jnp.einsum('bhqk,bhkd->bhqd', p.astype(v.dtype), v)

    out = lax.map(block, (q_blocks, c_blocks, starts))
    return out.transpose(1, 0, 3, 2, 4).reshape(bsz, s, FOX_WIDTH)

def odd_mixer(x, w_in, sgu_norm, sgu_w, sgu_b, fox_bf, w_out):
    p = x @ w_in
    Z, F = 2 * SGU_WIDTH, FOX_WIDTH
    z, q, k, v, f = jnp.split(p, [Z, Z + F, Z + 2 * F, Z + 3 * F], axis=-1)
    z = jax.nn.gelu(z)
    u, g = jnp.split(z, 2, axis=-1)
    yc = chunked_spatial_gating(u, g, sgu_norm, sgu_w, sgu_b)
    yd = forgetting_attention(q, k, v, f, fox_bf)
    return jnp.concatenate([yc, yd], axis=-1) @ w_out

def conv_glu_ffn(x, w_up, conv_w, conv_b, w_down):
    h = causal_depthwise_conv(x @ w_up, conv_w, conv_b)
    gate, val = jnp.split(h, 2, axis=-1)
    return (jax.nn.silu(gate) * val) @ w_down

def second_inputs(seed: int = 0) -> dict:
    key = jax.random.key(seed)
    ks = jax.random.split(key, 32)
    f32 = jnp.float32

    def dense(k, shape, fan_in):
        return jax.random.normal(k, shape, f32) * fan_in ** -0.5

    def gain(k, shape):
        return 1.0 + 0.05 * jax.random.normal(k, shape, f32)

    def bias(k, shape):
        return 0.1 * jax.random.normal(k, shape, f32)

    a_c = jax.random.uniform(ks[9], (N_EVEN, LRU_WIDTH), f32, LRU_MIN_RAD, LRU_MAX_RAD)
    s_base = a_c ** (1.0 / LRU_C)
    lru_lambda = jnp.log(s_base) - jnp.log1p(-s_base)

    return {
        "x": jax.random.normal(ks[0], (BATCH, SEQ, D_MODEL), f32),
        "mix0_norm": gain(ks[1], (N_EVEN, D_MODEL)),
        "mix0_w_in": dense(ks[2], (N_EVEN, D_MODEL, EVEN_IN), D_MODEL),
        "lru_conv_w": dense(ks[3], (N_EVEN, LRU_CONV, LRU_WIDTH), LRU_CONV),
        "lru_conv_b": bias(ks[4], (N_EVEN, LRU_WIDTH)),
        "lru_wa": dense(ks[5], (N_EVEN, LRU_HEADS, LRU_HEAD_DIM, LRU_HEAD_DIM), LRU_HEAD_DIM),
        "lru_ba": bias(ks[6], (N_EVEN, LRU_WIDTH)),
        "lru_wx": dense(ks[7], (N_EVEN, LRU_HEADS, LRU_HEAD_DIM, LRU_HEAD_DIM), LRU_HEAD_DIM),
        "lru_bx": bias(ks[8], (N_EVEN, LRU_WIDTH)),
        "lru_lambda": lru_lambda,
        "sconv_w": dense(ks[10], (N_EVEN, SC_CONV, SC_WIDTH), SC_CONV),
        "sconv_b": bias(ks[11], (N_EVEN, SC_WIDTH)),
        "mix0_w_out": dense(ks[12], (N_EVEN, LRU_WIDTH + SC_WIDTH, D_MODEL), LRU_WIDTH + SC_WIDTH),
        "mix1_norm": gain(ks[13], (N_ODD, D_MODEL)),
        "mix1_w_in": dense(ks[14], (N_ODD, D_MODEL, ODD_IN), D_MODEL),
        "sgu_norm": gain(ks[15], (N_ODD, SGU_WIDTH)),
        "sgu_w": dense(ks[16], (N_ODD, SGU_HEADS, CHUNK, CHUNK), CHUNK),
        "sgu_b": 1.0 + bias(ks[17], (N_ODD, SGU_HEADS, CHUNK)),
        "fox_bf": bias(ks[18], (N_ODD, FOX_HEADS)),
        "mix1_w_out": dense(ks[19], (N_ODD, SGU_WIDTH + FOX_WIDTH, D_MODEL), SGU_WIDTH + FOX_WIDTH),
        "ffn_norm": gain(ks[20], (DEPTH, D_MODEL)),
        "ffn_up": dense(ks[21], (DEPTH, D_MODEL, 2 * D_FF), D_MODEL),
        "ffn_conv_w": dense(ks[22], (DEPTH, FFN_CONV, 2 * D_FF), FFN_CONV),
        "ffn_conv_b": bias(ks[23], (DEPTH, 2 * D_FF)),
        "ffn_down": dense(ks[24], (DEPTH, D_FF, D_MODEL), D_FF),
        "final_norm": gain(ks[25], (D_MODEL,)),
    }

def second_block(x, mix0_norm, mix0_w_in, lru_conv_w, lru_conv_b, lru_wa, lru_ba, lru_wx, lru_bx,
              lru_lambda, sconv_w, sconv_b, mix0_w_out, mix1_norm, mix1_w_in, sgu_norm, sgu_w,
              sgu_b, fox_bf, mix1_w_out, ffn_norm, ffn_up, ffn_conv_w, ffn_conv_b, ffn_down,
              final_norm):
    h = x
    for layer in range(DEPTH):
        i = layer // 2
        if layer % 2 == 0:
            h = h + even_mixer(rmsnorm_2(h, mix0_norm[i]), mix0_w_in[i], lru_conv_w[i], lru_conv_b[i],
                               lru_wa[i], lru_ba[i], lru_wx[i], lru_bx[i], lru_lambda[i],
                               sconv_w[i], sconv_b[i], mix0_w_out[i])
        else:
            h = h + odd_mixer(rmsnorm_2(h, mix1_norm[i]), mix1_w_in[i], sgu_norm[i], sgu_w[i],
                              sgu_b[i], fox_bf[i], mix1_w_out[i])
        h = h + conv_glu_ffn(rmsnorm_2(h, ffn_norm[layer]), ffn_up[layer], ffn_conv_w[layer],
                             ffn_conv_b[layer], ffn_down[layer])
    return rmsnorm_2(h, final_norm)


def setup_inputs(seed=0):
    out = dict(first_inputs(seed))
    for name, value in second_inputs(seed + 1).items():
        if name != "x":
            out[name + "_2"] = value
    return out


def reference(
    x, p, norm_g, w_in, hgrn_lb, hgrn_onorm_g, nsa_qnorm_g, nsa_knorm_g, cmp_pe, cmp_w1, cmp_w2,
    w_out, ple_norm_g, w_pg, w_pp, mix0_norm_2, mix0_w_in_2, lru_conv_w_2, lru_conv_b_2,
    lru_wa_2, lru_ba_2, lru_wx_2, lru_bx_2, lru_lambda_2, sconv_w_2, sconv_b_2, mix0_w_out_2,
    mix1_norm_2, mix1_w_in_2, sgu_norm_2, sgu_w_2, sgu_b_2, fox_bf_2, mix1_w_out_2, ffn_norm_2,
    ffn_up_2, ffn_conv_w_2, ffn_conv_b_2, ffn_down_2, final_norm_2,
):
    x = first_block(
        x, p, norm_g, w_in, hgrn_lb, hgrn_onorm_g, nsa_qnorm_g, nsa_knorm_g, cmp_pe, cmp_w1,
        cmp_w2, w_out, ple_norm_g, w_pg, w_pp,
    )
    return second_block(
        x, mix0_norm_2, mix0_w_in_2, lru_conv_w_2, lru_conv_b_2, lru_wa_2, lru_ba_2, lru_wx_2,
        lru_bx_2, lru_lambda_2, sconv_w_2, sconv_b_2, mix0_w_out_2, mix1_norm_2, mix1_w_in_2,
        sgu_norm_2, sgu_w_2, sgu_b_2, fox_bf_2, mix1_w_out_2, ffn_norm_2, ffn_up_2,
        ffn_conv_w_2, ffn_conv_b_2, ffn_down_2, final_norm_2,
    )


_drawn_inputs = setup_inputs


def setup_inputs(seed=0):
    import zlib

    import numpy as np

    out = dict(_drawn_inputs(seed))
    spreads = {}
    factors = {'hgrn_onorm_g': 4.602,
     'nsa_qnorm_g': 8.0,
     'nsa_knorm_g': 8.0,
     'cmp_pe': 4.902,
     'ple_norm_g': 5.378,
     'lru_ba_2': 8.0,
     'lru_bx_2': 5.257,
     'sgu_norm_2': 5.59,
     'fox_bf_2': 4.945,
     'sgu_b_2': 2.892}
    for name, (base, spread) in spreads.items():
        noise = np.random.default_rng([zlib.crc32(name.encode()), seed]).standard_normal(out[name].shape)
        drawn = base * np.exp(spread * noise) if base else spread * noise
        out[name] = __import__('jax').numpy.asarray(drawn.astype(out[name].dtype))
    for name, factor in factors.items():
        out[name] = (out[name] * factor).astype(out[name].dtype)
    return out
```

```python
from contextlib import ExitStack

import numpy as np

import concourse.bass as bass
from concourse import mybir

P = 128
T = 256
NT = T // P
D = 1024
ND = D // P
DEPTH = 2
HALF = 512
NH4 = HALF // P
IN1 = 4376
PLE = 256
FF = 2816
NFF = FF // P
FF_ROUNDS = NFF // 2
NCMP = 15
EPS = 1e-6
NEG = -1e30
SLOTS = 4
PANEL = 4096
NLVL = 8

ALU = mybir.AluOpType
ACT = mybir.ActivationFunctionType
F32 = mybir.dt.float32
BF16 = mybir.dt.bfloat16
I32 = mybir.dt.int32
AX_X = mybir.AxisListType.X
LOG_EXP = "natural_log_exp_and_others"

CONST_COLS = {}


def const_table():
    p = np.arange(P)
    parts = [("ident", np.eye(P)), ("ones", np.ones((P, P))),
             ("head_ones", (p[:, None] // 64 == p[None, :] // 64).astype(float))]
    rot = np.zeros((P, P))
    for h in (0, 64):
        for d in range(8):
            rot[h + 8 + d, h + d] = -1.0
            rot[h + d, h + 8 + d] = 1.0
    parts.append(("rot", rot))
    inv = (np.float32(500000.0) ** (-np.arange(0, 16, 2, dtype=np.float32) / np.float32(16))).astype(np.float32)
    ang = np.arange(T, dtype=np.float32)[None, :] * inv[:, None]
    cos, sin = np.ones((P, T)), np.zeros((P, T))
    for h in (0, 8, 64, 72):
        cos[h:h + 8] = np.cos(ang.astype(np.float32))
        sin[h:h + 8] = np.sin(ang.astype(np.float32))
    parts += [("cos", cos), ("sin", sin)]
    t = p[:, None, None] + P * np.arange(NT)[None, :, None]
    seen = (16 * np.arange(16)[None, None, :] + 31 <= t).astype(float)
    parts += [("cmp_neg", ((1 - seen) * NEG).reshape(P, NT * 16)), ("cmp_seen", seen.reshape(P, NT * 16))]
    parts.append(("head16", (p[:, None] // 16 == np.arange(8)[None, :]).astype(float)))
    parts.append(("upper", (p[:, None] <= p[None, :]).astype(float)))
    parts.append(("causal_neg", np.where(p[None, :] > p[:, None], NEG, 0.0)))
    at = 0
    for name, a in parts:
        CONST_COLS[name] = (at, a.shape[1])
        at += a.shape[1]
    levels = [(p[:, None] == p[None, :])]
    for n in range(1, NLVL):
        h = 1 << (n - 1)
        levels.append((p[:, None] // (2 * h) == p[None, :] // (2 * h)) & (p[:, None] % (2 * h) < h)
                      & (p[None, :] % (2 * h) >= h))
    masks = np.stack(levels, axis=1).astype(np.int32).reshape(P, NLVL * P)
    return np.concatenate([a for _, a in parts], axis=1).astype(np.float32), masks


const_table()
NCONST = max(a + n for a, n in CONST_COLS.values())

VEC_ROWS = [("norm_g", 16), ("ple_norm_g", 16), ("hgrn_lb", 8), ("hgrn_onorm_g", 2), ("nsa_qnorm_g", 2),
            ("nsa_knorm_g", 6), ("cmp_pe", 64), ("mix0_norm_2", 8), ("lru_conv_w_2", 16), ("lru_conv_b_2", 4),
            ("lru_ba_2", 4), ("lru_bx_2", 4), ("lru_lambda_2", 4), ("sconv_w_2", 12), ("sconv_b_2", 4),
            ("mix1_norm_2", 8), ("sgu_norm_2", 4), ("ffn_norm_2", 16), ("final_norm_2", 8),
            ("ffn_conv_w_2", 264), ("ffn_conv_b_2", 88)]
VEC_AT, _n = {}, 0
for _name, _rows in VEC_ROWS:
    VEC_AT[_name] = _n
    _n += _rows
NVEC = _n
NVT = (NVEC + P - 1) // P
DUPLICATED = ("nsa_qnorm_g", "nsa_knorm_g")

FIRST_PANELS = ["hf", "hq", "hi", "nq", "kv", "kw", "cmp1", "hgo", "hz", "nz", "wo0", "wo1", "pp", "pg0", "pg1"]
EVEN_PANELS = ["xa", "cp", "vb", "ga", "bp", "wo0", "wo1"]
ODD_PANELS = ["fq", "fk", "ff", "fv", "zg", "zu", "wo0", "wo1"]


def panel_plan():
    place, used, nxt = {}, [0] * SLOTS, 0

    def put(key, slot):
        place[key] = (slot, used[slot])
        used[slot] += 1

    order = []
    for l in range(DEPTH):
        for name in FIRST_PANELS:
            put((name, l), nxt % SLOTS)
            order.append((name, l))
            nxt += 1
    for l in range(DEPTH):
        for name in (EVEN_PANELS if l == 0 else ODD_PANELS):
            put((name, DEPTH + l), nxt % SLOTS)
            order.append((name, DEPTH + l))
            nxt += 1
        for it in range(FF_ROUNDS):
            put(("up", l, it), it % 2)
            put(("down", l, it), 2 + it % 2)
        order.append(("ffn", l))
        nxt = 0
    return place, order


PLACE, ORDER = panel_plan()


def build(nc, a, out):
    fills = {}
    bank_fills = [0] * 8

    with ExitStack() as ctx:
        def sb(name, cols, dt=F32):
            return ctx.enter_context(nc.sbuf_tensor(name, [P, cols], dt))

        sems = {}

        def sem(name):
            if name not in sems:
                sems[name] = ctx.enter_context(nc.semaphore(name))
            return sems[name]

        ps = [ctx.enter_context(nc.psum_tensor(f"ps{b}", [P, 512], F32)) for b in range(8)]
        psum_full = [sem(f"psum_full{b}") for b in range(8)]
        psum_free = [sem(f"psum_free{b}") for b in range(8)]
        panel_landed = [sem(f"panel_landed{s}") for s in range(SLOTS)]
        value_landed = [sem(f"value_panel_landed{s}") for s in range(2)]
        panel_free = {}

        def v3(t, n, off=0):
            w = t.shape[1] - off
            return t[:, off:off + w].rearrange("p (n w) -> p n w", n=n)

        H = sb("residual", ND * T)
        XN = sb("normed", ND * T)
        SQ = sb("squares", ND * T)
        RING = sb("panels", SLOTS * PANEL)
        Y = sb("mixed", ND * T)
        UW = sb("rope_terms", 2048)
        RINV = sb("rinv", T)
        RBIG = sb("rinv_heads", 1024)
        CN = sb("consts", NCONST)
        LM = sb("level_masks", NLVL * P, I32)
        VC = sb("vectors", NVT * P)
        IDB = sb("ident_bf16", P, BF16)
        NGB = sb("causal_neg_bf16", P, BF16)
        EPSC = sb("eps", 2)
        LB = sb("lower_bound", 32)
        GQ = sb("q_gain_scaled", 2)
        SPC = sb("lru_rate", 40)
        W2 = sb("cmp_w2", 256)
        FK = sb("forget_key", 2048)
        FG, KQ = FK[:, 0:1024], FK[:, 1024:2048]
        QP = sb("query", 1024)
        FLV = sb("forget_levels", 1024)
        AD = sb("decay_diag", 1024)
        VH = sb("values_hg", 1024)
        SG = sb("gate_o", 1024)
        HZ = sb("gate_z", 1024)
        NZ = sb("nsa_z", 1024)
        QN = sb("q_nope", 1024)
        QR = sb("q_rope", 1024)
        AC = sb("decay_cross", 512)
        VT = sb("values_nsa", 512)
        GT = sb("nsa_gates", 48)
        KN = sb("k_normed", 512)
        UK = sb("k_rope_terms", 1024)
        KZ = sb("k_padded", 2048)
        PB = sb("probs", 2 * 768)
        PT = sb("probs_t", 2 * 768)
        SC = sb("cmp_scores", 256)
        SS = sb("small", 256)
        PCT = sb("cmp_probs_t", 256)
        VCB = sb("cmp_values", 512)
        HID = sb("cmp_hidden", 64)
        HIDV = sb("cmp_hidden_rep", P)
        KC = sb("cmp_k", 64)
        KCZ = sb("cmp_k_padded", 64)
        NM = sb("neg_max", 8)
        SM = sb("prob_sums", 8)
        PP = FK
        ZR = sb("zeros", P)
        NT16 = sb("head_stats", 16)

        ring = [RING[:, s * PANEL:(s + 1) * PANEL] for s in range(SLOTS)]

        def const(name):
            at, n = CONST_COLS[name]
            return CN[:, at:at + n]

        def vec(name, n=0, m=1):
            at = VEC_AT[name] + n
            return VC[:, at:at + m]

        h3, xn3, sq3, y3 = (v3(t, ND) for t in (H, XN, SQ, Y))
        ident = const("ident")
        K2 = PB[:, 0:1024].rearrange("p (kv g t) -> p kv g t", kv=2, g=2)
        M2 = PT[:, 0:1024].rearrange("p (kv jj g c) -> p kv jj g c", kv=2, jj=16, g=2)
        kz = KZ[:, :].rearrange("p (k par g t) -> p k par g t", k=2, par=2, g=2)
        ad = AD[:, :].rearrange("p (h n t) -> p h n t", h=4, n=NT)
        ac = v3(AC, 4)
        vh = v3(VH, NT)
        vt = VT[:, :].rearrange("p (k n d) -> p k n d", k=2, n=NT)
        gates = GT[:, :].rearrange("p (n a) -> p n a", n=NT)
        probs = [[PB[:, b * 768:b * 768 + 256].rearrange("p (r s) -> p r s", r=2),
                  PB[:, b * 768 + 256:b * 768 + 768].rearrange("p (r s) -> p r s", r=2)] for b in range(2)]
        pt_lo = [PT[:, b * 768:b * 768 + 512].rearrange("p (r t) -> p r t", r=2) for b in range(2)]
        pt_hi = [PT[:, b * 768 + 512:b * 768 + 768].rearrange("p (r t) -> p r t", r=2) for b in range(2)]
        flevel = {0: FG}
        at = 0
        for n in range(1, NLVL):
            w = 1024 >> n
            flevel[n] = FLV[:, at:at + w]
            at += w
        xt = XN[:, :].rearrange("p (n d) -> p n d", n=NT)
        ptok = Y[:, 0:1024].rearrange("p (l d) -> p l d", l=2 * NT)
        PTR = ctx.enter_context(nc.sbuf_tensor("p_transposed", [P, 1024], F32))
        ptr = PTR[:, :].rearrange("p (l k t) -> p l k t", l=DEPTH, k=2)
        vrows = v3(SQ, 16)

        def full(eng, name):
            b, k = fills[name]
            eng.wait_ge(psum_full[b], k + 1)

        def free(name):
            return psum_free[fills[name][0]]

        def drained(eng, name):
            b, k = fills[name]
            eng.wait_ge(psum_free[b], k + 1)

        def bank(name):
            return ps[fills[name][0]]

        agenda = {l: [] for l in range(2 * DEPTH)}
        normed_last = {}

        vec_dmas = []
        for name, rows in VEC_ROWS:
            src = a[name]
            wide64 = name in DUPLICATED
            src = src.rearrange(" ".join("abcd"[:len(src.shape)]) + " -> (" + " ".join("abcd"[:len(src.shape)]) + ")")
            src = src.rearrange("(r w) -> r w", w=64 if wide64 else P)
            done_rows = 0
            while done_rows < rows:
                at = VEC_AT[name] + done_rows
                n = min(rows - done_rows, P - at % P)
                for c0 in ((0, 64) if wide64 else (0,)):
                    vec_dmas.append((at // P, at % P, n, c0, c0 + (64 if wide64 else P),
                                     src[done_rows:done_rows + n, :]))
                done_rows += n
        N_VEC_DMAS = len(vec_dmas)

        const_landed = sem("const_landed")
        x_landed, p_landed, vec_landed = sem("x_landed"), sem("p_landed"), sem("vec_landed")
        w2_landed, bd_landed, sgu_landed = sem("cmp_w2_landed"), sem("lru_weights_landed"), sem("sgu_landed")
        bias_landed, bt_landed = sem("forget_bias_landed"), sem("sgu_bias_landed")
        eps_ready, bd_zeroed = sem("eps_ready"), sem("lru_weights_zeroed")
        sq_ready = sem("squares_ready")
        rinv_ready = sem("rinv_ready")
        xn_ready = sem("normed_ready")
        h_ready = sem("residual_ready")
        small_ready = sem("setup_vectors_ready")
        hg_ready = sem("hg_keys_ready")
        level_ready = sem("hg_level_ready")
        qsq_ready, ksq_ready = sem("q_squares_ready"), sem("k_squares_ready")
        kcsq_ready, osq_ready = sem("cmp_k_squares_ready"), sem("hg_o_squares_ready")
        q_rinv_ready, k_rinv_ready = sem("q_rinv_ready"), sem("k_rinv_ready")
        kc_rinv_ready, o_rinv_ready = sem("cmp_k_rinv_ready"), sem("hg_o_rinv_ready")
        rope_ready, k_rope_ready = sem("q_rope_terms_ready"), sem("k_rope_terms_ready")
        blocks_ready = sem("cmp_blocks_ready")
        gate_exp_ready, gates_ready = sem("gate_exp_ready"), sem("gates_ready")
        hid_exp_ready, hidden_ready = sem("cmp_hidden_exp_ready"), sem("cmp_hidden_ready")
        kc_ready = sem("cmp_k_ready")
        cmp_shift_ready, cmp_exp_ready, cp_ready = (sem("cmp_shifted_ready"), sem("cmp_exp_ready"),
                                                    sem("cmp_probs_ready"))
        nmax_ready = sem("neg_max_ready")
        exps_ready = sem("exps_ready")
        p_ready = sem("probs_ready")
        sig_ready = sem("gate_sigmoids_ready")
        conv_ready = sem("conv_first_tap_ready")
        act_part = sem("scalar_part_ready")
        dve_part = sem("vector_part_ready")
        forget_ready, sgu_ready, y_ready = sem("forget_ready"), sem("sgu_ready"), sem("y_ready")
        taps_ready, first_back_done = sem("ffn_first_taps_ready"), sem("ffn_second_taps_done")
        silu_ready, act_ready = sem("ffn_silu_ready"), sem("ffn_hidden_ready")
        down_done = sem("ffn_down_done")
        out_copied, out_stored = sem("out_copied"), sem("out_stored")
        dve_step, act_step = sem("vector_step"), sem("scalar_step")
        BF = sb("forget_bias", 1)
        glu = [v3(t, 4) for t in (SG, HZ)]
        ones, head_ones = const("ones"), const("head_ones")
        ffn_base = {}
        act3 = [VH[:, par * 512:(par + 1) * 512].rearrange("p (k t) -> p k t", k=2) for par in range(2)]

        block = ctx.enter_context(nc.Block())

        @block.tensor
        def _(pe):
            last_done = [None]

            def begin(name, b):
                k = bank_fills[b]
                bank_fills[b] += 1
                fills[name] = (b, k)
                if k > 0:
                    pe.wait_ge(psum_free[b], k)
                return ps[b]

            def done(name, ins):
                ins.then_inc(psum_full[fills[name][0]], 1)
                last_done[0] = name

            def landed(key):
                s, k = PLACE[key]
                pe.wait_ge(panel_landed[s], 16 * (k + 1))

            def release(key):
                b, k = fills[last_done[0]]
                panel_free[key] = (psum_full[b], k + 1)

            def panel(key, nk=ND, n=512):
                return ring[PLACE[key][0]][:, 0:nk * n].rearrange("p (k n) -> p k n", k=nk)

            def chunk(dst, w3, col, x3, nk=ND, m=P, norm=None):
                for k in range(nk):
                    if norm is not None:
                        pe.wait_ge(xn_ready, 8 * norm + k + 1)
                    ins = pe.matmul(dst, w3[:, k, col:col + m], x3[:, k, :], start=(k == 0), stop=(k == nk - 1))
                return ins

            def by_token(dst, w3, col, n, tile):
                for k in range(ND):
                    ins = pe.matmul(dst, xn3[:, k, tile * P:(tile + 1) * P], w3[:, k, col:col + n],
                                    start=(k == 0), stop=(k == ND - 1))
                return ins

            def two_chunks(name, b, key, first, x3=xn3, norm=None):
                begin(name, b)
                for j in range(2):
                    ins = chunk(ps[b][:, j * T:(j + 1) * T], panel(key), (first + j) * P, x3,
                                norm=norm if j == 0 else None)
                done(name, ins)

            def norm_sum(nidx, b=0):
                begin(f"ms{nidx}", b)
                for c in range(ND):
                    if c % 2 == 0:
                        pe.wait_ge(sq_ready, 4 * nidx + c // 2 + 1)
                    ins = pe.matmul(ps[b][:, 0:T], ones, sq3[:, c, :], start=(c == 0), stop=(c == ND - 1))
                done(f"ms{nidx}", ins)

            def product(name, b, n, lhs, rhs):
                begin(name, b)
                done(name, pe.matmul(ps[b][:, 0:n], lhs, rhs, start=True, stop=True))

            pe.wait_ge(const_landed, 32)
            pe.wait_ge(x_landed, 16)
            for g in range(4):
                begin(f"x{g}", g)
                for j in range(4):
                    c, n = 2 * g + j // 2, j % 2
                    ins = pe.transpose(ps[g][:, j * P:(j + 1) * P], xt[:, n, c * P:(c + 1) * P], ident)
                done(f"x{g}", ins)
            pe.wait_ge(vec_landed, 16 * N_VEC_DMAS)
            for g in range((NVT + 3) // 4):
                begin(f"vec{g}", 4 + g)
                for j in range(min(4, NVT - 4 * g)):
                    r = min(P, NVEC - (4 * g + j) * P)
                    ins = pe.transpose(ps[4 + g][:, j * P:j * P + r], vrows[0:r, 4 * g + j, :], ident[0:r, 0:r])
                done(f"vec{g}", ins)
            pe.wait_ge(p_landed, 16)
            for l in range(DEPTH):
                begin(f"p{l}", 6 + l)
                for k in range(2):
                    for n in range(NT):
                        ins = pe.transpose(ps[6 + l][:, k * T + n * P:k * T + (n + 1) * P],
                                           ptok[:, l * NT + n, k * P:(k + 1) * P], ident)
                done(f"p{l}", ins)

            def scores(tag, u, q, keys, forget=None):
                begin(f"{tag}Y{u}", 5)
                begin(f"{tag}X{u}", 3 + u % 2)
                for n, b, x in ((0, 5, "Y"), (1, 3 + u % 2, "X")):
                    w = (n + 1) * P
                    o = ps[b][:, 0:2 * w].rearrange("p (r s) -> p r s", r=2)
                    pe.matmul(o, q[:, n * P:(n + 1) * P], keys[:, :, 0:w], start=True, stop=True)
                    if forget is not None:
                        pe.matmul(o, ones[0:8, :], forget[:, :, 0:w], start=False, stop=True,
                                  skip_group_check=True)
                    ins = pe.matmul(o[:, :, n * P:w], IDB[:, :], NGB[:, :].unsqueeze(1).to_broadcast([P, 2, P]),
                                    start=False, stop=True, skip_group_check=True)
                    done(f"{tag}{x}{u}", ins)

            def turn(tag, u, pidx):
                bb = pidx % 2
                pe.wait_ge(p_ready, pidx + 1)
                begin(f"{tag}A{u}", 6)
                for r in range(2):
                    pe.transpose(ps[6][:, r * T:r * T + P], probs[bb][0][:, r, :], ident)
                    ins = pe.transpose(ps[6][:, r * T + P:(r + 1) * T], probs[bb][1][:, r, 0:P], ident)
                done(f"{tag}A{u}", ins)
                begin(f"{tag}B{u}", 7)
                for r in range(2):
                    ins = pe.transpose(ps[7][:, r * P:(r + 1) * P], probs[bb][1][:, r, P:T], ident)
                done(f"{tag}B{u}", ins)

            def values(tag, u, pidx, vals, o, start, close=None):
                bb = pidx % 2
                drained(pe, f"{tag}A{u}")
                drained(pe, f"{tag}B{u}")
                for r in range(2):
                    pe.matmul(o[64 * r:64 * r + 64, :], vals(0, r), pt_lo[bb][:, r, :],
                              start=start, stop=True, skip_group_check=True)
                    ins = pe.matmul(o[64 * r:64 * r + 64, P:T], vals(1, r), pt_hi[bb][:, r, :],
                                    start=False, stop=True, skip_group_check=True)
                if close:
                    done(close, ins)

            def output(tag, l):
                for g in range(4):
                    key = (f"wo{g // 2}", l)
                    if g % 2 == 0:
                        landed(key)
                    two_chunks(f"{tag}{g}", 3 + g, key, 2 * (g % 2), x3=y3)
                    if g % 2 == 1:
                        release(key)

            nidx, pidx = 0, 0
            for l in range(DEPTH):
                todo = agenda[l].append
                norm_sum(nidx)
                for name, b in (("hf", 1), ("hq", 3)):
                    landed((name, l))
                    for g in range(2):
                        two_chunks(f"{name}{g}_{l}", b + g, (name, l), 2 * g,
                                   norm=nidx if (name, g) == ("hf", 0) else None)
                    release((name, l))
                landed(("hi", l))
                for n in range(NT):
                    begin(f"hi{n}_{l}", 5 + n)
                    done(f"hi{n}_{l}", by_token(ps[5 + n][:, :], panel(("hi", l)), 0, 512, n))
                release(("hi", l))

                def level(n, g):
                    if n == 0:
                        pe.wait_ge(hg_ready, l + 1)
                        drained(pe, f"hq{g}_{l}")
                    else:
                        pe.wait_ge(level_ready, 16 * l + 2 * (n - 1) + g + 1)
                    b = (7, 0)[g]
                    begin(f"lv{n}_{g}_{l}", b)
                    for j in range(4):
                        s = (2 * g + j // 2) * T + (j % 2) * P
                        ins = pe.matmul(ps[b][:, j * P:(j + 1) * P], KQ[:, s:s + P], QP[:, s:s + P],
                                        start=True, stop=True)
                    done(f"lv{n}_{g}_{l}", ins)
                    todo(("level", n, g))

                levels = [(n, g) for n in range(NLVL) for g in range(2)]

                def some(k):
                    for _ in range(min(k, len(levels))):
                        level(*levels.pop(0))

                some(2)
                landed(("nq", l))
                for g in range(2):
                    begin(f"nq{g}_{l}", 1 + g)
                    for j in range(2):
                        ins = chunk(ps[1 + g][:, j * T:(j + 1) * T], panel(("nq", l)), (2 * g + j) * P, xn3)
                        if j == 0:
                            some(1)
                    done(f"nq{g}_{l}", ins)
                    todo(("copy", f"nq{g}"))
                    some(1)
                release(("nq", l))
                landed(("kv", l))
                begin(f"kcvc_{l}", 3)
                for j in range(2):
                    ins = chunk(ps[3][:, j * T:(j + 1) * T], panel(("kv", l)), j * P, xn3)
                    if j == 0:
                        some(1)
                done(f"kcvc_{l}", ins)
                todo(("blocks",))
                some(1)
                begin(f"ks_{l}", 4)
                chunk(ps[4][:, 0:T], panel(("kv", l)), 2 * P, xn3)
                some(1)
                begin(f"vs_{l}", 5)
                for n in range(NT):
                    ins = by_token(ps[5][:, n * P:(n + 1) * P], panel(("kv", l)), 3 * P, P, n)
                done(f"vs_{l}", ins)
                release(("kv", l))
                todo(("copy", "vs"))
                some(1)
                landed(("kw", l))
                done(f"ks_{l}", chunk(ps[4][:, T:2 * T], panel(("kw", l)), 0, xn3))
                todo(("k_square",))
                some(1)
                begin(f"vw_{l}", 6)
                for n in range(NT):
                    ins = by_token(ps[6][:, n * 152:(n + 1) * 152], panel(("kw", l)), P, 152, n)
                done(f"vw_{l}", ins)
                release(("kw", l))
                todo(("gates",))
                pe.wait_ge(qsq_ready, l + 1)
                for j in range(2):
                    product(f"qss{j}_{l}", 1 + j, 512, head_ones, SQ[:, j * 512:(j + 1) * 512])
                todo(("q_norm",))
                some(1)
                pe.wait_ge(ksq_ready, l + 1)
                product(f"kss_{l}", 4, 512, head_ones, SQ[:, 1024:1536])
                todo(("k_norm",))
                some(1)
                landed(("cmp1", l))
                pe.wait_ge(blocks_ready, l + 1)
                begin(f"hid_{l}", 3)
                w1 = ring[PLACE[("cmp1", l)][0]]
                for kv in range(2):
                    for jj in range(16):
                        s = (kv * 16 + jj) * P
                        ins = pe.matmul(ps[3][:, kv * 32:(kv + 1) * 32], w1[:, s:s + P], M2[:, kv, jj, :, :],
                                        start=(jj == 0), stop=(jj == 15))
                done(f"hid_{l}", ins)
                release(("cmp1", l))
                todo(("hidden",))
                some(1)
                pe.wait_ge(rope_ready, l + 1)
                for j in range(2):
                    begin(f"qr{j}_{l}", 1 + j)
                    pe.matmul(ps[1 + j][:, :], ident, UW[:, j * 512:(j + 1) * 512], start=True, stop=False)
                    done(f"qr{j}_{l}", pe.matmul(ps[1 + j][:, :], const("rot"),
                                                 UW[:, 1024 + j * 512:1024 + (j + 1) * 512],
                                                 start=False, stop=True))
                    todo(("copy", f"qr{j}"))
                some(1)
                pe.wait_ge(k_rope_ready, l + 1)
                begin(f"kr_{l}", 4)
                pe.matmul(ps[4][:, :], ident, UK[:, 0:512], start=True, stop=False)
                done(f"kr_{l}", pe.matmul(ps[4][:, :], const("rot"), UK[:, 512:1024], start=False, stop=True))
                todo(("k_pad",))
                some(16)
                pe.wait_ge(level_ready, 16 * l + 16)
                begin(f"cross_{l}", 7)
                for hd in range(4):
                    ins = pe.matmul(ps[7][:, hd * P:(hd + 1) * P], KQ[:, hd * T:hd * T + P],
                                    QP[:, hd * T + P:(hd + 1) * T], start=True, stop=True)
                done(f"cross_{l}", ins)
                todo(("cross",))
                pe.wait_ge(w2_landed, 48 * (l + 1))
                pe.wait_ge(hidden_ready, l + 1)
                product(f"kc_{l}", 0, 32, W2[:, 0:P], HID[:, 0:32])
                product(f"vc_{l}", 3, 64, HIDV[:, :], W2[:, P:P + 64])
                todo(("cmp_kv",))
                drained(pe, f"hi1_{l}")
                drained(pe, f"cross_{l}")
                drained(pe, f"lv{NLVL - 1}_0_{l}")
                drained(pe, f"lv{NLVL - 1}_1_{l}")
                for g in range(2):
                    begin(f"o{g}_{l}", 5 + g)
                    for j in range(2):
                        hd = 2 * g + j
                        v = [vh[:, n, hd * P:(hd + 1) * P] for n in range(NT)]
                        pe.matmul(ps[5 + g][:, j * T:j * T + P], v[0], ad[:, hd, 0, :], start=True, stop=True)
                        pe.matmul(ps[5 + g][:, j * T + P:(j + 1) * T], v[0], ac[:, hd, :], start=True, stop=False)
                        ins = pe.matmul(ps[5 + g][:, j * T + P:(j + 1) * T], v[1], ad[:, hd, 1, :],
                                        start=False, stop=True)
                    done(f"o{g}_{l}", ins)
                todo(("o_square",))
                pe.wait_ge(kcsq_ready, l + 1)
                product(f"kcss_{l}", 0, 32, head_ones, KC[:, 32:64])
                todo(("kc_norm",))
                gate_chunks = [(name, g, j) for name in ("hgo", "hz", "nz") for g in range(2) for j in range(2)]

                def gate_chunk():
                    if not gate_chunks:
                        return
                    name, g, j = gate_chunks.pop(0)
                    if g == 0 and j == 0:
                        landed((name, l))
                    if j == 0:
                        begin(f"{name}{g}_{l}", 0)
                    ins = chunk(ps[0][:, j * T:(j + 1) * T], panel((name, l)), (2 * g + j) * P, xn3)
                    if j == 1:
                        done(f"{name}{g}_{l}", ins)
                        todo(("copy", f"{name}{g}"))
                        if g == 1:
                            release((name, l))

                gate_chunk()
                pe.wait_ge(osq_ready, l + 1)
                for g in range(2):
                    product(f"oss{g}_{l}", 5 + g, 512, ones, SQ[:, g * 512:(g + 1) * 512])
                todo(("o_norm",))
                pe.wait_ge(kc_ready, l + 1)
                begin(f"cs_{l}", 3)
                for n in range(NT):
                    for j in range(4):
                        s = n * P + j * 32
                        ins = pe.matmul(ps[3][:, s:s + 32].rearrange("p (r c) -> p r c", r=2),
                                        QN[:, j * T + n * P:j * T + (n + 1) * P],
                                        v3(KCZ, 2)[:, :, (j // 2) * 16:(j // 2) * 16 + 16], start=True, stop=True)
                done(f"cs_{l}", ins)
                todo(("cmp_softmax",))
                gate_chunk()
                drained(pe, f"qr1_{l}")
                drained(pe, f"kr_{l}")
                drained(pe, f"vs_{l}")
                pe.wait_ge(gates_ready, l + 1)

                def unit(u):
                    kind, j = u // 4, u % 4
                    scores(f"n{l}", u, QR[:, j * T:(j + 1) * T], kz[:, kind, :, j // 2, :])
                    todo(("scores", u))

                unit(0)
                pe.wait_ge(cp_ready, l + 1)
                begin(f"ct_{l}", 7)
                for n in range(NT):
                    ins = pe.transpose(ps[7][:, n * P:(n + 1) * P], SC[:, n * P:(n + 1) * P], ident)
                done(f"ct_{l}", ins)
                todo(("copy", "ct"))
                gate_chunk()
                drained(pe, f"ct_{l}")
                drained(pe, f"vc_{l}")
                begin(f"on0_{l}", 1)
                begin(f"on1_{l}", 2)
                for j in range(4):
                    pe.matmul(ps[1 + j // 2][:, (j % 2) * T:(j % 2 + 1) * T], VCB[:, j * P:(j + 1) * P], PCT[:, :],
                              start=(j % 2 == 0), stop=True, skip_group_check=True)
                for u in range(8):
                    if u < 7:
                        unit(u + 1)
                    turn(f"n{l}", u, pidx)
                    todo(("values", u))
                    gate_chunk()
                    kind, j = u // 4, u % 4
                    values(f"n{l}", u, pidx, lambda n, r: vt[:, kind, n, (j // 2) * 64:(j // 2) * 64 + 64],
                           ps[1 + j // 2][:, (j % 2) * T:(j % 2 + 1) * T], False,
                           close={5: f"on0_{l}", 7: f"on1_{l}"}.get(u))
                    pidx += 1
                while gate_chunks:
                    gate_chunk()
                normed_last[nidx] = f"nz1_{l}"
                nidx += 1
                todo(("mix",))
                drained(pe, f"on0_{l}")
                drained(pe, f"on1_{l}")
                output(f"wo_{l}_", l)
                landed(("pp", l))
                for g in range(4):
                    b = (7, 0, 1, 2)[g]
                    if g == 2:
                        norm_sum(nidx, b=3)
                    begin(f"pp{g}_{l}", b)
                    for j in range(2):
                        ins = chunk(ps[b][:, j * T:(j + 1) * T], panel(("pp", l), 2, 1024), (2 * g + j) * P,
                                    ptr[:, l], nk=2)
                    done(f"pp{g}_{l}", ins)
                release(("pp", l))
                for g in range(4):
                    key = (f"pg{g // 2}", l)
                    if g % 2 == 0:
                        landed(key)
                    two_chunks(f"pg{g}_{l}", 4 + g, key, 2 * (g % 2), norm=nidx if g == 0 else None)
                    if g % 2 == 1:
                        release(key)
                normed_last[nidx] = f"pg3_{l}"
                nidx += 1

            for l in range(DEPTH):
                L = DEPTH + l
                todo = agenda[L].append
                norm_sum(nidx)
                if l == 0:
                    for name, b in (("xa", 1), ("cp", 3)):
                        landed((name, L))
                        for g in range(2):
                            two_chunks(f"{name}{g}", b + g, (name, L), 2 * g,
                                       norm=nidx if (name, g) == ("xa", 0) else None)
                        release((name, L))
                    landed(("vb", L))
                    for g in range(2):
                        two_chunks(f"vb{g}", 5 + g, ("vb", L), 2 * g)
                    release(("vb", L))
                    pe.wait_ge(bd_landed, 64)
                    for name, w, b in (("lr", 0, (7, 0)), ("li", 512, (1, 2))):
                        for g in range(2):
                            drained(pe, f"xa{g}")
                            begin(f"{name}{g}", b[g])
                            for j in range(2):
                                c = 2 * g + j
                                ins = pe.matmul(ps[b[g]][:, j * T:(j + 1) * T], PB[:, w + c * P:w + (c + 1) * P],
                                                FG[:, c * T:(c + 1) * T], start=True, stop=True)
                            done(f"{name}{g}", ins)
                    for name, b in (("ga", 3), ("bp", 5)):
                        landed((name, L))
                        for g in range(2):
                            two_chunks(f"{name}{g}", b + g, (name, L), 2 * g)
                        release((name, L))
                    normed_last[nidx] = "bp1"
                else:
                    for name, b in (("fq", 1), ("fk", 3)):
                        landed((name, L))
                        for g in range(2):
                            two_chunks(f"{name}{g}", b + g, (name, L), 2 * g,
                                       norm=nidx if (name, g) == ("fq", 0) else None)
                        release((name, L))
                    landed(("ff", L))
                    begin("fl", 7)
                    done("fl", chunk(ps[7][0:8, 0:T], panel(("ff", L), ND, 8), 0, xn3, m=8))
                    release(("ff", L))
                    landed(("fv", L))
                    for n in range(NT):
                        begin(f"fv{n}", 5 + n)
                        done(f"fv{n}", by_token(ps[5 + n][:, :], panel(("fv", L)), 0, 512, n))
                    release(("fv", L))
                    landed(("zg", L))
                    for n in range(NT):
                        begin(f"zg{n}", 1 + n)
                        done(f"zg{n}", by_token(ps[1 + n][:, :], panel(("zg", L)), 0, 512, n))
                    release(("zg", L))
                    pe.wait_ge(sgu_landed, 16)
                    for g in range(2):
                        begin(f"wt{g}", (7, 0)[g])
                        for j in range(4):
                            hd = 4 * g + j
                            ins = pe.transpose(ps[(7, 0)[g]][:, j * P:(j + 1) * P], PT[:, hd * P:(hd + 1) * P],
                                               ident)
                        done(f"wt{g}", ins)
                    landed(("zu", L))
                    two_chunks("zu0", 3, ("zu", L), 0)
                    pe.wait_ge(forget_ready, 1)
                    drained(pe, "fq1")
                    drained(pe, "fk1")
                    drained(pe, "fv1")
                    drained(pe, "wt1")

                    def unit(u):
                        scores("f", u, QR[:, u * T:(u + 1) * T], kz[:, u // 2, :, u % 2, :],
                               UW[0:8, :].rearrange("p (h t) -> p h t", h=8)[:, 2 * u:2 * u + 2, :])
                        todo(("scores", u))

                    def mix_tokens(g):
                        begin(f"sg{g}", 0)
                        for j in range(2):
                            for n in range(NT):
                                for r in range(2):
                                    hd = 4 * g + 2 * j + r
                                    s = j * T + n * P
                                    ins = pe.matmul(ps[0][64 * r:64 * r + 64, s:s + P],
                                                    QN[:, n * 512 + hd * 64:n * 512 + (hd + 1) * 64],
                                                    AD[:, hd * P:(hd + 1) * P], start=True, stop=True)
                        done(f"sg{g}", ins)
                        todo((f"sg{g}",))

                    unit(0)
                    for u in range(4):
                        if u < 3:
                            unit(u + 1)
                        if u == 0:
                            two_chunks("zu1", 0, ("zu", L), 2)
                            release(("zu", L))
                            todo(("zu1",))
                        turn("f", u, pidx)
                        todo(("values", u))
                        if u == 1:
                            pe.wait_ge(sgu_ready, 1)
                            mix_tokens(0)
                        if u % 2 == 0:
                            begin(f"fo{u // 2}", 1 + u // 2)
                        values("f", u, pidx, lambda n, r: vh[:, n, (2 * u + r) * 64:(2 * u + r + 1) * 64],
                               ps[1 + u // 2][:, (u % 2) * T:(u % 2 + 1) * T], True,
                               close=f"fo{u // 2}" if u % 2 == 1 else None)
                        pidx += 1
                    mix_tokens(1)
                    normed_last[nidx] = "zu1"
                nidx += 1
                pe.wait_ge(y_ready, l + 1)
                output(f"wm_{l}_", L)

                norm_sum(nidx, b=0)
                pe.wait_ge(xn_ready, 8 * nidx + 8)
                for g in range(4):
                    begin(f"down{g}_{l}", 4 + g)
                    pe.matmul(ps[4 + g][:, :], ZR[:, :], CN[:, 0:512], start=True, stop=True,
                              skip_group_check=True)
                up0 = [bank_fills[b] for b in range(4)]
                loads = [PLACE[("up", l, 0)][1], PLACE[("up", l, 1)][1],
                         PLACE[("down", l, 0)][1], PLACE[("down", l, 1)][1]]
                ffn_base[l] = (up0, loads)

                def up(par, i):
                    w3 = ring[par].rearrange("p (k n) -> p k n", k=ND)
                    for half in range(2):
                        if half == 0:
                            pe.wait_ge(panel_landed[par], i * 16 + 16 * (loads[par] + 1))
                        else:
                            pe.wait_ge(value_landed[par], i * 16 + 16 * (1 + l * ((FF_ROUNDS + 1 - par) // 2)))
                        b = 2 * par + half
                        pe.wait_ge(psum_free[b], i + up0[b])
                        for j in range(2):
                            for k in range(ND):
                                ins = pe.matmul(ps[b][:, j * T:(j + 1) * T],
                                                w3[:, k, (2 * half + j) * P:(2 * half + j + 1) * P],
                                                xn3[:, k, :], start=(k == 0), stop=(k == ND - 1))
                        ins.then_inc(psum_full[b], 1)

                def down(par, i, close=False):
                    pe.wait_ge(panel_landed[2 + par], i * 16 + 16 * (loads[2 + par] + 1))
                    pe.wait_ge(act_ready, 2 * i + (par + 1 + FF_ROUNDS * l))
                    w3 = ring[2 + par][:, 0:2048].rearrange("p (k n) -> p k n", k=2)
                    for g in range(4):
                        for j in range(2):
                            for k in range(2):
                                c = 2 * g + j
                                ins = pe.matmul(ps[4 + g][:, j * T:(j + 1) * T], w3[:, k, c * P:(c + 1) * P],
                                                act3[par][:, k, :], start=False, stop=True,
                                                skip_group_check=True)
                        if close:
                            done(f"down{g}_{l}", ins)
                    if not close:
                        ins.then_inc(down_done, 1)

                up(0, 0)
                up(1, 0)
                down(0, 0)
                with pe.Fori(1, FF_ROUNDS // 2) as i:
                    up(0, i)
                    down(1, i - 1)
                    up(1, i)
                    down(0, i)
                up(0, FF_ROUNDS // 2)
                down(1, FF_ROUNDS // 2 - 1)
                down(0, FF_ROUNDS // 2, close=True)
                for b in range(4):
                    bank_fills[b] += FF_ROUNDS // 2 + (b < 2)
                for s in range(2):
                    panel_free[("up", l, s)] = (psum_full[2 * s + 1], bank_fills[2 * s + 1])
                    panel_free[("down", l, s)] = (psum_full[7], bank_fills[7])
                last_up = f"ffn_up{l}"
                fills[last_up] = (1, bank_fills[1] - 1)
                normed_last[nidx] = last_up
                nidx += 1

            norm_sum(nidx)
            pe.wait_ge(xn_ready, 8 * nidx + 8)
            for g in range(4):
                n, c0 = g // 2, 4 * (g % 2)
                begin(f"out{g}", (1, 2, 3, 4)[g])
                for j in range(4):
                    ins = pe.transpose(ps[(1, 2, 3, 4)[g]][:, j * P:(j + 1) * P],
                                       xn3[:, c0 + j, n * P:(n + 1) * P], ident)
                done(f"out{g}", ins)

        @block.scalar
        def _(act):
            steps = [0]

            def link(ins):
                steps[0] += 1
                ins.then_inc(act_step, 1)
                act.wait_ge(act_step, steps[0])

            def f(dst, src, func, **kw):
                return nc.scalar.activation(dst, src, func, **kw)

            def copy_out(name, dst, src):
                full(act, name)
                nc.scalar.copy(dst, src).then_inc(free(name), 1)

            def log_exp():
                nc.scalar.preload_act_table_set(LOG_EXP)

            def squares(nidx, ready):
                for g in range(4):
                    ready(g)
                    f(sq3[:, 2 * g:2 * g + 2, :], h3[:, 2 * g:2 * g + 2, :], ACT.Square).then_inc(sq_ready, 1)

            def norm(nidx):
                log_exp()
                full(act, f"ms{nidx}")
                f(RINV[:, :], bank(f"ms{nidx}")[:, 0:T], ACT.Ln, bias=EPSC[:, 0:1],
                  scale=1.0 / D).then_inc(free(f"ms{nidx}"), 1)
                drained(act, f"ms{nidx}")
                f(RINV[:, :], RINV[:, :], ACT.Exp, scale=-0.5).then_inc(rinv_ready, 1)

            def head_rinv(names, dst, width, n):
                for j, name in enumerate(names):
                    full(act, name)
                    w = n // len(names)
                    f(dst[:, j * w:(j + 1) * w], bank(name)[:, 0:w], ACT.Ln, bias=EPSC[:, 0:1],
                      scale=1.0 / width).then_inc(free(name), 1)
                drained(act, names[-1])
                return f(dst, dst, ACT.Exp, scale=-0.5)

            def exps(tag, u, pidx):
                bb = pidx % 2
                act.wait_ge(nmax_ready, pidx + 1)
                if pidx >= 2:
                    act.wait_ge(*turned[pidx - 2])
                for n, x in ((0, "Y"), (1, "X")):
                    s3 = bank(f"{tag}{x}{u}")[:, 0:2 * (n + 1) * P].rearrange("p (r s) -> p r s", r=2)
                    for r in range(2):
                        i = 2 * n + r
                        ins = f(probs[bb][n][:, r, :], s3[:, r, :], ACT.Exp, bias=NM[:, 4 * bb + i:4 * bb + i + 1],
                                accum_out=SM[:, 4 * bb + i:4 * bb + i + 1])
                    ins.then_inc(free(f"{tag}{x}{u}"), 1)

            def turned_copies(tag, u, pidx):
                bb = pidx % 2
                copy_out(f"{tag}A{u}", pt_lo[bb].rearrange("p r t -> p (r t)"), bank(f"{tag}A{u}")[:, :])
                copy_out(f"{tag}B{u}", pt_hi[bb].rearrange("p r t -> p (r t)"), bank(f"{tag}B{u}")[:, 0:T])
                b, k = fills[f"{tag}B{u}"]
                turned[pidx] = (psum_full[b], k + 1)

            turned = {}
            act.wait_ge(eps_ready, 1)
            for g in range((NVT + 3) // 4):
                n = min(512, NVEC - 512 * g)
                copy_out(f"vec{g}", VC[:, 512 * g:512 * g + n], bank(f"vec{g}")[:, 0:n])
            for l in range(DEPTH):
                copy_out(f"p{l}", PTR[:, l * 512:(l + 1) * 512], bank(f"p{l}")[:, :])
            log_exp()
            act.wait_ge(dve_part, 1)
            f(SPC[:, 8:20], SPC[:, 8:20], ACT.Exp).then_inc(act_part, 1)
            squares(0, lambda g: drained(act, f"x{g}"))
            norm(0)

            nidx, pidx = 0, 0
            for l in range(DEPTH):
                if l > 0:
                    squares(nidx, lambda g: act.wait_ge(h_ready, 4 * l + g - 3))
                    norm(nidx)
                nidx += 1
                for g in range(2):
                    full(act, f"hf{g}_{l}")
                    s = slice(g * 512, (g + 1) * 512)
                    f(FG[:, s], bank(f"hf{g}_{l}")[:, :], ACT.Sigmoid)
                    f(KQ[:, s], bank(f"hf{g}_{l}")[:, :], ACT.Sigmoid, scale=-1.0).then_inc(free(f"hf{g}_{l}"), 1)
                for g in range(2):
                    copy_out(f"hq{g}_{l}", QP[:, g * 512:(g + 1) * 512], bank(f"hq{g}_{l}")[:, :])
                for n in range(NT):
                    copy_out(f"hi{n}_{l}", vh[:, n, :], bank(f"hi{n}_{l}")[:, :])
                log_exp()
                dest = {"nq0": QN[:, 0:512], "nq1": QN[:, 512:1024], "qr0": QR[:, 0:512], "qr1": QR[:, 512:1024],
                        "vs": VT[:, 0:T], "ct": PCT[:, :], "hgo0": SG[:, 0:512], "hgo1": SG[:, 512:1024],
                        "hz0": HZ[:, 0:512], "hz1": HZ[:, 512:1024], "nz0": NZ[:, 0:512], "nz1": NZ[:, 512:1024]}
                for step, *arg in agenda[l]:
                    if step == "copy":
                        name, dst = f"{arg[0]}_{l}", dest[arg[0]]
                        copy_out(name, dst, bank(name)[:, 0:dst.shape[1]])
                        if arg[0] == "nq1":
                            drained(act, name)
                            f(SQ[:, 0:1024], QN[:, :], ACT.Square).then_inc(qsq_ready, 1)
                    elif step == "blocks":
                        name = f"kcvc_{l}"
                        full(act, name)
                        src = v3(bank(name), 2)
                        for g in range(2):
                            s = src[64 * g:64 * g + 64]
                            nc.scalar.copy(K2[0:64, :, g, :], s)
                            ins = nc.scalar.copy(K2[64:128, :, g, 0:T - 1], s[:, :, 1:T])
                        ins.then_inc(free(name), 1)
                    elif step == "k_square":
                        name = f"ks_{l}"
                        copy_out(name, KN[:, :], bank(name)[:, :])
                        drained(act, name)
                        f(SQ[:, 1024:1536], KN[:, :], ACT.Square).then_inc(ksq_ready, 1)
                    elif step == "gates":
                        name = f"vw_{l}"
                        full(act, name)
                        src = bank(name)[:, 0:304].rearrange("p (n w) -> p n w", n=NT)
                        nc.scalar.copy(vt[:, 1, :, :], src[:, :, 0:P])
                        f(gates, src[:, :, P:152], ACT.Exp, scale=-1.0).then_inc(free(name), 1)
                    elif step == "q_norm":
                        head_rinv([f"qss{j}_{l}" for j in range(2)], RBIG[:, :], 64, 1024).then_inc(q_rinv_ready, 1)
                    elif step == "k_norm":
                        head_rinv([f"kss_{l}"], UK[:, 512:1024], 64, 512).then_inc(k_rinv_ready, 1)
                    elif step == "hidden":
                        full(act, f"hid_{l}")
                        f(SS[:, 0:64], bank(f"hid_{l}")[:, 0:64], ACT.Exp, scale=-1.0).then_inc(hid_exp_ready, 1)
                    elif step == "k_pad":
                        name = f"kr_{l}"
                        full(act, name)
                        src = v3(bank(name), 2)
                        for g in range(2):
                            s = src[64 * g:64 * g + 64]
                            nc.scalar.copy(kz[0:64, :, 0, g, :], s)
                            ins = nc.scalar.copy(kz[64:128, :, 1, g, :], s)
                        ins.then_inc(free(name), 1)
                    elif step == "cross":
                        copy_out(f"cross_{l}", AC[:, :], bank(f"cross_{l}")[:, :])
                    elif step == "cmp_kv":
                        name = f"kc_{l}"
                        copy_out(name, KC[:, 0:32], bank(name)[:, 0:32])
                        drained(act, name)
                        f(KC[:, 32:64], KC[:, 0:32], ACT.Square).then_inc(kcsq_ready, 1)
                    elif step == "o_square":
                        for g in range(2):
                            copy_out(f"o{g}_{l}", QP[:, g * 512:(g + 1) * 512], bank(f"o{g}_{l}")[:, :])
                        drained(act, f"o1_{l}")
                        f(SQ[:, 0:1024], QP[:, :], ACT.Square).then_inc(osq_ready, 1)
                    elif step == "kc_norm":
                        head_rinv([f"kcss_{l}"], SS[:, 64:96], 64, 32).then_inc(kc_rinv_ready, 1)
                    elif step == "o_norm":
                        act.wait_ge(rope_ready, l + 1)
                        head_rinv([f"oss{g}_{l}" for g in range(2)], RBIG[:, :], P, 1024).then_inc(o_rinv_ready, 1)
                    elif step == "cmp_softmax":
                        act.wait_ge(cmp_shift_ready, l + 1)
                        f(SC[:, :], SC[:, :], ACT.Exp).then_inc(cmp_exp_ready, 1)
                    elif step == "scores":
                        exps(f"n{l}", arg[0], 8 * l + arg[0])
                    elif step == "values":
                        turned_copies(f"n{l}", arg[0], 8 * l + arg[0])
                    elif step == "mix":
                        drained(act, f"nz1_{l}")
                        f(FLV[:, :], HZ[:, :], ACT.Sigmoid).then_inc(sig_ready, 1)
                        f(SG[:, :], SG[:, :], ACT.Sigmoid).then_inc(sig_ready, 1)
                        f(VH[:, :], NZ[:, :], ACT.Sigmoid).then_inc(sig_ready, 1)
                squares(nidx, lambda g: drained(act, f"wo_{l}_{g}"))

                def pp_out(g):
                    copy_out(f"pp{g}_{l}", PP[:, g * 512:(g + 1) * 512], bank(f"pp{g}_{l}")[:, :])

                pp_out(0)
                pp_out(1)
                norm(nidx)
                nidx += 1
                pp_out(2)
                pp_out(3)
                for g in range(4):
                    name = f"pg{g}_{l}"
                    full(act, name)
                    f(Y[:, g * 512:(g + 1) * 512], bank(name)[:, :], ACT.Sigmoid).then_inc(free(name), 1)

            pidx = 8 * DEPTH
            for l in range(DEPTH):
                if l == 0:
                    squares(nidx, lambda g: act.wait_ge(h_ready, 4 * DEPTH + g - 3))
                    norm(nidx)
                    nidx += 1

                    def first_tap(c, src, dst, w, bias):
                        return f(dst, src, ACT.Identity, scale=w, bias=bias)

                    for g in range(2):
                        full(act, f"xa{g}")
                        for j in range(2):
                            c = 2 * g + j
                            ins = first_tap(c, bank(f"xa{g}")[:, j * T:(j + 1) * T], FG[:, c * T:(c + 1) * T],
                                            vec("lru_conv_w_2", 12 + c), vec("lru_conv_b_2", c))
                        ins.then_inc(conv_ready, 1)
                    for g in range(2):
                        copy_out(f"cp{g}", KQ[:, g * 512:(g + 1) * 512], bank(f"cp{g}")[:, :])
                    for g in range(2):
                        drained(act, f"vb{g}")
                        for j in range(2):
                            c = 2 * g + j
                            ins = first_tap(c, QP[:, c * T:(c + 1) * T], FLV[:, c * T:(c + 1) * T],
                                            vec("sconv_w_2", 8 + c), vec("sconv_b_2", c))
                        ins.then_inc(conv_ready, 1)
                    for name, dst, bias in (("lr", HZ, "lru_ba_2"), ("li", NZ, "lru_bx_2")):
                        for g in range(2):
                            full(act, f"{name}{g}")
                            for j in range(2):
                                c = 2 * g + j
                                ins = f(dst[:, c * T:(c + 1) * T], bank(f"{name}{g}")[:, j * T:(j + 1) * T],
                                        ACT.Sigmoid, bias=vec(bias, c))
                            ins.then_inc(free(f"{name}{g}"), 1)
                    drained(act, "lr1")
                    act.wait_ge(small_ready, 1)
                    for c in range(4):
                        ins = f(QR[:, c * T:(c + 1) * T], HZ[:, c * T:(c + 1) * T], ACT.Tanh,
                                scale=SPC[:, 4 + c:5 + c])
                    ins.then_inc(act_part, 1)
                    for c in range(4):
                        ins = f(QN[:, c * T:(c + 1) * T], HZ[:, c * T:(c + 1) * T], ACT.Exp, scale=SPC[:, c:c + 1])
                    ins.then_inc(act_part, 1)
                    act.wait_ge(dve_part, 2)
                    f(QR[:, :], QR[:, :], ACT.Sqrt).then_inc(act_part, 1)
                    for g in range(2):
                        full(act, f"ga{g}")
                        f(SG[:, g * 512:(g + 1) * 512], bank(f"ga{g}")[:, :],
                          ACT.Gelu_apprx_tanh).then_inc(free(f"ga{g}"), 1)
                else:
                    squares(nidx, lambda g: drained(act, f"down{g}_0"))
                    norm(nidx)
                    nidx += 1
                    for g in range(2):
                        full(act, f"fq{g}")
                        nc.scalar.mul(QR[:, g * 512:(g + 1) * 512], bank(f"fq{g}")[:, :],
                                      0.125).then_inc(free(f"fq{g}"), 1)
                    for g in range(2):
                        full(act, f"fk{g}")
                        src = v3(bank(f"fk{g}"), 2)
                        nc.scalar.copy(kz[0:64, g, 0, :, :], src[0:64])
                        nc.scalar.copy(kz[64:128, g, 1, :, :], src[64:128]).then_inc(free(f"fk{g}"), 1)
                    act.wait_ge(dve_part, 3)
                    link(f(SS[0:8, :], SS[0:8, :], ACT.Exp))
                    f(SS[0:8, :], SS[0:8, :], ACT.Ln, bias=EPSC[0:8, 1:2]).then_inc(act_part, 1)
                    for n in range(NT):
                        copy_out(f"fv{n}", vh[:, n, :], bank(f"fv{n}")[:, :])
                    for n in range(NT):
                        full(act, f"zg{n}")
                        f(QN[:, n * 512:(n + 1) * 512], bank(f"zg{n}")[:, :],
                          ACT.Gelu_apprx_tanh).then_inc(free(f"zg{n}"), 1)
                    drained(act, "zg1")
                    f(SQ[:, 0:1024], QN[:, :], ACT.Square).then_inc(act_part, 1)
                    full(act, "zu0")
                    f(SG[:, 0:512], bank("zu0")[:, :], ACT.Gelu_apprx_tanh).then_inc(free("zu0"), 1)
                    log_exp()
                    act.wait_ge(dve_part, 4)
                    link(f(NT16[:, :], NT16[:, :], ACT.Ln, bias=EPSC[:, 0:1], scale=1.0 / 64))
                    f(NT16[:, :], NT16[:, :], ACT.Exp, scale=-0.5).then_inc(act_part, 1)
                    for step, *arg in agenda[DEPTH + l]:
                        if step == "scores":
                            exps("f", arg[0], pidx + arg[0])
                        elif step == "values":
                            turned_copies("f", arg[0], pidx + arg[0])
                        elif step == "zu1":
                            copy_out("zu1", SG[:, 512:1024], bank("zu1")[:, :])
                    drained(act, "zu1")
                    f(SG[:, 512:1024], SG[:, 512:1024], ACT.Gelu_apprx_tanh).then_inc(act_part, 1)

                squares(nidx, lambda g: drained(act, f"wm_{l}_{g}"))
                norm(nidx)
                nidx += 1
                up0, _ = ffn_base[l]
                w0, b0 = VEC_AT["ffn_conv_w_2"] + l * 3 * 2 * NFF, VEC_AT["ffn_conv_b_2"] + l * 2 * NFF

                def rounds(par, i, first=False):
                    for half in range(2):
                        act.wait_ge(psum_full[2 * par + half], i + (up0[2 * par + half] + 1))
                    if not (first and l == 0):
                        prev = 2 * i + (par - 1) + FF_ROUNDS * l if not first else FF_ROUNDS * l
                        act.wait_ge(act_ready, prev)
                    for half in range(2):
                        for j in range(2):
                            c = 2 * half + j
                            m = i * 4 + (2 * par + j + half * NFF)
                            ins = f(glu[par][:, c, :], ps[2 * par + half][:, j * T:(j + 1) * T], ACT.Identity,
                                    scale=VC[:, bass.ds(m + (w0 + 2 * 2 * NFF), 1)],
                                    bias=VC[:, bass.ds(m + b0, 1)])
                    ins.then_inc(taps_ready, 1)
                    act.wait_ge(psum_free[2 * par], i + (up0[2 * par] + 1))
                    f(glu[par][:, 0:2, :], glu[par][:, 0:2, :], ACT.Silu).then_inc(silu_ready, 1)

                rounds(0, 0, first=True)
                rounds(1, 0, first=True)
                with act.Fori(1, FF_ROUNDS // 2) as i:
                    rounds(0, i)
                    rounds(1, i)
                rounds(0, FF_ROUNDS // 2)

            squares(nidx, lambda g: drained(act, f"down{g}_1"))
            norm(nidx)
            for n in range(NT):
                for g in range(2):
                    copy_out(f"out{2 * n + g}", Y[:, n * D + g * 512:n * D + (g + 1) * 512],
                             bank(f"out{2 * n + g}")[:, :])
                drained(act, f"out{2 * n + 1}")
                act.dma_start(out[0, n * P:(n + 1) * P, :], Y[:, n * D:(n + 1) * D]).then_inc(out_stored, 16)
            act.wait_ge(out_stored, 16 * NT)

        @block.vector
        def _(dve):
            steps = [0]
            V = nc.vector

            def step(ins):
                steps[0] += 1
                ins.then_inc(dve_step, 1)

            def settle():
                dve.wait_ge(dve_step, steps[0])

            def link(ins):
                step(ins)
                settle()

            def wide(col, shape):
                return col.to_broadcast(shape)

            def normed(nidx, gain, g0):
                dve.wait_ge(rinv_ready, nidx + 1)
                if nidx > 0:
                    full(dve, normed_last[nidx - 1])
                for c in range(ND):
                    V.scalar_tensor_tensor(xn3[:, c, :], h3[:, c, :], vec(gain, g0 + c), RINV[:, :],
                                           ALU.mult, ALU.mult).then_inc(xn_ready, 1)

            def row_max(tag, u, pidx):
                bb = pidx % 2
                for n, x in ((0, "Y"), (1, "X")):
                    full(dve, f"{tag}{x}{u}")
                    s3 = bank(f"{tag}{x}{u}")[:, 0:2 * (n + 1) * P].rearrange("p (r s) -> p r s", r=2)
                    ins = V.tensor_reduce(NM[:, 4 * bb + 2 * n:4 * bb + 2 * n + 2], s3, AX_X, ALU.max, negate=True)
                ins.then_inc(nmax_ready, 1)

            def normalise(tag, u, pidx, gate=None):
                bb = pidx % 2
                s4 = SM[:, 4 * bb:4 * bb + 4]
                drained(dve, f"{tag}X{u}")
                link(V.tensor_scalar(s4, s4, 1e-30, None, ALU.max))
                link(V.reciprocal(s4, s4))
                if gate is not None:
                    link(V.tensor_tensor(s4.rearrange("p (n r) -> p n r", n=NT),
                                         s4.rearrange("p (n r) -> p n r", n=NT), gate, ALU.mult))
                for n in range(NT):
                    w = (n + 1) * P
                    ins = V.tensor_tensor(probs[bb][n], probs[bb][n],
                                          s4[:, 2 * n:2 * n + 2].unsqueeze(2).to_broadcast([P, 2, w]), ALU.mult)
                ins.then_inc(p_ready, 1)

            def add_out(prefix, suffix=""):
                for g in range(4):
                    name = f"{prefix}{g}{suffix}"
                    full(dve, name)
                    s = slice(g * 512, (g + 1) * 512)
                    V.tensor_tensor(H[:, s], H[:, s], bank(name)[:, :], ALU.add).then_inc(free(name), 1)

            V.memset(EPSC[:, 0:1], EPS)
            V.memset(EPSC[:, 1:2], 1.0).then_inc(eps_ready, 1)
            for t in (AD, KZ, KCZ):
                V.memset(t[:, :], 0.0)
            step(V.memset(ZR[:, :], 0.0))
            dve.wait_ge(const_landed, 32)
            V.tensor_copy(IDB[:, :], ident)
            step(V.tensor_copy(NGB[:, :], const("causal_neg")))
            for g in range(4):
                full(dve, f"x{g}")
                V.tensor_copy(H[:, g * 512:(g + 1) * 512], bank(f"x{g}")[:, :]).then_inc(free(f"x{g}"), 1)
            settle()
            for g in range((NVT + 3) // 4):
                drained(dve, f"vec{g}")
            lb = vec("hgrn_lb", 0, 8)
            mx, e = LB[:, 16:20], SPC[:, 8:16]
            link(V.tensor_tensor(mx, lb[:, 0:4], lb[:, 4:8], ALU.max))
            for l in range(DEPTH):
                V.tensor_tensor(e[:, 4 * l:4 * l + 4], lb[:, 4 * l:4 * l + 4], mx, ALU.subtract)
            lam = vec("lru_lambda_2", 0, 4)
            V.scalar_tensor_tensor(SPC[:, 16:20], lam, -1.0, lam, ALU.mult, ALU.min).then_inc(dve_part, 1)
            V.tensor_scalar(GQ[:, :], vec("nsa_qnorm_g", 0, 2), 0.125, None, ALU.mult)
            dve.wait_ge(act_part, 1)
            link(V.tensor_tensor(mx, e[:, 0:4], e[:, 4:8], ALU.add))
            link(V.reciprocal(mx, mx))
            for l in range(DEPTH):
                step(V.tensor_tensor(e[:, 4 * l:4 * l + 4], e[:, 4 * l:4 * l + 4], mx, ALU.mult))
            settle()
            V.tensor_tensor(LB[:, 0:4], e[:, 0:4], e[:, 0:4], ALU.subtract)
            link(V.tensor_tensor(LB[:, 4:8], e[:, 0:4], e[:, 4:8], ALU.add))
            link(V.tensor_tensor(LB[:, 4:8], LB[:, 4:8], e[:, 0:4], ALU.subtract))
            link(V.tensor_scalar(LB[:, 8:16], LB[:, 0:8], -1.0, 1.0, ALU.mult, ALU.add))

            for l in range(DEPTH):
                normed(2 * l, "norm_g", 8 * l)
                drained(dve, f"hf0_{l}")
                drained(dve, f"hf1_{l}")
                for c in range(4):
                    low, rest = LB[:, 4 * l + c:4 * l + c + 1], LB[:, 8 + 4 * l + c:8 + 4 * l + c + 1]
                    s = slice(c * T, (c + 1) * T)
                    step(V.tensor_scalar(FG[:, s], FG[:, s], rest, low, ALU.mult, ALU.add))
                    ins = V.tensor_scalar(KQ[:, s], KQ[:, s], rest, None, ALU.mult)
                ins.then_inc(hg_ready, 1)

                def level(n, g):
                    name = f"lv{n}_{g}_{l}"
                    full(dve, name)
                    V.copy_predicated(AD[:, g * 512:(g + 1) * 512].rearrange("p (j t) -> p j t", j=4),
                                      v3(LM, NLVL)[:, n:n + 1, :].to_broadcast([P, 4, P]),
                                      v3(bank(name), 4)).then_inc(free(name), 1)
                    q, k = QP[:, g * 512:(g + 1) * 512], KQ[:, g * 512:(g + 1) * 512]
                    if n == 0:
                        settle()
                        V.tensor_tensor(q, q, FG[:, g * 512:(g + 1) * 512], ALU.mult).then_inc(level_ready, 1)
                        return
                    dve.wait_ge(level_ready, 16 * l + 2 * (n - 1) + g + 1)
                    h = 1 << (n - 1)
                    nb = 512 // (2 * h)
                    f_in = flevel[n - 1][:, g * (512 >> (n - 1)):(g + 1) * (512 >> (n - 1))]
                    f_in = f_in.rearrange("p (b e) -> p b e", e=2)
                    q = q.rearrange("p (b e t) -> p b e t", e=2, t=h)
                    k = k.rearrange("p (b e t) -> p b e t", e=2, t=h)
                    settle()
                    if n < NLVL - 1:
                        f_out = flevel[n][:, g * (512 >> n):(g + 1) * (512 >> n)]
                        step(V.tensor_tensor(f_out, f_in[:, :, 0], f_in[:, :, 1], ALU.mult))
                    V.tensor_tensor(q[:, :, 1, :], q[:, :, 1, :], f_in[:, :, 0:1].to_broadcast([P, nb, h]), ALU.mult)
                    V.tensor_tensor(k[:, :, 0, :], k[:, :, 0, :], f_in[:, :, 1:2].to_broadcast([P, nb, h]),
                                    ALU.mult).then_inc(level_ready, 1)

                for kind, *arg in agenda[l]:
                    if kind == "level":
                        level(*arg)
                    elif kind == "blocks":
                        drained(dve, f"kcvc_{l}")
                        pe3 = vec("cmp_pe", 32 * l, 32).rearrange("p (kv jj) -> p kv jj", kv=2)
                        V.memset(M2[:, :, :, :, NCMP:16], 0.0)
                        for kv in range(2):
                            for g in range(2):
                                src = K2[:, kv, g, 0:T].rearrange("p (c jj two) -> p jj c two", jj=8, two=2)
                                for hi in range(2):
                                    ins = V.tensor_tensor(
                                        M2[:, kv, 8 * hi:8 * hi + 8, g, 0:NCMP],
                                        src[:, :, hi:hi + NCMP, 0],
                                        pe3[:, kv, 8 * hi:8 * hi + 8].unsqueeze(2).to_broadcast([P, 8, NCMP]),
                                        ALU.add)
                        ins.then_inc(blocks_ready, 1)
                    elif kind == "gates":
                        drained(dve, f"vw_{l}")
                        link(V.tensor_scalar(GT[:, :], GT[:, :], 1.0, None, ALU.add))
                        V.reciprocal(GT[:, :], GT[:, :]).then_inc(gates_ready, 1)
                    elif kind == "q_norm":
                        dve.wait_ge(q_rinv_ready, l + 1)
                        link(V.scalar_tensor_tensor(QN[:, :], QN[:, :], GQ[:, l:l + 1], RBIG[:, :],
                                                    ALU.mult, ALU.mult))
                        qn4 = v3(QN, 4)
                        for i, tab in enumerate(("cos", "sin")):
                            ins = V.tensor_tensor(UW[:, i * 1024:(i + 1) * 1024].rearrange("p (j t) -> p j t", j=4),
                                                  qn4, const(tab).unsqueeze(1).to_broadcast([P, 4, T]), ALU.mult)
                        ins.then_inc(rope_ready, 1)
                    elif kind == "k_norm":
                        dve.wait_ge(k_rinv_ready, l + 1)
                        for j in range(2):
                            s = slice(j * T, (j + 1) * T)
                            step(V.scalar_tensor_tensor(KN[:, s], KN[:, s], vec("nsa_knorm_g", 3 * l + 1 + j),
                                                        UK[:, 512 + j * T:512 + (j + 1) * T], ALU.mult, ALU.mult))
                        settle()
                        for i, tab in enumerate(("cos", "sin")):
                            ins = V.tensor_tensor(UK[:, i * 512:(i + 1) * 512].rearrange("p (j t) -> p j t", j=2),
                                                  v3(KN, 2), const(tab).unsqueeze(1).to_broadcast([P, 2, T]),
                                                  ALU.mult)
                        ins.then_inc(k_rope_ready, 1)
                    elif kind == "hidden":
                        dve.wait_ge(hid_exp_ready, l + 1)
                        link(V.tensor_scalar(SS[:, 0:64], SS[:, 0:64], 1.0, None, ALU.add))
                        link(V.reciprocal(SS[:, 0:64], SS[:, 0:64]))
                        V.tensor_tensor(HID[:, :], bank(f"hid_{l}")[:, 0:64], SS[:, 0:64],
                                        ALU.mult).then_inc(free(f"hid_{l}"), 1)
                        drained(dve, f"hid_{l}")
                        V.tensor_copy(HIDV[:, :].rearrange("p (g r c) -> p g r c", g=2, r=4),
                                      HID[:, 32:64].rearrange("p (g c) -> p g c", g=2).unsqueeze(2)
                                      .to_broadcast([P, 2, 4, 16])).then_inc(hidden_ready, 1)
                    elif kind == "cmp_kv":
                        full(dve, f"vc_{l}")
                        V.tensor_tensor(v3(VCB, 8), const("head16").unsqueeze(2).to_broadcast([P, 8, 64]),
                                        bank(f"vc_{l}")[:, 0:64].unsqueeze(1).to_broadcast([P, 8, 64]),
                                        ALU.mult).then_inc(free(f"vc_{l}"), 1)
                    elif kind == "kc_norm":
                        dve.wait_ge(kc_rinv_ready, l + 1)
                        for r in range(2):
                            h = slice(64 * r, 64 * r + 64)
                            ins = V.scalar_tensor_tensor(KCZ[h, 32 * r:32 * r + 32], KC[h, 0:32],
                                                         vec("nsa_knorm_g", 3 * l)[h, :], SS[h, 64:96],
                                                         ALU.mult, ALU.mult)
                        ins.then_inc(kc_ready, 1)
                    elif kind == "o_norm":
                        dve.wait_ge(o_rinv_ready, l + 1)
                        step(V.scalar_tensor_tensor(QP[:, :], QP[:, :], vec("hgrn_onorm_g", l), RBIG[:, :],
                                                    ALU.mult, ALU.mult))
                    elif kind == "cmp_softmax":
                        name = f"cs_{l}"
                        full(dve, name)
                        s4 = SC[:, :].rearrange("p (n h c) -> p n h c", n=NT, h=8)
                        s3 = SC[:, :].rearrange("p (q c) -> p q c", c=16)
                        r2 = SS[:, 96:112]

                        def by_tile(tab):
                            return const(tab).rearrange("p (n c) -> p n c", n=NT).unsqueeze(2) \
                                .to_broadcast([P, NT, 8, 16])

                        V.tensor_tensor(s4, by_tile("cmp_neg"),
                                        bank(name)[:, 0:256].rearrange("p (n h c) -> p n h c", n=NT, h=8),
                                        ALU.add).then_inc(free(name), 1)
                        drained(dve, name)
                        link(V.tensor_reduce(r2, s3, AX_X, ALU.max))
                        V.tensor_tensor(s3, s3, r2.unsqueeze(2).to_broadcast([P, 16, 16]),
                                        ALU.subtract).then_inc(cmp_shift_ready, 1)
                        dve.wait_ge(cmp_exp_ready, l + 1)
                        link(V.tensor_tensor(s4, s4, by_tile("cmp_seen"), ALU.mult))
                        link(V.tensor_reduce(r2, s3, AX_X, ALU.add))
                        link(V.tensor_scalar(r2, r2, 1e-30, None, ALU.max))
                        link(V.reciprocal(r2, r2))
                        link(V.tensor_tensor(r2.rearrange("p (n h) -> p n h", n=NT),
                                             r2.rearrange("p (n h) -> p n h", n=NT), gates[:, :, 0:8], ALU.mult))
                        V.tensor_tensor(s3, s3, r2.unsqueeze(2).to_broadcast([P, 16, 16]),
                                        ALU.mult).then_inc(cp_ready, 1)
                    elif kind == "scores":
                        row_max(f"n{l}", arg[0], 8 * l + arg[0])
                    elif kind == "values":
                        u = arg[0]
                        g0 = 8 * (u // 4 + 1) + 2 * (u % 4)
                        normalise(f"n{l}", u, 8 * l + u, gates[:, :, g0:g0 + 2])
                    elif kind == "mix":
                        dve.wait_ge(sig_ready, 3 * l + 1)
                        link(V.tensor_tensor(HZ[:, :], HZ[:, :], FLV[:, :], ALU.mult))
                        dve.wait_ge(sig_ready, 3 * l + 2)
                        link(V.tensor_tensor(HZ[:, :], HZ[:, :], SG[:, :], ALU.mult))
                        V.tensor_tensor(Y[:, 0:1024], QP[:, :], HZ[:, :], ALU.mult)
                        dve.wait_ge(sig_ready, 3 * l + 3)
                        link(V.tensor_tensor(NZ[:, :], NZ[:, :], VH[:, :], ALU.mult))
                        for g in range(2):
                            name = f"on{g}_{l}"
                            full(dve, name)
                            V.tensor_tensor(Y[:, 1024 + g * 512:1024 + (g + 1) * 512], bank(name)[:, :],
                                            NZ[:, g * 512:(g + 1) * 512], ALU.mult).then_inc(free(name), 1)
                add_out(f"wo_{l}_")
                normed(2 * l + 1, "ple_norm_g", 8 * l)
                for g in range(4):
                    drained(dve, f"pg{g}_{l}")
                    drained(dve, f"pp{g}_{l}")
                    s = slice(g * 512, (g + 1) * 512)
                    link(V.tensor_tensor(Y[:, s], Y[:, s], PP[:, s], ALU.mult))
                    V.tensor_tensor(H[:, s], H[:, s], Y[:, s], ALU.add).then_inc(h_ready, 1)

            z, s, s2, q = SPC[:, 16:20], SPC[:, 20:24], SPC[:, 24:28], SPC[:, 28:32]
            link(V.tensor_scalar(s, z, 2.0, None, ALU.add))
            link(V.reciprocal(s, s))
            link(V.tensor_tensor(s, s, z, ALU.mult))
            link(V.tensor_tensor(s2, s, s, ALU.mult))
            link(V.tensor_scalar(q, s2, 1.0 / 19, None, ALU.mult))
            for k in range(17, 1, -2):
                link(V.scalar_tensor_tensor(q, q, 1.0 / k, s2, ALU.add, ALU.mult))
            link(V.tensor_scalar(q, q, 1.0, 2.0, ALU.add, ALU.mult))
            link(V.tensor_tensor(q, q, s, ALU.mult))
            link(V.tensor_scalar(s, vec("lru_lambda_2", 0, 4), -1.0, 0.0, ALU.mult, ALU.max))
            link(V.tensor_tensor(q, q, s, ALU.add))
            V.tensor_scalar(SPC[:, 0:4], q, -8.0, None, ALU.mult)
            V.tensor_scalar(SPC[:, 4:8], q, 8.0, None, ALU.mult).then_inc(small_ready, 1)

            nidx = 2 * DEPTH
            for l in range(DEPTH):
                if l == 0:
                    normed(nidx, "mix0_norm_2", 0)
                    V.memset(PB[:, 0:1024], 0.0).then_inc(bd_zeroed, 1)

                    def taps(name, g, src, dst, wname, n):
                        for back in range(1, n):
                            for j in range(2):
                                c = 2 * g + j
                                d = dst[:, c * T + back:(c + 1) * T]
                                ins = V.scalar_tensor_tensor(d, src(j)[:, 0:T - back],
                                                             vec(wname, 4 * (n - 1 - back) + c), d,
                                                             ALU.mult, ALU.add)
                                if back < n - 1 or j == 0:
                                    step(ins)
                            settle()
                        return ins

                    for g in range(2):
                        dve.wait_ge(conv_ready, g + 1)
                        src = bank(f"xa{g}")
                        taps(f"xa{g}", g, lambda j: src[:, j * T:(j + 1) * T], FG, "lru_conv_w_2",
                             4).then_inc(free(f"xa{g}"), 1)
                    for g in range(2):
                        drained(dve, f"cp{g}")
                        full(dve, f"vb{g}")
                        V.tensor_tensor(QP[:, g * 512:(g + 1) * 512], bank(f"vb{g}")[:, :],
                                        KQ[:, g * 512:(g + 1) * 512], ALU.mult).then_inc(free(f"vb{g}"), 1)
                    for g in range(2):
                        dve.wait_ge(conv_ready, 3 + g)
                        step(taps(None, g, lambda j: QP[:, (2 * g + j) * T:(2 * g + j + 1) * T], FLV,
                                  "sconv_w_2", 3))
                    drained(dve, "li1")
                    link(V.tensor_tensor(NZ[:, :], NZ[:, :], FG, ALU.mult))
                    dve.wait_ge(act_part, 3)
                    link(V.tensor_tensor(UW[:, 0:1024], QN[:, :], QN[:, :], ALU.mult))
                    V.scalar_tensor_tensor(QR[:, :], UW[:, 0:1024], 1.0, QR[:, :], ALU.add,
                                           ALU.mult).then_inc(dve_part, 1)
                    dve.wait_ge(act_part, 4)
                    link(V.tensor_tensor(QR[:, :], QR[:, :], NZ[:, :], ALU.mult))
                    for c in range(4):
                        s = slice(c * T, (c + 1) * T)
                        step(V.tensor_tensor_scan(UW[:, 1024 + c * T:1024 + (c + 1) * T], QN[:, s], QR[:, s], 0.0,
                                                  ALU.mult, ALU.add))
                    for g in range(2):
                        full(dve, f"bp{g}")
                        V.tensor_tensor(Y[:, 1024 + g * 512:1024 + (g + 1) * 512], bank(f"bp{g}")[:, :],
                                        FLV[:, g * 512:(g + 1) * 512], ALU.mult).then_inc(free(f"bp{g}"), 1)
                    settle()
                    drained(dve, "ga0")
                    drained(dve, "ga1")
                    V.tensor_tensor(Y[:, 0:1024], UW[:, 1024:2048], SG[:, :], ALU.mult).then_inc(y_ready, 1)
                else:
                    normed(nidx, "mix1_norm_2", 0)
                    dve.wait_ge(bias_landed, 16)
                    full(dve, "fl")
                    V.tensor_scalar(SC[0:8, :], bank("fl")[0:8, 0:T], BF[0:8, 0:1], None,
                                    ALU.add).then_inc(free("fl"), 1)
                    drained(dve, "fl")
                    V.scalar_tensor_tensor(SS[0:8, :], SC[0:8, :], -1.0, SC[0:8, :], ALU.mult,
                                           ALU.min).then_inc(dve_part, 1)
                    link(V.tensor_scalar(SC[0:8, :], SC[0:8, :], 0.0, None, ALU.min))
                    dve.wait_ge(act_part, 5)
                    link(V.tensor_tensor(SC[0:8, :], SS[0:8, :], SC[0:8, :], ALU.subtract))
                    link(V.tensor_tensor_scan(PCT[0:8, :], ones[0:8, 0:1].to_broadcast([8, T]), SC[0:8, :], 0.0,
                                              ALU.mult, ALU.add))
                    V.tensor_tensor(UW[0:8, :].rearrange("p (h t) -> p h t", h=8),
                                    PCT[0:8, :].unsqueeze(1).to_broadcast([8, 8, T]),
                                    ident[0:8, 0:8].unsqueeze(2).to_broadcast([8, 8, T]),
                                    ALU.mult).then_inc(forget_ready, 1)
                    for g in range(2):
                        full(dve, f"wt{g}")
                        V.tensor_tensor(AD[:, g * 512:(g + 1) * 512].rearrange("p (j t) -> p j t", j=4),
                                        v3(bank(f"wt{g}"), 4), const("upper").unsqueeze(1).to_broadcast([P, 4, P]),
                                        ALU.mult).then_inc(free(f"wt{g}"), 1)
                    dve.wait_ge(act_part, 6)
                    V.tensor_reduce(NT16[:, :], SQ[:, 0:1024].rearrange("p (q d) -> p q d", d=64), AX_X,
                                    ALU.add).then_inc(dve_part, 1)
                    todo = list(agenda[DEPTH + l])
                    for kind, *arg in todo:
                        if kind == "scores":
                            row_max("f", arg[0], 8 * DEPTH + arg[0])
                            if arg[0] == 0:
                                dve.wait_ge(act_part, 7)
                                V.tensor_tensor(QN[:, :].rearrange("p (q d) -> p q d", d=64),
                                                QN[:, :].rearrange("p (q d) -> p q d", d=64),
                                                NT16[:, :].unsqueeze(2).to_broadcast([P, 16, 64]),
                                                ALU.mult).then_inc(sgu_ready, 1)
                        elif kind == "values":
                            normalise("f", arg[0], 8 * DEPTH + arg[0])
                        elif kind in ("sg0", "sg1"):
                            g = int(kind[2])
                            full(dve, kind)
                            if g == 0:
                                dve.wait_ge(bt_landed, 16 * 8)
                            for j in range(2):
                                c = 2 * g + j
                                ins = V.scalar_tensor_tensor(
                                    v3(HZ, 4)[:, c, :].rearrange("p (n t) -> p n t", n=NT),
                                    bank(kind)[:, j * T:(j + 1) * T].rearrange("p (n t) -> p n t", n=NT),
                                    vec("sgu_norm_2", c), v3(AC, 4)[:, c:c + 1, :].to_broadcast([P, NT, P]),
                                    ALU.mult, ALU.add)
                            ins.then_inc(free(kind), 1)
                    for g in range(2):
                        full(dve, f"fo{g}")
                        V.tensor_copy(Y[:, 1024 + g * 512:1024 + (g + 1) * 512],
                                      bank(f"fo{g}")[:, :]).then_inc(free(f"fo{g}"), 1)
                    drained(dve, "sg1")
                    dve.wait_ge(act_part, 8)
                    V.tensor_tensor(Y[:, 0:1024], HZ[:, :], SG[:, :], ALU.mult).then_inc(y_ready, 1)
                nidx += 1
                add_out(f"wm_{l}_")

                normed(nidx, "ffn_norm_2", 8 * l)
                nidx += 1
                w0 = VEC_AT["ffn_conv_w_2"] + l * 3 * 2 * NFF

                def rounds(par, i):
                    dve.wait_ge(taps_ready, 2 * i + (par + 1 + FF_ROUNDS * l))
                    for back in (1, 2):
                        if back == 2:
                            dve.wait_ge(first_back_done, 2 * i + (par + 1 + FF_ROUNDS * l))
                        for half in range(2):
                            for j in range(2):
                                m = i * 4 + (2 * par + j + half * NFF)
                                d = glu[par][:, 2 * half + j, back:T]
                                ins = V.scalar_tensor_tensor(
                                    d, ps[2 * par + half][:, j * T:(j + 1) * T - back],
                                    VC[:, bass.ds(m + (w0 + (2 - back) * 2 * NFF), 1)], d, ALU.mult, ALU.add)
                            if back == 2:
                                ins.then_inc(psum_free[2 * par + half], 1)
                        if back == 1:
                            ins.then_inc(first_back_done, 1)
                    up0, _ = ffn_base[l]
                    dve.wait_ge(psum_free[2 * par + 1], i + (up0[2 * par + 1] + 1))
                    dve.wait_ge(silu_ready, 2 * i + (par + 1 + FF_ROUNDS * l))
                    V.tensor_tensor(act3[par], glu[par][:, 0:2, :], glu[par][:, 2:4, :],
                                    ALU.mult).then_inc(act_ready, 1)

                rounds(0, 0)
                rounds(1, 0)
                with dve.Fori(1, FF_ROUNDS // 2) as i:
                    rounds(0, i)
                    rounds(1, i)
                rounds(0, FF_ROUNDS // 2)
                add_out(f"down", f"_{l}")

            normed(nidx, "final_norm_2", 0)

        @block.sync
        def _(sp):
            occupant = [None] * SLOTS

            def slot_for(key):
                s, _ = PLACE[key]
                if occupant[s] is not None:
                    sp.wait_ge(*panel_free[occupant[s]])
                occupant[s] = key
                return s

            def load(key, dst, src):
                sp.dma_start(dst, src).then_inc(panel_landed[PLACE[key][0]], 16)

            def columns(w, c0, n):
                return w[:, c0:c0 + n].rearrange("(k p) n -> p k n", p=P)

            def panel_of(key, w, c0, n=512, nk=ND):
                s = slot_for(key)
                load(key, ring[s][:, 0:nk * n].rearrange("p (k n) -> p k n", k=nk), columns(w, c0, n))

            sp.dma_start(CN[:, :], a["const_table"]).then_inc(const_landed, 16)
            sp.dma_start(xt, a["x"][0].rearrange("(n p) d -> p n d", p=P)).then_inc(x_landed, 16)
            for tile, r, n, c0, c1, src in vec_dmas:
                sp.dma_start(vrows[r:r + n, tile, c0:c1], src).then_inc(vec_landed, 16)
            sp.dma_start(ptok.rearrange("p (l n) d -> p l n d", l=DEPTH),
                         a["p"][:, 0].rearrange("l (n p) d -> p l n d", p=P)).then_inc(p_landed, 16)
            sp.dma_start(LM[:, :], a["mask_table"]).then_inc(const_landed, 16)
            sp.dma_start(BF[0:8, 0:1], a["fox_bf_2"].rearrange("a h -> h a")).then_inc(bias_landed, 16)

            first = {"hq": 0, "hf": 512, "hi": 1024, "hgo": 1536, "hz": 2048, "nq": 2560, "kv": 3072}
            for l in range(DEPTH):
                w = a["w_in"][l]
                for name in FIRST_PANELS:
                    key = (name, l)
                    if name in first:
                        panel_of(key, w, first[name])
                    elif name == "kw":
                        s = slot_for(key)
                        load(key, ring[s].rearrange("p (k n) -> p k n", k=ND)[:, :, 0:280], columns(w, 3584, 280))
                    elif name == "nz":
                        panel_of(key, w, IN1 - HALF)
                    elif name in ("wo0", "wo1"):
                        panel_of(key, a["w_out"][l], 512 * int(name[2]))
                    elif name in ("pg0", "pg1"):
                        panel_of(key, a["w_pg"][l], 512 * int(name[2]))
                    elif name == "pp":
                        panel_of(key, a["w_pp"][l], 0, n=D, nk=2)
                    elif name == "cmp1":
                        s = slot_for(key)
                        load(key, ring[s].rearrange("p (kv jj n) -> p kv jj n", kv=2, jj=16),
                             a["cmp_w1"][l].rearrange("kv (jj p) n -> p kv jj n", p=P))
                        if l > 0:
                            b, k = fills[f"vc_{l - 1}"]
                            sp.wait_ge(psum_full[b], k + 1)
                        for c0, kv in ((0, 0), (64, 0), (P, 1)):
                            sp.dma_start(W2[:, c0:c0 + 64], a["cmp_w2"][l, kv]).then_inc(w2_landed, 16)

            def ffn(l):
                up0, loads = ffn_base[l]

                def loads_of(par, i, first=False):
                    if first:
                        slot_for(("up", l, par))
                    else:
                        b = 2 * par + 1
                        sp.wait_ge(psum_full[b], i + up0[b])
                    c = i * 512 + par * T
                    wup = a["ffn_up_2"][l].rearrange("(k p) n -> p k n", p=P)
                    w3 = ring[par].rearrange("p (k n) -> p k n", k=ND)
                    sp.dma_start(w3[:, :, 0:T], wup[:, :, bass.ds(c, T)]).then_inc(panel_landed[par], 16)
                    sp.dma_start(w3[:, :, T:2 * T], wup[:, :, bass.ds(c + FF, T)]).then_inc(value_landed[par], 16)
                    if first:
                        slot_for(("down", l, par))
                    else:
                        sp.wait_ge(down_done, 2 * i + (par - 1 + (FF_ROUNDS - 1) * l))
                    wdn = a["ffn_down_2"][l][bass.ds(c, T), :].rearrange("(k p) n -> p k n", p=P)
                    sp.dma_start(ring[2 + par][:, 0:2048].rearrange("p (k n) -> p k n", k=2),
                                 wdn).then_inc(panel_landed[2 + par], 16)

                loads_of(0, 0, first=True)
                loads_of(1, 0, first=True)
                with sp.Fori(1, FF_ROUNDS // 2) as i:
                    loads_of(0, i)
                    loads_of(1, i)
                loads_of(0, FF_ROUNDS // 2)

            even = {"xa": 0, "ga": 512, "cp": 1024, "bp": 1536, "vb": 2048}
            odd = {"zu": 0, "zg": 512, "fq": 1024, "fk": 1536, "fv": 2048}
            for l in range(DEPTH):
                for name in (EVEN_PANELS, ODD_PANELS)[l]:
                    key = (name, DEPTH + l)
                    if name in ("wo0", "wo1"):
                        panel_of(key, a[("mix0_w_out_2", "mix1_w_out_2")[l]][0], 512 * int(name[2]))
                    elif name == "ff":
                        panel_of(key, a["mix1_w_in_2"][0], 2560, n=8)
                    else:
                        panel_of(key, a[("mix0_w_in_2", "mix1_w_in_2")[l]][0], (even, odd)[l][name])
                    if name == "vb":
                        sp.wait_ge(bd_zeroed, 1)
                        for at, w in ((0, "lru_wa_2"), (512, "lru_wx_2")):
                            src = a[w][0].rearrange("(c r) i j -> r i c j", r=2)
                            for r in range(2):
                                dst = PB[64 * r:64 * r + 64, at:at + 512].rearrange("p (c m) -> p c m", c=4)
                                sp.dma_start(dst[:, :, 64 * r:64 * r + 64], src[r]).then_inc(bd_landed, 16)
                    if name == "fk":
                        sp.dma_start(PT[:, 0:1024].rearrange("p (h s) -> p h s", h=8),
                                     a["sgu_w_2"][0].rearrange("h t s -> t h s")).then_inc(sgu_landed, 16)
                        for h in range(8):
                            r, c = h % 2, h // 2
                            sp.dma_start(AC[64 * r:64 * r + 64, c * P:(c + 1) * P],
                                         a["sgu_b_2"][0, h:h + 1, :].to_broadcast([64, P])).then_inc(bt_landed, 16)
                ffn(l)


_INS = ["x", "p", "norm_g", "w_in", "hgrn_lb", "hgrn_onorm_g", "nsa_qnorm_g", "nsa_knorm_g", "cmp_pe", "cmp_w1",
        "cmp_w2", "w_out", "ple_norm_g", "w_pg", "w_pp", "mix0_norm_2", "mix0_w_in_2", "lru_conv_w_2",
        "lru_conv_b_2", "lru_wa_2", "lru_ba_2", "lru_wx_2", "lru_bx_2", "lru_lambda_2", "sconv_w_2", "sconv_b_2",
        "mix0_w_out_2", "mix1_norm_2", "mix1_w_in_2", "sgu_norm_2", "sgu_w_2", "sgu_b_2", "fox_bf_2",
        "mix1_w_out_2", "ffn_norm_2", "ffn_up_2", "ffn_conv_w_2", "ffn_conv_b_2", "ffn_down_2", "final_norm_2"]


def kernel(**inputs):
    import concourse.bacc as bacc
    from concourse.bass_utils import run_bass_kernel_spmd

    nc = bacc.Bacc("TRN2", target_bir_lowering=False, num_devices=1)
    arrays, args = {}, {}
    table, masks = const_table()
    for name, value in [(n, inputs[n]) for n in _INS] + [("const_table", table), ("mask_table", masks)]:
        v = np.ascontiguousarray(value)
        arrays[f"in_{name}"] = v
        args[name] = nc.dram_tensor(f"in_{name}", v.shape, mybir.dt.from_np(v.dtype), kind="ExternalInput").ap()
    out = nc.dram_tensor("out", (1, T, D), F32, kind="ExternalOutput").ap()
    build(nc, args, out)
    r = run_bass_kernel_spmd(nc, [arrays], core_ids=[0])
    return r.results[0]["out"]
```

```python
from contextlib import ExitStack

import numpy as np

import concourse.bass as bass
from concourse import mybir

P = 128
T = 256
NT = T // P
D = 1024
ND = D // P
DEPTH = 2
HALF = 512
NH4 = HALF // P
IN1 = 4376
PLE = 256
FF = 2816
NFF = FF // P
FF_ROUNDS = NFF // 2
NCMP = 15
EPS = 1e-6
NEG = -1e30
SLOTS = 3
PANEL = 2048
MIXED_ORDER = [(0, 1, 2, 3)] * 2 + [(2, 3, 0, 1)] * 2
NLVL = 8

ALU = mybir.AluOpType
ACT = mybir.ActivationFunctionType
F32 = mybir.dt.float32
F32R = mybir.dt.float32r
BF16 = mybir.dt.bfloat16
I32 = mybir.dt.int32
AX_X = mybir.AxisListType.X
LOG_EXP = "natural_log_exp_and_others"

CONST_COLS = {}


def const_table():
    p = np.arange(P)
    parts = [("ident", np.eye(P)), ("ones", np.ones((P, P))),
             ("head_ones", (p[:, None] // 64 == p[None, :] // 64).astype(float))]
    rot = np.zeros((P, P))
    for h in (0, 64):
        for d in range(8):
            rot[h + 8 + d, h + d] = -1.0
            rot[h + d, h + 8 + d] = 1.0
    parts.append(("rot", rot))
    inv = (np.float32(500000.0) ** (-np.arange(0, 16, 2, dtype=np.float32) / np.float32(16))).astype(np.float32)
    ang = np.arange(T, dtype=np.float32)[None, :] * inv[:, None]
    cos, sin = np.ones((P, T)), np.zeros((P, T))
    for h in (0, 8, 64, 72):
        cos[h:h + 8] = np.cos(ang.astype(np.float32))
        sin[h:h + 8] = np.sin(ang.astype(np.float32))
    parts += [("cos", cos), ("sin", sin)]
    t = p[:, None, None] + P * np.arange(NT)[None, :, None]
    seen = (16 * np.arange(16)[None, None, :] + 31 <= t).astype(float)
    parts += [("cmp_neg", ((1 - seen) * NEG).reshape(P, NT * 16)), ("cmp_seen", seen.reshape(P, NT * 16))]
    parts.append(("head16", (p[:, None] // 16 == np.arange(8)[None, :]).astype(float)))
    parts.append(("upper", (p[:, None] <= p[None, :]).astype(float)))
    parts.append(("causal_neg", np.where(p[None, :] > p[:, None], NEG, 0.0)))
    at = 0
    for name, a in parts:
        CONST_COLS[name] = (at, a.shape[1])
        at += a.shape[1]
    levels = [(p[:, None] == p[None, :])]
    for n in range(1, NLVL):
        h = 1 << (n - 1)
        levels.append((p[:, None] // (2 * h) == p[None, :] // (2 * h)) & (p[:, None] % (2 * h) < h)
                      & (p[None, :] % (2 * h) >= h))
    masks = np.stack(levels, axis=1).astype(np.int32).reshape(P, NLVL * P)
    return np.concatenate([a for _, a in parts], axis=1).astype(np.float32), masks


const_table()
NCONST = max(a + n for a, n in CONST_COLS.values())

VEC_ROWS = [("norm_g", 16), ("ple_norm_g", 16), ("hgrn_lb", 8), ("hgrn_onorm_g", 2), ("nsa_qnorm_g", 2),
            ("nsa_knorm_g", 6), ("cmp_pe", 64), ("mix0_norm_2", 8), ("lru_conv_w_2", 16), ("lru_conv_b_2", 4),
            ("lru_ba_2", 4), ("lru_bx_2", 4), ("lru_lambda_2", 4), ("sconv_w_2", 12), ("sconv_b_2", 4),
            ("mix1_norm_2", 8), ("sgu_norm_2", 4), ("ffn_norm_2", 16), ("final_norm_2", 8),
            ("ffn_conv_w_2", 264), ("ffn_conv_b_2", 88)]
VEC_AT, _n = {}, 0
for _name, _rows in VEC_ROWS:
    VEC_AT[_name] = _n
    _n += _rows
NVEC = _n
NVT = (NVEC + P - 1) // P
DUPLICATED = ("nsa_qnorm_g", "nsa_knorm_g")

FIRST_PANELS = [(f"{name}{h}", "w_in", c0 + 256 * h, 256) for name, c0 in
                (("hf", 512), ("hq", 0), ("hi", 1024), ("nq", 2560), ("kv", 3072)) for h in range(2)]
FIRST_PANELS += [("kw0", "w_in", 3584, 256), ("kw1", "w_in", 3840, 24), ("cmp0", "cmp_w1", 0, P), ("cmp1", "cmp_w1", 1, P)]
FIRST_PANELS += [(f"{name}{h}", "w_in", c0 + 256 * h, 256) for name, c0 in
                 (("hgo", 1536), ("hz", 2048), ("nz", IN1 - HALF)) for h in range(2)]
FIRST_PANELS += [(f"wo{g}", "w_out", 256 * g, 256) for g in range(4)]
FIRST_PANELS += [("pp", "w_pp", 0, D)] + [(f"pg{g}", "w_pg", 256 * g, 256) for g in range(4)]
EVEN_PANELS = [(f"{name}{h}", "mix0_w_in_2", c0 + 256 * h, 256) for name, c0 in
               (("xa", 0), ("cp", 1024), ("vb", 2048), ("ga", 512), ("bp", 1536)) for h in range(2)]
EVEN_PANELS += [(f"wo{g}", "mix0_w_out_2", 256 * g, 256) for g in range(4)]
ODD_PANELS = [(f"{name}{h}", "mix1_w_in_2", c0 + 256 * h, 256) for name, c0 in
              (("fq", 1024), ("fk", 1536)) for h in range(2)]
ODD_PANELS += [("ff", "mix1_w_in_2", 2560, 8)]
ODD_PANELS += [(f"{name}{h}", "mix1_w_in_2", c0 + 256 * h, 256) for name, c0 in
               (("fv", 2048), ("zg", 512), ("zu", 0)) for h in range(2)]
ODD_PANELS += [(f"wo{g}", "mix1_w_out_2", 256 * g, 256) for g in range(4)]
AS_THEY_ARE = ("cmp0", "cmp1", "pp", "ff")


def panel_plan():
    loads, load_no, split_no = [], {}, {}

    def put(key, src, c0, n, split=True):
        load_no[key] = len(load_no)
        if split:
            split_no[key] = len(split_no)
        loads.append((key, src, c0, n))

    for block in range(2):
        for l in range(DEPTH):
            for name, src, c0, n in FIRST_PANELS if block == 0 else (EVEN_PANELS, ODD_PANELS)[l]:
                put((name, DEPTH * block + l), src, c0, n, name not in AS_THEY_ARE)
            if block == 1:
                order = [("gate", 0), ("value", 0)]
                for r in range(FF_ROUNDS):
                    order += [("gate", r + 1), ("value", r + 1)] if r + 1 < FF_ROUNDS else []
                    order += [("down", r)]
                for kind, r in order:
                    put((kind, l, r), kind, r, T)
    return loads, load_no, split_no


LOADS, LOAD_NO, SPLIT_NO = panel_plan()
FFN_SLOT = (2, 0, 1)
SPLIT_KEYS = list(SPLIT_NO)


def build(nc, a, out):
    fills = {}
    bank_fills = [0] * 8

    with ExitStack() as ctx:
        def sb(name, cols, dt=F32):
            return ctx.enter_context(nc.sbuf_tensor(name, [P, cols], dt))

        sems = {}

        def sem(name):
            if name not in sems:
                sems[name] = ctx.enter_context(nc.semaphore(name))
            return sems[name]

        ps = [ctx.enter_context(nc.psum_tensor(f"ps{b}", [P, 512], F32)) for b in range(8)]
        psum_full = [sem(f"psum_full{b}") for b in range(8)]
        psum_free = [sem(f"psum_free{b}") for b in range(8)]
        panel_landed = [sem(f"panel_landed{s}") for s in range(SLOTS)]
        high_ready, low_ready = sem("panel_high_ready"), sem("panel_low_ready")
        panel_free = {}
        order_of = {}
        high_from = {}
        split_from = {}

        def v3(t, n, off=0):
            w = t.shape[1] - off
            return t[:, off:off + w].rearrange("p (n w) -> p n w", n=n)

        H = sb("residual", ND * T)
        XH, XL = sb("input_high", ND * T, F32R), sb("input_low", ND * T, F32R)
        SQ = sb("squares", ND * T)
        RAW = sb("panels", SLOTS * PANEL)
        HI, LO = sb("panels_high", SLOTS * PANEL, F32R), sb("panels_low", SLOTS * PANEL, F32R)
        Y = UW = XF = SQ
        RINV = sb("rinv", T)
        CN = sb("consts", NCONST)
        LM = sb("level_masks", NLVL * P, I32)
        VC = sb("vectors", NVT * P)
        IDB = sb("ident_bf16", P, BF16)
        NGB = sb("causal_neg_bf16", P, BF16)
        EPSC = sb("eps", 2)
        LB = sb("lower_bound", 32)
        GQ = sb("q_gain_scaled", 2)
        SPC = sb("lru_rate", 40)
        W2 = sb("cmp_w2", 256)
        FK = sb("forget_key", 2048)
        FG, KQ = FK[:, 0:1024], FK[:, 1024:2048]
        QP = sb("query", 1024)
        AD = sb("decay_diag", 1024)
        VH = sb("values_hg", 1024)
        SG = FLV = sb("gate_o", 1024)
        HZ = sb("gate_z", 1024)
        NZ = sb("nsa_z", 1024)
        QN = sb("q_nope", 1024)
        QR = sb("q_rope", 1024)
        AC = sb("decay_cross", 512)
        VT = sb("values_nsa", 512)
        GT = sb("nsa_gates", 48)
        KN = sb("k_normed", 512)
        UK = sb("k_rope_terms", 1024)
        KZ = sb("k_padded", 2048)
        PB = sb("probs", 2 * 768)
        PT = sb("probs_t", 2 * 768)
        SC = sb("cmp_scores", 256)
        SS = sb("small", 256)
        PCT = sb("cmp_probs_t", 256)
        VCB = sb("cmp_values", 512)
        HID = sb("cmp_hidden", 64)
        HIDV = sb("cmp_hidden_rep", P)
        KC = sb("cmp_k", 64)
        KCZ = sb("cmp_k_padded", 64)
        NM = sb("neg_max", 8)
        SM = sb("prob_sums", 8)
        PP = FK
        ZR = sb("zeros", P)
        NT16 = sb("head_stats", 16)

        raw, high_slots, low_slots = ([t[:, s * PANEL:(s + 1) * PANEL] for s in range(SLOTS)] for t in (RAW, HI, LO))

        def const(name):
            at, n = CONST_COLS[name]
            return CN[:, at:at + n]

        def vec(name, n=0, m=1):
            at = VEC_AT[name] + n
            return VC[:, at:at + m]

        h3, xf3, sq3, xh3, xl3 = (v3(t, ND) for t in (H, XF, SQ, XH, XL))
        ident = const("ident")
        K2 = PB[:, 0:1024].rearrange("p (kv g t) -> p kv g t", kv=2, g=2)
        M2 = PT[:, 0:1024].rearrange("p (kv jj g c) -> p kv jj g c", kv=2, jj=16, g=2)
        kz = KZ[:, :].rearrange("p (k par g t) -> p k par g t", k=2, par=2, g=2)
        ad = AD[:, :].rearrange("p (h n t) -> p h n t", h=4, n=NT)
        ac = v3(AC, 4)
        vh = v3(VH, NT)
        vt = VT[:, :].rearrange("p (k n d) -> p k n d", k=2, n=NT)
        gates = GT[:, :].rearrange("p (n a) -> p n a", n=NT)
        probs = [[PB[:, b * 768:b * 768 + 256].rearrange("p (r s) -> p r s", r=2),
                  PB[:, b * 768 + 256:b * 768 + 768].rearrange("p (r s) -> p r s", r=2)] for b in range(2)]
        pt_lo = [PT[:, b * 768:b * 768 + 512].rearrange("p (r t) -> p r t", r=2) for b in range(2)]
        pt_hi = [PT[:, b * 768 + 512:b * 768 + 768].rearrange("p (r t) -> p r t", r=2) for b in range(2)]
        flevel = {0: FG}
        at = 0
        for n in range(1, NLVL):
            w = 1024 >> n
            flevel[n] = FLV[:, at:at + w]
            at += w
        xt = FK[:, :].rearrange("p (n d) -> p n d", n=NT)
        ptok = QR[:, :].rearrange("p (l d) -> p l d", l=2 * NT)
        PTR = ctx.enter_context(nc.sbuf_tensor("p_transposed", [P, 1024], F32))
        ptr = PTR[:, :].rearrange("p (l k t) -> p l k t", l=DEPTH, k=2)
        vrows = v3(QN, 8)

        def panel_size(n):
            name, l, *r = LOADS[n][0]
            return {"kw1": ND * 24, "ff": ND * 8}.get(name, PANEL)

        def full(eng, name):
            b, k = fills[name]
            eng.wait_ge(psum_full[b], k + 1)

        def free(name):
            return psum_free[fills[name][0]]

        def drained(eng, name):
            b, k = fills[name]
            eng.wait_ge(psum_free[b], k + 1)

        def bank(name):
            return ps[fills[name][0]]

        agenda = {l: [] for l in range(2 * DEPTH)}
        normed_last = {}

        vec_dmas = []
        for name, rows in VEC_ROWS:
            src = a[name]
            wide64 = name in DUPLICATED
            src = src.rearrange(" ".join("abcd"[:len(src.shape)]) + " -> (" + " ".join("abcd"[:len(src.shape)]) + ")")
            src = src.rearrange("(r w) -> r w", w=64 if wide64 else P)
            done_rows = 0
            while done_rows < rows:
                at = VEC_AT[name] + done_rows
                n = min(rows - done_rows, P - at % P)
                for c0 in ((0, 64) if wide64 else (0,)):
                    vec_dmas.append((at // P, at % P, n, c0, c0 + (64 if wide64 else P),
                                     src[done_rows:done_rows + n, :]))
                done_rows += n
        N_VEC_DMAS = len(vec_dmas)

        const_landed = sem("const_landed")
        x_landed, p_landed, vec_landed = sem("x_landed"), sem("p_landed"), sem("vec_landed")
        w2_landed, bd_landed, sgu_landed = sem("cmp_w2_landed"), sem("lru_weights_landed"), sem("sgu_landed")
        bias_landed, bt_landed = sem("forget_bias_landed"), sem("sgu_bias_landed")
        eps_ready, bd_zeroed = sem("eps_ready"), sem("lru_weights_zeroed")
        sq_ready = sem("squares_ready")
        rinv_ready = sem("rinv_ready")
        xf_ready, xh_ready = sem("normed_f32_ready"), sem("normed_high_ready")
        xn_ready = sem("normed_ready")
        yf_ready, yh_ready = sem("mixed_f32_ready"), sem("mixed_high_ready")
        gf_ready, gh_ready = sem("ffn_hidden_f32_ready"), sem("ffn_hidden_high_ready")
        h_ready = sem("residual_ready")
        small_ready = sem("setup_vectors_ready")
        hg_ready = sem("hg_keys_ready")
        level_ready = sem("hg_level_ready")
        qsq_ready, ksq_ready = sem("q_squares_ready"), sem("k_squares_ready")
        kcsq_ready, osq_ready = sem("cmp_k_squares_ready"), sem("hg_o_squares_ready")
        q_rinv_ready, k_rinv_ready = sem("q_rinv_ready"), sem("k_rinv_ready")
        kc_rinv_ready, o_rinv_ready = sem("cmp_k_rinv_ready"), sem("hg_o_rinv_ready")
        rope_ready, k_rope_ready = sem("q_rope_terms_ready"), sem("k_rope_terms_ready")
        blocks_ready = sem("cmp_blocks_ready")
        gate_exp_ready, gates_ready = sem("gate_exp_ready"), sem("gates_ready")
        hid_exp_ready, hidden_ready = sem("cmp_hidden_exp_ready"), sem("cmp_hidden_ready")
        kc_ready = sem("cmp_k_ready")
        cmp_shift_ready, cmp_exp_ready, cp_ready = (sem("cmp_shifted_ready"), sem("cmp_exp_ready"),
                                                    sem("cmp_probs_ready"))
        nmax_ready = sem("neg_max_ready")
        exps_ready = sem("exps_ready")
        p_ready = sem("probs_ready")
        sig_ready = sem("gate_sigmoids_ready")
        conv_ready = sem("conv_first_tap_ready")
        act_part = sem("scalar_part_ready")
        dve_part = sem("vector_part_ready")
        forget_ready, sgu_ready, y_ready = sem("forget_ready"), sem("sgu_ready"), sem("mixed_ready")
        taps_ready, first_back_done = sem("ffn_first_taps_ready"), sem("ffn_second_taps_done")
        silu_ready, act_ready = sem("ffn_silu_ready"), sem("ffn_hidden_ready")
        down_done, half_done = sem("ffn_down_done"), sem("half_by_token_done")
        out_copied, out_stored = sem("out_copied"), sem("out_stored")
        dve_step, act_step = sem("vector_step"), sem("scalar_step")
        BF = sb("forget_bias", 1)
        glu = [v3(t, 4) for t in (SG, HZ)]
        ones, head_ones = const("ones"), const("head_ones")
        ffn_base = {}
        GH, GL = sb("ffn_hidden_high", 1024, F32R), sb("ffn_hidden_low", 1024, F32R)
        hidden = [v3(VH[:, par * 512:(par + 1) * 512], 2) for par in range(2)]
        gh3, gl3 = ([v3(t[:, par * 512:(par + 1) * 512], 2) for par in range(2)] for t in (GH, GL))

        block = ctx.enter_context(nc.Block())

        @block.tensor
        def _(pe):
            last_done = [None]

            def begin(name, b):
                k = bank_fills[b]
                bank_fills[b] += 1
                fills[name] = (b, k)
                if k > 0:
                    pe.wait_ge(psum_free[b], k)
                return ps[b]

            def done(name, ins):
                order_of[name] = len(order_of)
                ins.then_inc(psum_full[fills[name][0]], 1)
                last_done[0] = name

            next_split = [SLOTS]

            def release(key):
                b, k = fills[last_done[0]]
                freed(key, (psum_full[b], k + 1), order_of[last_done[0]])

            def freed(key, when, place):
                panel_free[key] = when
                while next_split[0] < len(SPLIT_KEYS):
                    q = next_split[0]
                    n = LOAD_NO[SPLIT_KEYS[q]]
                    before, loaded_before = SPLIT_KEYS[q - SLOTS], LOADS[n - SLOTS][0]
                    if before not in panel_free:
                        break
                    if loaded_before not in SPLIT_NO and loaded_before not in panel_free:
                        break
                    split_from[q] = place
                    next_split[0] += 1

            def landed(key):
                n = LOAD_NO[key]
                pe.wait_ge(panel_landed[n % SLOTS], 16 * (n // SLOTS + 1))

            def split(key):
                pe.wait_ge(low_ready, SPLIT_NO[key] + 1)

            def raw_panel(key, nk=ND, n=512):
                return raw[LOAD_NO[key] % SLOTS][:, 0:nk * n].rearrange("p (k n) -> p k n", k=nk)

            def parts(key, nk=ND, n=256):
                s = SPLIT_NO[key] % SLOTS
                return [t[s][:, 0:nk * n].rearrange("p (k n) -> p k n", k=nk) for t in (high_slots, low_slots)]

            def product3(dst, w, x, start, stop, **kw):
                pe.matmul(dst, w[1], x[0], start=start, stop=False if not kw else True, **kw)
                pe.matmul(dst, w[0], x[1], start=False, stop=False if not kw else True, **kw)
                return pe.matmul(dst, w[0], x[0], start=False, stop=stop, **kw)

            def chunk(dst, w, col, norm=None, mixed=None):
                for i in range(ND):
                    k = i
                    if norm is not None:
                        pe.wait_ge(xn_ready, 8 * norm + k + 1)
                    if mixed is not None:
                        k = 2 * MIXED_ORDER[mixed][i // 2] + i % 2
                        if i % 2 == 0:
                            pe.wait_ge(y_ready, 4 * mixed + i // 2 + 1)
                    ins = product3(dst, [t[:, k, col:col + P] for t in w], (xh3[:, k, :], xl3[:, k, :]),
                                   i == 0, i == ND - 1)
                return ins

            def small_chunk(dst, w3, col, x3, nk=ND, m=P):
                for k in range(nk):
                    ins = pe.matmul(dst, w3[:, k, col:col + m], x3[:, k, :], start=(k == 0), stop=(k == nk - 1))
                return ins

            def by_token(dst, w, col, n, tile):
                t = slice(tile * P, (tile + 1) * P)
                for k in range(ND):
                    ins = product3(dst, (xh3[:, k, t], xl3[:, k, t]), [part[:, k, col:col + n] for part in w],
                                   k == 0, k == ND - 1)
                return ins

            def two_chunks(name, b, key, norm=None, mixed=None):
                begin(name, b)
                split(key)
                for j in range(2):
                    ins = chunk(ps[b][:, j * T:(j + 1) * T], parts(key), j * P,
                                norm=norm if j == 0 else None, mixed=mixed if j == 0 else None)
                done(name, ins)
                release(key)

            def tokens(names, b, keys):
                for n in range(NT):
                    begin(names[n], b + n)
                for h, key in enumerate(keys):
                    split(key)
                    for n in range(NT):
                        ins = by_token(ps[b + n][:, h * T:(h + 1) * T], parts(key), 0, T, n)
                        if h == 1:
                            done(names[n], ins)
                    if h == 0:
                        ins.then_inc(half_done, 1)
                        halves[0] += 1
                        freed(key, (half_done, halves[0]), len(order_of) - 1)
                release(keys[1])

            halves = [0]

            def norm_sum(nidx, b=0):
                begin(f"ms{nidx}", b)
                for c in range(ND):
                    if c % 2 == 0:
                        pe.wait_ge(sq_ready, 4 * nidx + c // 2 + 1)
                    ins = pe.matmul(ps[b][:, 0:T], ones, sq3[:, c, :], start=(c == 0), stop=(c == ND - 1))
                done(f"ms{nidx}", ins)

            def product(name, b, n, lhs, rhs):
                begin(name, b)
                done(name, pe.matmul(ps[b][:, 0:n], lhs, rhs, start=True, stop=True))

            pe.wait_ge(const_landed, 32)
            pe.wait_ge(x_landed, 16)
            for g in range(4):
                begin(f"x{g}", g)
                for j in range(4):
                    c, n = 2 * g + j // 2, j % 2
                    ins = pe.transpose(ps[g][:, j * P:(j + 1) * P], xt[:, n, c * P:(c + 1) * P], ident)
                done(f"x{g}", ins)
            pe.wait_ge(vec_landed, 16 * N_VEC_DMAS)
            for g in range((NVT + 3) // 4):
                begin(f"vec{g}", 4 + g)
                for j in range(min(4, NVT - 4 * g)):
                    r = min(P, NVEC - (4 * g + j) * P)
                    ins = pe.transpose(ps[4 + g][:, j * P:j * P + r], vrows[0:r, 4 * g + j, :], ident[0:r, 0:r])
                done(f"vec{g}", ins)
            pe.wait_ge(p_landed, 16)
            for l in range(DEPTH):
                begin(f"p{l}", 6 + l)
                for k in range(2):
                    for n in range(NT):
                        ins = pe.transpose(ps[6 + l][:, k * T + n * P:k * T + (n + 1) * P],
                                           ptok[:, l * NT + n, k * P:(k + 1) * P], ident)
                done(f"p{l}", ins)

            def scores(tag, u, q, keys, forget=None):
                begin(f"{tag}Y{u}", 5)
                begin(f"{tag}X{u}", 3 + u % 2)
                for n, b, x in ((0, 5, "Y"), (1, 3 + u % 2, "X")):
                    w = (n + 1) * P
                    o = ps[b][:, 0:2 * w].rearrange("p (r s) -> p r s", r=2)
                    pe.matmul(o, q[:, n * P:(n + 1) * P], keys[:, :, 0:w], start=True, stop=True)
                    if forget is not None:
                        pe.matmul(o, ones[0:8, :], forget[:, :, 0:w], start=False, stop=True,
                                  skip_group_check=True)
                    ins = pe.matmul(o[:, :, n * P:w], IDB[:, :], NGB[:, :].unsqueeze(1).to_broadcast([P, 2, P]),
                                    start=False, stop=True, skip_group_check=True)
                    done(f"{tag}{x}{u}", ins)

            def turn(tag, u, pidx):
                bb = pidx % 2
                pe.wait_ge(p_ready, pidx + 1)
                begin(f"{tag}A{u}", 6)
                for r in range(2):
                    pe.transpose(ps[6][:, r * T:r * T + P], probs[bb][0][:, r, :], ident)
                    ins = pe.transpose(ps[6][:, r * T + P:(r + 1) * T], probs[bb][1][:, r, 0:P], ident)
                done(f"{tag}A{u}", ins)
                begin(f"{tag}B{u}", 7)
                for r in range(2):
                    ins = pe.transpose(ps[7][:, r * P:(r + 1) * P], probs[bb][1][:, r, P:T], ident)
                done(f"{tag}B{u}", ins)

            def values(tag, u, pidx, vals, o, start, close=None):
                bb = pidx % 2
                drained(pe, f"{tag}A{u}")
                drained(pe, f"{tag}B{u}")
                for r in range(2):
                    pe.matmul(o[64 * r:64 * r + 64, :], vals(0, r), pt_lo[bb][:, r, :],
                              start=start, stop=True, skip_group_check=True)
                    ins = pe.matmul(o[64 * r:64 * r + 64, P:T], vals(1, r), pt_hi[bb][:, r, :],
                                    start=False, stop=True, skip_group_check=True)
                if close:
                    done(close, ins)

            def output(tag, l):
                for g in range(4):
                    two_chunks(f"{tag}{g}", 3 + g, (f"wo{g}", l), mixed=l if g == 0 else None)

            def noting(l):
                return lambda step: agenda[l].append((len(order_of) - 1, *step))

            nidx, pidx = 0, 0
            for l in range(DEPTH):
                todo = noting(l)
                norm_sum(nidx)
                for name, b in (("hf", 1), ("hq", 3)):
                    for g in range(2):
                        two_chunks(f"{name}{g}_{l}", b + g, (f"{name}{g}", l),
                                   norm=nidx if (name, g) == ("hf", 0) else None)
                tokens([f"hi{n}_{l}" for n in range(NT)], 5, [(f"hi{h}", l) for h in range(2)])

                def level(n, g):
                    if n == 0:
                        pe.wait_ge(hg_ready, l + 1)
                        drained(pe, f"hq{g}_{l}")
                    else:
                        pe.wait_ge(level_ready, 16 * l + 2 * (n - 1) + g + 1)
                    b = (7, 0)[g]
                    begin(f"lv{n}_{g}_{l}", b)
                    for j in range(4):
                        s = (2 * g + j // 2) * T + (j % 2) * P
                        ins = pe.matmul(ps[b][:, j * P:(j + 1) * P], KQ[:, s:s + P], QP[:, s:s + P],
                                        start=True, stop=True)
                    done(f"lv{n}_{g}_{l}", ins)
                    todo(("level", n, g))

                levels = [(n, g) for n in range(NLVL) for g in range(2)]

                def some(k):
                    for _ in range(min(k, len(levels))):
                        level(*levels.pop(0))

                some(2)
                for g in range(2):
                    key = (f"nq{g}", l)
                    begin(f"nq{g}_{l}", 1 + g)
                    split(key)
                    for j in range(2):
                        ins = chunk(ps[1 + g][:, j * T:(j + 1) * T], parts(key), j * P)
                        if j == 0:
                            some(1)
                    done(f"nq{g}_{l}", ins)
                    release(key)
                    todo(("copy", f"nq{g}"))
                    some(1)
                begin(f"kcvc_{l}", 3)
                split(("kv0", l))
                for j in range(2):
                    ins = chunk(ps[3][:, j * T:(j + 1) * T], parts(("kv0", l)), j * P)
                    if j == 0:
                        some(1)
                done(f"kcvc_{l}", ins)
                release(("kv0", l))
                todo(("blocks",))
                some(1)
                begin(f"ks_{l}", 4)
                split(("kv1", l))
                chunk(ps[4][:, 0:T], parts(("kv1", l)), 0)
                some(1)
                begin(f"vs_{l}", 5)
                for n in range(NT):
                    ins = by_token(ps[5][:, n * P:(n + 1) * P], parts(("kv1", l)), P, P, n)
                done(f"vs_{l}", ins)
                release(("kv1", l))
                todo(("copy", "vs"))
                some(1)
                split(("kw0", l))
                done(f"ks_{l}", chunk(ps[4][:, T:2 * T], parts(("kw0", l)), 0))
                todo(("k_square",))
                some(1)
                begin(f"vw_{l}", 6)
                for n in range(NT):
                    ins = by_token(ps[6][:, n * 152:n * 152 + P], parts(("kw0", l)), P, P, n)
                split(("kw1", l))
                for n in range(NT):
                    ins = by_token(ps[6][:, n * 152 + P:(n + 1) * 152], parts(("kw1", l), n=24), 0, 24, n)
                done(f"vw_{l}", ins)
                release(("kw0", l))
                release(("kw1", l))
                todo(("gates",))
                pe.wait_ge(qsq_ready, l + 1)
                for j in range(2):
                    product(f"qss{j}_{l}", 1 + j, 512, head_ones, SQ[:, j * 512:(j + 1) * 512])
                todo(("q_norm",))
                some(1)
                pe.wait_ge(ksq_ready, l + 1)
                product(f"kss_{l}", 4, 512, head_ones, UK[:, 0:512])
                todo(("k_norm",))
                some(1)
                pe.wait_ge(blocks_ready, l + 1)
                begin(f"hid_{l}", 3)
                for kv in range(2):
                    landed((f"cmp{kv}", l))
                    w1 = raw_panel((f"cmp{kv}", l), 16, P)
                    for jj in range(16):
                        ins = pe.matmul(ps[3][:, kv * 32:(kv + 1) * 32], w1[:, jj, :], M2[:, kv, jj, :, :],
                                        start=(jj == 0), stop=(jj == 15))
                done(f"hid_{l}", ins)
                release(("cmp0", l))
                release(("cmp1", l))
                todo(("hidden",))
                some(1)
                pe.wait_ge(rope_ready, l + 1)
                for j in range(2):
                    begin(f"qr{j}_{l}", 1 + j)
                    pe.matmul(ps[1 + j][:, :], ident, UW[:, j * 512:(j + 1) * 512], start=True, stop=False)
                    done(f"qr{j}_{l}", pe.matmul(ps[1 + j][:, :], const("rot"),
                                                 UW[:, 1024 + j * 512:1024 + (j + 1) * 512],
                                                 start=False, stop=True))
                    todo(("copy", f"qr{j}"))
                some(1)
                pe.wait_ge(k_rope_ready, l + 1)
                begin(f"kr_{l}", 4)
                pe.matmul(ps[4][:, :], ident, UK[:, 0:512], start=True, stop=False)
                done(f"kr_{l}", pe.matmul(ps[4][:, :], const("rot"), UK[:, 512:1024], start=False, stop=True))
                todo(("k_pad",))
                some(16)
                pe.wait_ge(level_ready, 16 * l + 16)
                begin(f"cross_{l}", 7)
                for hd in range(4):
                    ins = pe.matmul(ps[7][:, hd * P:(hd + 1) * P], KQ[:, hd * T:hd * T + P],
                                    QP[:, hd * T + P:(hd + 1) * T], start=True, stop=True)
                done(f"cross_{l}", ins)
                todo(("cross",))
                pe.wait_ge(w2_landed, 48 * (l + 1))
                pe.wait_ge(hidden_ready, l + 1)
                product(f"kc_{l}", 0, 32, W2[:, 0:P], HID[:, 0:32])
                product(f"vc_{l}", 3, 64, HIDV[:, :], W2[:, P:P + 64])
                todo(("cmp_kv",))
                drained(pe, f"hi1_{l}")
                drained(pe, f"cross_{l}")
                drained(pe, f"lv{NLVL - 1}_0_{l}")
                drained(pe, f"lv{NLVL - 1}_1_{l}")
                for g in range(2):
                    begin(f"o{g}_{l}", 5 + g)
                    for j in range(2):
                        hd = 2 * g + j
                        v = [vh[:, n, hd * P:(hd + 1) * P] for n in range(NT)]
                        pe.matmul(ps[5 + g][:, j * T:j * T + P], v[0], ad[:, hd, 0, :], start=True, stop=True)
                        pe.matmul(ps[5 + g][:, j * T + P:(j + 1) * T], v[0], ac[:, hd, :], start=True, stop=False)
                        ins = pe.matmul(ps[5 + g][:, j * T + P:(j + 1) * T], v[1], ad[:, hd, 1, :],
                                        start=False, stop=True)
                    done(f"o{g}_{l}", ins)
                todo(("o_square",))
                pe.wait_ge(kcsq_ready, l + 1)
                product(f"kcss_{l}", 0, 32, head_ones, KC[:, 32:64])
                todo(("kc_norm",))
                gate_chunks = [(name, g, j) for name in ("hgo", "hz", "nz") for g in range(2) for j in range(2)]

                def gate_chunk():
                    if not gate_chunks:
                        return
                    name, g, j = gate_chunks.pop(0)
                    key = (f"{name}{g}", l)
                    if j == 0:
                        begin(f"{name}{g}_{l}", 0)
                        split(key)
                    ins = chunk(ps[0][:, j * T:(j + 1) * T], parts(key), j * P)
                    if j == 1:
                        done(f"{name}{g}_{l}", ins)
                        release(key)
                        todo(("copy", f"{name}{g}"))

                gate_chunk()
                pe.wait_ge(osq_ready, l + 1)
                for g in range(2):
                    product(f"oss{g}_{l}", 5 + g, 512, ones, SQ[:, g * 512:(g + 1) * 512])
                todo(("o_norm",))
                pe.wait_ge(kc_ready, l + 1)
                begin(f"cs_{l}", 3)
                for n in range(NT):
                    for j in range(4):
                        s = n * P + j * 32
                        ins = pe.matmul(ps[3][:, s:s + 32].rearrange("p (r c) -> p r c", r=2),
                                        QN[:, j * T + n * P:j * T + (n + 1) * P],
                                        v3(KCZ, 2)[:, :, (j // 2) * 16:(j // 2) * 16 + 16], start=True, stop=True)
                done(f"cs_{l}", ins)
                todo(("cmp_softmax",))
                gate_chunk()
                drained(pe, f"qr1_{l}")
                drained(pe, f"kr_{l}")
                drained(pe, f"vs_{l}")
                pe.wait_ge(gates_ready, l + 1)

                def unit(u):
                    kind, j = u // 4, u % 4
                    scores(f"n{l}", u, QR[:, j * T:(j + 1) * T], kz[:, kind, :, j // 2, :])
                    todo(("scores", u))

                unit(0)
                pe.wait_ge(cp_ready, l + 1)
                begin(f"ct_{l}", 7)
                for n in range(NT):
                    ins = pe.transpose(ps[7][:, n * P:(n + 1) * P], SC[:, n * P:(n + 1) * P], ident)
                done(f"ct_{l}", ins)
                todo(("copy", "ct"))
                gate_chunk()
                drained(pe, f"ct_{l}")
                drained(pe, f"vc_{l}")
                begin(f"on0_{l}", 1)
                begin(f"on1_{l}", 2)
                for j in range(4):
                    pe.matmul(ps[1 + j // 2][:, (j % 2) * T:(j % 2 + 1) * T], VCB[:, j * P:(j + 1) * P], PCT[:, :],
                              start=(j % 2 == 0), stop=True, skip_group_check=True)
                for u in range(8):
                    if u < 7:
                        unit(u + 1)
                    turn(f"n{l}", u, pidx)
                    todo(("values", u))
                    gate_chunk()
                    kind, j = u // 4, u % 4
                    values(f"n{l}", u, pidx, lambda n, r: vt[:, kind, n, (j // 2) * 64:(j // 2) * 64 + 64],
                           ps[1 + j // 2][:, (j % 2) * T:(j % 2 + 1) * T], False,
                           close={5: f"on0_{l}", 7: f"on1_{l}"}.get(u))
                    pidx += 1
                while gate_chunks:
                    gate_chunk()
                normed_last[nidx] = f"nz1_{l}"
                nidx += 1
                todo(("mix",))
                output(f"wo_{l}_", l)
                landed(("pp", l))
                for g in range(4):
                    b = (7, 0, 1, 2)[g]
                    if g == 2:
                        norm_sum(nidx, b=3)
                    begin(f"pp{g}_{l}", b)
                    for j in range(2):
                        ins = small_chunk(ps[b][:, j * T:(j + 1) * T], raw_panel(("pp", l), 2, 1024),
                                          (2 * g + j) * P, ptr[:, l], nk=2)
                    done(f"pp{g}_{l}", ins)
                release(("pp", l))
                for g in range(4):
                    two_chunks(f"pg{g}_{l}", 4 + g, (f"pg{g}", l), norm=nidx if g == 0 else None)
                normed_last[nidx] = f"pg3_{l}"
                nidx += 1

            for l in range(DEPTH):
                L = DEPTH + l
                todo = noting(L)
                norm_sum(nidx)
                if l == 0:
                    for name, b in (("xa", 1), ("cp", 3), ("vb", 5)):
                        for g in range(2):
                            two_chunks(f"{name}{g}", b + g, (f"{name}{g}", L),
                                       norm=nidx if (name, g) == ("xa", 0) else None)
                    pe.wait_ge(bd_landed, 64)
                    for name, w, b in (("lr", 0, (7, 0)), ("li", 512, (1, 2))):
                        for g in range(2):
                            drained(pe, f"xa{g}")
                            begin(f"{name}{g}", b[g])
                            for j in range(2):
                                c = 2 * g + j
                                ins = pe.matmul(ps[b[g]][:, j * T:(j + 1) * T], PB[:, w + c * P:w + (c + 1) * P],
                                                FG[:, c * T:(c + 1) * T], start=True, stop=True)
                            done(f"{name}{g}", ins)
                    for name, b in (("ga", 3), ("bp", 5)):
                        for g in range(2):
                            two_chunks(f"{name}{g}", b + g, (f"{name}{g}", L))
                    normed_last[nidx] = "bp1"
                else:
                    for name, b in (("fq", 1), ("fk", 3)):
                        for g in range(2):
                            two_chunks(f"{name}{g}", b + g, (f"{name}{g}", L),
                                       norm=nidx if (name, g) == ("fq", 0) else None)
                    landed(("ff", L))
                    begin("fl", 7)
                    done("fl", small_chunk(ps[7][0:8, 0:T], raw_panel(("ff", L), ND, 8), 0, xf3, m=8))
                    release(("ff", L))
                    tokens(["fv0", "fv1"], 5, [("fv0", L), ("fv1", L)])
                    tokens(["zg0", "zg1"], 1, [("zg0", L), ("zg1", L)])
                    pe.wait_ge(sgu_landed, 16)
                    for g in range(2):
                        begin(f"wt{g}", (7, 0)[g])
                        for j in range(4):
                            hd = 4 * g + j
                            ins = pe.transpose(ps[(7, 0)[g]][:, j * P:(j + 1) * P], PT[:, hd * P:(hd + 1) * P],
                                               ident)
                        done(f"wt{g}", ins)
                    two_chunks("zu0", 3, ("zu0", L))
                    pe.wait_ge(forget_ready, 1)
                    drained(pe, "fq1")
                    drained(pe, "fk1")
                    drained(pe, "fv1")
                    drained(pe, "wt1")

                    def unit(u):
                        scores("f", u, QR[:, u * T:(u + 1) * T], kz[:, u // 2, :, u % 2, :],
                               UW[0:8, :].rearrange("p (h t) -> p h t", h=8)[:, 2 * u:2 * u + 2, :])
                        todo(("scores", u))

                    def mix_tokens(g):
                        begin(f"sg{g}", 0)
                        for j in range(2):
                            for n in range(NT):
                                for r in range(2):
                                    hd = 4 * g + 2 * j + r
                                    s = j * T + n * P
                                    ins = pe.matmul(ps[0][64 * r:64 * r + 64, s:s + P],
                                                    QN[:, n * 512 + hd * 64:n * 512 + (hd + 1) * 64],
                                                    AD[:, hd * P:(hd + 1) * P], start=True, stop=True)
                        done(f"sg{g}", ins)
                        todo((f"sg{g}",))

                    unit(0)
                    for u in range(4):
                        if u < 3:
                            unit(u + 1)
                        if u == 0:
                            two_chunks("zu1", 0, ("zu1", L))
                            todo(("zu1",))
                        turn("f", u, pidx)
                        todo(("values", u))
                        if u == 1:
                            pe.wait_ge(sgu_ready, 1)
                            mix_tokens(0)
                        if u % 2 == 0:
                            begin(f"fo{u // 2}", 1 + u // 2)
                        values("f", u, pidx, lambda n, r: vh[:, n, (2 * u + r) * 64:(2 * u + r + 1) * 64],
                               ps[1 + u // 2][:, (u % 2) * T:(u % 2 + 1) * T], True,
                               close=f"fo{u // 2}" if u % 2 == 1 else None)
                        pidx += 1
                    mix_tokens(1)
                    normed_last[nidx] = "zu1"
                nidx += 1
                output(f"wm_{l}_", L)

                norm_sum(nidx, b=0)
                for g in range(4):
                    begin(f"down{g}_{l}", 4 + g)
                    pe.matmul(ps[4 + g][:, :], ZR[:, :], CN[:, 0:512], start=True, stop=True,
                              skip_group_check=True)
                ffn_base[l] = up0 = [bank_fills[b] for b in range(4)]
                q0 = SPLIT_NO[("gate", l, 0)]

                def up(par, i, norm=None):
                    for half in range(2):
                        b = 2 * par + half
                        pe.wait_ge(psum_free[b], i + up0[b])
                        if norm is None:
                            slot = (q0 + FFN_SLOT[half]) % SLOTS
                            pe.wait_ge(low_ready, i * 6 + (q0 + 3 * par + half))
                        else:
                            slot = (q0 + half) % SLOTS
                            pe.wait_ge(low_ready, q0 + half + 1)
                        w = [v3(t[slot], ND) for t in (high_slots, low_slots)]
                        for j in range(2):
                            ins = chunk(ps[b][:, j * T:(j + 1) * T], w, j * P,
                                        norm=norm if (half, j) == (0, 0) else None)
                        ins.then_inc(psum_full[b], 1)

                def down(par, i, close=False):
                    slot = (q0 + FFN_SLOT[2]) % SLOTS
                    if close:
                        slot = (q0 + 2 + 3 * (FF_ROUNDS - 1)) % SLOTS
                        pe.wait_ge(low_ready, q0 + 3 * FF_ROUNDS)
                    else:
                        pe.wait_ge(low_ready, i * 6 + (q0 + 3 * par + 5))
                    pe.wait_ge(act_ready, 2 * i + (par + 1 + FF_ROUNDS * l))
                    w = [v3(t[slot], 2) for t in (high_slots, low_slots)]
                    for g in range(4):
                        for j in range(2):
                            c = slice((2 * g + j) * P, (2 * g + j + 1) * P)
                            for k in range(2):
                                ins = product3(ps[4 + g][:, j * T:(j + 1) * T], [w[i][:, k, c] for i in range(2)],
                                               (gh3[par][:, k, :], gl3[par][:, k, :]), False, True,
                                               skip_group_check=True)
                        if close:
                            done(f"down{g}_{l}", ins)
                    if not close:
                        ins.then_inc(down_done, 1)

                up(0, 0, norm=nidx)
                up(1, 0)
                down(0, 0)
                with pe.Fori(1, FF_ROUNDS // 2) as i:
                    up(0, i)
                    down(1, i - 1)
                    up(1, i)
                    down(0, i)
                up(0, FF_ROUNDS // 2)
                for b in range(4):
                    bank_fills[b] += FF_ROUNDS // 2 + (b < 2)
                last_up = f"ffn_up{l}"
                fills[last_up] = (1, bank_fills[1] - 1)
                order_of[last_up] = len(order_of)
                for r in range(FF_ROUNDS):
                    for b, kind in ((0, "gate"), (1, "value")):
                        freed((kind, l, r), (psum_full[b], bank_fills[b]), order_of[last_up])
                down(1, FF_ROUNDS // 2 - 1)
                for r in range(FF_ROUNDS - 1):
                    freed(("down", l, r), (down_done, (FF_ROUNDS - 1) * (l + 1)), order_of[last_up])
                down(0, FF_ROUNDS // 2, close=True)
                release(("down", l, FF_ROUNDS - 1))
                normed_last[nidx] = last_up
                nidx += 1

            norm_sum(nidx)
            pe.wait_ge(xf_ready, 8 * nidx + 8)
            for g in range(4):
                n, c0 = g // 2, 4 * (g % 2)
                begin(f"out{g}", (1, 2, 3, 4)[g])
                for j in range(4):
                    ins = pe.transpose(ps[(1, 2, 3, 4)[g]][:, j * P:(j + 1) * P],
                                       xf3[:, c0 + j, n * P:(n + 1) * P], ident)
                done(f"out{g}", ins)

        @block.scalar
        def _(act):
            steps = [0]

            def link(ins):
                steps[0] += 1
                ins.then_inc(act_step, 1)
                act.wait_ge(act_step, steps[0])

            def f(dst, src, func, **kw):
                return nc.scalar.activation(dst, src, func, **kw)

            def copy_out(name, dst, src):
                full(act, name)
                nc.scalar.copy(dst, src).then_inc(free(name), 1)

            def high_part(n, slot, size=PANEL, when=None, landed=None):
                if landed is None:
                    landed = 16 * (n // SLOTS + 1)
                act.wait_ge(panel_landed[n % SLOTS], landed)
                if when is not None:
                    act.wait_ge(*when)
                nc.scalar.copy(high_slots[slot][:, 0:size], raw[n % SLOTS][:, 0:size]).then_inc(high_ready, 1)

            next_high = [0]

            def split_high(place, first_of_ffn=None):
                while next_high[0] < len(SPLIT_KEYS):
                    q = next_high[0]
                    key = SPLIT_KEYS[q]
                    if q >= SLOTS and split_from.get(q, 1 << 30) > place or len(key) == 3 and \
                            key not in (("gate", key[1], 0), ("value", key[1], 0)):
                        break
                    n = LOAD_NO[key]
                    high_part(n, q % SLOTS, panel_size(n), panel_free[SPLIT_KEYS[q - SLOTS]] if q >= SLOTS else None)
                    high_from[q] = place
                    next_high[0] += 1

            def split_after(name):
                split_high(order_of[name])

            def input_high(nidx):
                for c in range(ND):
                    act.wait_ge(xf_ready, 8 * nidx + c + 1)
                    nc.scalar.copy(xh3[:, c, :], xf3[:, c, :]).then_inc(xh_ready, 1)

            def mixed_high(m, names):
                for g in MIXED_ORDER[m]:
                    if g < 2:
                        act.wait_ge(yf_ready, 2 * m + g + 1)
                    else:
                        drained(act, names[g - 2])
                    nc.scalar.copy(XH[:, g * 512:(g + 1) * 512], Y[:, g * 512:(g + 1) * 512]).then_inc(yh_ready, 1)

            def log_exp():
                nc.scalar.preload_act_table_set(LOG_EXP)

            def squares(nidx, ready, between=None):
                for g in range(4):
                    ready(g)
                    f(sq3[:, 2 * g:2 * g + 2, :], h3[:, 2 * g:2 * g + 2, :], ACT.Square).then_inc(sq_ready, 1)
                    if between and g < 3:
                        between(g)

            def norm(nidx):
                log_exp()
                full(act, f"ms{nidx}")
                f(RINV[:, :], bank(f"ms{nidx}")[:, 0:T], ACT.Ln, bias=EPSC[:, 0:1],
                  scale=1.0 / D).then_inc(free(f"ms{nidx}"), 1)
                drained(act, f"ms{nidx}")
                f(RINV[:, :], RINV[:, :], ACT.Exp, scale=-0.5).then_inc(rinv_ready, 1)
                if nidx < 4 * DEPTH:
                    input_high(nidx)

            def head_rinv(names, dst, width, n):
                for j, name in enumerate(names):
                    full(act, name)
                    w = n // len(names)
                    f(dst[:, j * w:(j + 1) * w], bank(name)[:, 0:w], ACT.Ln, bias=EPSC[:, 0:1],
                      scale=1.0 / width).then_inc(free(name), 1)
                drained(act, names[-1])
                return f(dst, dst, ACT.Exp, scale=-0.5)

            def exps(tag, u, pidx):
                bb = pidx % 2
                act.wait_ge(nmax_ready, pidx + 1)
                if pidx >= 2:
                    act.wait_ge(*turned[pidx - 2])
                for n, x in ((0, "Y"), (1, "X")):
                    s3 = bank(f"{tag}{x}{u}")[:, 0:2 * (n + 1) * P].rearrange("p (r s) -> p r s", r=2)
                    for r in range(2):
                        i = 2 * n + r
                        ins = f(probs[bb][n][:, r, :], s3[:, r, :], ACT.Exp, bias=NM[:, 4 * bb + i:4 * bb + i + 1],
                                accum_out=SM[:, 4 * bb + i:4 * bb + i + 1])
                    ins.then_inc(free(f"{tag}{x}{u}"), 1)

            def turned_copies(tag, u, pidx):
                bb = pidx % 2
                copy_out(f"{tag}A{u}", pt_lo[bb].rearrange("p r t -> p (r t)"), bank(f"{tag}A{u}")[:, :])
                copy_out(f"{tag}B{u}", pt_hi[bb].rearrange("p r t -> p (r t)"), bank(f"{tag}B{u}")[:, 0:T])
                b, k = fills[f"{tag}B{u}"]
                turned[pidx] = (psum_full[b], k + 1)

            turned = {}
            act.wait_ge(eps_ready, 1)
            split_high(-1)
            for g in range((NVT + 3) // 4):
                n = min(512, NVEC - 512 * g)
                copy_out(f"vec{g}", VC[:, 512 * g:512 * g + n], bank(f"vec{g}")[:, 0:n])
            for l in range(DEPTH):
                copy_out(f"p{l}", PTR[:, l * 512:(l + 1) * 512], bank(f"p{l}")[:, :])
            log_exp()
            act.wait_ge(dve_part, 1)
            f(SPC[:, 8:20], SPC[:, 8:20], ACT.Exp).then_inc(act_part, 1)
            squares(0, lambda g: drained(act, f"x{g}"))
            norm(0)

            nidx, pidx = 0, 0
            for l in range(DEPTH):
                if l > 0:
                    squares(nidx, lambda g: act.wait_ge(h_ready, 4 * l + g - 3))
                    norm(nidx)
                    split_after(f"pg3_{l - 1}")
                nidx += 1
                for g in range(2):
                    full(act, f"hf{g}_{l}")
                    s = slice(g * 512, (g + 1) * 512)
                    f(FG[:, s], bank(f"hf{g}_{l}")[:, :], ACT.Sigmoid)
                    f(KQ[:, s], bank(f"hf{g}_{l}")[:, :], ACT.Sigmoid, scale=-1.0).then_inc(free(f"hf{g}_{l}"), 1)
                    split_after(f"hf{g}_{l}")
                for g in range(2):
                    copy_out(f"hq{g}_{l}", QP[:, g * 512:(g + 1) * 512], bank(f"hq{g}_{l}")[:, :])
                    split_after(f"hq{g}_{l}")
                for n in range(NT):
                    copy_out(f"hi{n}_{l}", vh[:, n, :], bank(f"hi{n}_{l}")[:, :])
                    split_after(f"hi{n}_{l}")
                log_exp()
                dest = {"nq0": QN[:, 0:512], "nq1": QN[:, 512:1024], "qr0": QR[:, 0:512], "qr1": QR[:, 512:1024],
                        "vs": VT[:, 0:T], "ct": PCT[:, :], "hgo0": SG[:, 0:512], "hgo1": SG[:, 512:1024],
                        "hz0": HZ[:, 0:512], "hz1": HZ[:, 512:1024], "nz0": NZ[:, 0:512], "nz1": NZ[:, 512:1024]}
                for place, step, *arg in agenda[l]:
                    if step == "copy":
                        name, dst = f"{arg[0]}_{l}", dest[arg[0]]
                        copy_out(name, dst, bank(name)[:, 0:dst.shape[1]])
                        if arg[0] == "nq1":
                            drained(act, name)
                            f(SQ[:, 0:1024], QN[:, :], ACT.Square).then_inc(qsq_ready, 1)
                    elif step == "blocks":
                        name = f"kcvc_{l}"
                        full(act, name)
                        src = v3(bank(name), 2)
                        for g in range(2):
                            s = src[64 * g:64 * g + 64]
                            nc.scalar.copy(K2[0:64, :, g, :], s)
                            ins = nc.scalar.copy(K2[64:128, :, g, 0:T - 1], s[:, :, 1:T])
                        ins.then_inc(free(name), 1)
                    elif step == "k_square":
                        name = f"ks_{l}"
                        copy_out(name, KN[:, :], bank(name)[:, :])
                        drained(act, name)
                        f(UK[:, 0:512], KN[:, :], ACT.Square).then_inc(ksq_ready, 1)
                    elif step == "gates":
                        name = f"vw_{l}"
                        full(act, name)
                        src = bank(name)[:, 0:304].rearrange("p (n w) -> p n w", n=NT)
                        nc.scalar.copy(vt[:, 1, :, :], src[:, :, 0:P])
                        f(gates, src[:, :, P:152], ACT.Exp, scale=-1.0).then_inc(free(name), 1)
                    elif step == "q_norm":
                        head_rinv([f"qss{j}_{l}" for j in range(2)], HZ[:, :], 64, 1024).then_inc(q_rinv_ready, 1)
                    elif step == "k_norm":
                        head_rinv([f"kss_{l}"], UK[:, 512:1024], 64, 512).then_inc(k_rinv_ready, 1)
                    elif step == "hidden":
                        full(act, f"hid_{l}")
                        f(SS[:, 0:64], bank(f"hid_{l}")[:, 0:64], ACT.Exp, scale=-1.0).then_inc(hid_exp_ready, 1)
                    elif step == "k_pad":
                        name = f"kr_{l}"
                        full(act, name)
                        src = v3(bank(name), 2)
                        for g in range(2):
                            s = src[64 * g:64 * g + 64]
                            nc.scalar.copy(kz[0:64, :, 0, g, :], s)
                            ins = nc.scalar.copy(kz[64:128, :, 1, g, :], s)
                        ins.then_inc(free(name), 1)
                    elif step == "cross":
                        copy_out(f"cross_{l}", AC[:, :], bank(f"cross_{l}")[:, :])
                    elif step == "cmp_kv":
                        name = f"kc_{l}"
                        copy_out(name, KC[:, 0:32], bank(name)[:, 0:32])
                        drained(act, name)
                        f(KC[:, 32:64], KC[:, 0:32], ACT.Square).then_inc(kcsq_ready, 1)
                    elif step == "o_square":
                        for g in range(2):
                            copy_out(f"o{g}_{l}", QP[:, g * 512:(g + 1) * 512], bank(f"o{g}_{l}")[:, :])
                        drained(act, f"o1_{l}")
                        f(SQ[:, 0:1024], QP[:, :], ACT.Square).then_inc(osq_ready, 1)
                    elif step == "kc_norm":
                        head_rinv([f"kcss_{l}"], SS[:, 64:96], 64, 32).then_inc(kc_rinv_ready, 1)
                    elif step == "o_norm":
                        act.wait_ge(rope_ready, l + 1)
                        head_rinv([f"oss{g}_{l}" for g in range(2)], UK[:, :], P, 1024).then_inc(o_rinv_ready, 1)
                    elif step == "cmp_softmax":
                        act.wait_ge(cmp_shift_ready, l + 1)
                        f(SC[:, :], SC[:, :], ACT.Exp).then_inc(cmp_exp_ready, 1)
                    elif step == "scores":
                        exps(f"n{l}", arg[0], 8 * l + arg[0])
                    elif step == "values":
                        turned_copies(f"n{l}", arg[0], 8 * l + arg[0])
                    elif step == "mix":
                        drained(act, f"nz1_{l}")
                        f(FG[:, :], HZ[:, :], ACT.Sigmoid).then_inc(sig_ready, 1)
                        f(SG[:, :], SG[:, :], ACT.Sigmoid).then_inc(sig_ready, 1)
                        f(VH[:, :], NZ[:, :], ACT.Sigmoid).then_inc(sig_ready, 1)
                    split_high(place)
                mixed_high(l, [f"on{g}_{l}" for g in range(2)])
                squares(nidx, lambda g: drained(act, f"wo_{l}_{g}"), lambda g: split_after(f"wo_{l}_{g}"))

                def pp_out(g):
                    copy_out(f"pp{g}_{l}", PP[:, g * 512:(g + 1) * 512], bank(f"pp{g}_{l}")[:, :])

                pp_out(0)
                pp_out(1)
                norm(nidx)
                nidx += 1
                pp_out(2)
                pp_out(3)
                split_after(f"wo_{l}_3")
                for g in range(4):
                    name = f"pg{g}_{l}"
                    full(act, name)
                    f(Y[:, g * 512:(g + 1) * 512], bank(name)[:, :], ACT.Sigmoid).then_inc(free(name), 1)
                    if g < 3:
                        split_after(name)

            pidx = 8 * DEPTH
            for l in range(DEPTH):
                if l == 0:
                    squares(nidx, lambda g: act.wait_ge(h_ready, 4 * DEPTH + g - 3))
                    norm(nidx)
                    split_after(f"pg3_{DEPTH - 1}")
                    nidx += 1

                    def first_tap(c, src, dst, w, bias):
                        return f(dst, src, ACT.Identity, scale=w, bias=bias)

                    for g in range(2):
                        full(act, f"xa{g}")
                        for j in range(2):
                            c = 2 * g + j
                            ins = first_tap(c, bank(f"xa{g}")[:, j * T:(j + 1) * T], FG[:, c * T:(c + 1) * T],
                                            vec("lru_conv_w_2", 12 + c), vec("lru_conv_b_2", c))
                        ins.then_inc(conv_ready, 1)
                        split_after(f"xa{g}")
                    for g in range(2):
                        copy_out(f"cp{g}", KQ[:, g * 512:(g + 1) * 512], bank(f"cp{g}")[:, :])
                        split_after(f"cp{g}")
                    for g in range(2):
                        full(act, f"vb{g}")
                        split_after(f"vb{g}")
                        drained(act, f"vb{g}")
                        for j in range(2):
                            c = 2 * g + j
                            ins = first_tap(c, QP[:, c * T:(c + 1) * T], AD[:, c * T:(c + 1) * T],
                                            vec("sconv_w_2", 8 + c), vec("sconv_b_2", c))
                        ins.then_inc(conv_ready, 1)
                    for name, dst, bias in (("lr", HZ, "lru_ba_2"), ("li", NZ, "lru_bx_2")):
                        for g in range(2):
                            full(act, f"{name}{g}")
                            for j in range(2):
                                c = 2 * g + j
                                ins = f(dst[:, c * T:(c + 1) * T], bank(f"{name}{g}")[:, j * T:(j + 1) * T],
                                        ACT.Sigmoid, bias=vec(bias, c))
                            ins.then_inc(free(f"{name}{g}"), 1)
                    drained(act, "lr1")
                    act.wait_ge(small_ready, 1)
                    for c in range(4):
                        ins = f(QR[:, c * T:(c + 1) * T], HZ[:, c * T:(c + 1) * T], ACT.Tanh,
                                scale=SPC[:, 4 + c:5 + c])
                    ins.then_inc(act_part, 1)
                    for c in range(4):
                        ins = f(QN[:, c * T:(c + 1) * T], HZ[:, c * T:(c + 1) * T], ACT.Exp, scale=SPC[:, c:c + 1])
                    ins.then_inc(act_part, 1)
                    act.wait_ge(dve_part, 2)
                    f(QR[:, :], QR[:, :], ACT.Sqrt).then_inc(act_part, 1)
                    for g in range(2):
                        full(act, f"ga{g}")
                        f(SG[:, g * 512:(g + 1) * 512], bank(f"ga{g}")[:, :],
                          ACT.Gelu_apprx_tanh).then_inc(free(f"ga{g}"), 1)
                        split_after(f"ga{g}")
                    for g in range(2):
                        full(act, f"bp{g}")
                        split_after(f"bp{g}")
                    mixed_high(DEPTH, ["bp0", "bp1"])
                else:
                    squares(nidx, lambda g: drained(act, f"down{g}_0"))
                    norm(nidx)
                    split_after("down3_0")
                    nidx += 1
                    for g in range(2):
                        full(act, f"fq{g}")
                        nc.scalar.mul(QR[:, g * 512:(g + 1) * 512], bank(f"fq{g}")[:, :],
                                      0.125).then_inc(free(f"fq{g}"), 1)
                        split_after(f"fq{g}")
                    for g in range(2):
                        full(act, f"fk{g}")
                        src = v3(bank(f"fk{g}"), 2)
                        nc.scalar.copy(kz[0:64, g, 0, :, :], src[0:64])
                        nc.scalar.copy(kz[64:128, g, 1, :, :], src[64:128]).then_inc(free(f"fk{g}"), 1)
                        split_after(f"fk{g}")
                    act.wait_ge(dve_part, 3)
                    link(f(SS[0:8, :], SS[0:8, :], ACT.Exp))
                    f(SS[0:8, :], SS[0:8, :], ACT.Ln, bias=EPSC[0:8, 1:2]).then_inc(act_part, 1)
                    for n in range(NT):
                        copy_out(f"fv{n}", vh[:, n, :], bank(f"fv{n}")[:, :])
                        split_after(f"fv{n}")
                    for n in range(NT):
                        full(act, f"zg{n}")
                        f(QN[:, n * 512:(n + 1) * 512], bank(f"zg{n}")[:, :],
                          ACT.Gelu_apprx_tanh).then_inc(free(f"zg{n}"), 1)
                        split_after(f"zg{n}")
                    drained(act, "zg1")
                    f(NZ[:, :], QN[:, :], ACT.Square).then_inc(act_part, 1)
                    full(act, "zu0")
                    f(SG[:, 0:512], bank("zu0")[:, :], ACT.Gelu_apprx_tanh).then_inc(free("zu0"), 1)
                    split_after("zu0")
                    log_exp()
                    act.wait_ge(dve_part, 4)
                    link(f(NT16[:, :], NT16[:, :], ACT.Ln, bias=EPSC[:, 0:1], scale=1.0 / 64))
                    f(NT16[:, :], NT16[:, :], ACT.Exp, scale=-0.5).then_inc(act_part, 1)
                    for place, step, *arg in agenda[DEPTH + l]:
                        if step == "scores":
                            exps("f", arg[0], pidx + arg[0])
                        elif step == "values":
                            turned_copies("f", arg[0], pidx + arg[0])
                        elif step == "zu1":
                            copy_out("zu1", SG[:, 512:1024], bank("zu1")[:, :])
                        split_high(place)
                    drained(act, "zu1")
                    f(SG[:, 512:1024], SG[:, 512:1024], ACT.Gelu_apprx_tanh).then_inc(act_part, 1)
                    mixed_high(DEPTH + l, ["fo0", "fo1"])

                squares(nidx, lambda g: drained(act, f"wm_{l}_{g}"), lambda g: split_after(f"wm_{l}_{g}"))
                norm(nidx)
                split_after(f"wm_{l}_3")
                nidx += 1
                up0 = ffn_base[l]
                w0, b0 = VEC_AT["ffn_conv_w_2"] + l * 3 * 2 * NFF, VEC_AT["ffn_conv_b_2"] + l * 2 * NFF
                n0, q0 = LOAD_NO[("gate", l, 0)], SPLIT_NO[("gate", l, 0)]

                def ffn_high(kind, par, i, when):
                    n = n0 + 3 * par + 2 + kind
                    high_part(n, (q0 + FFN_SLOT[kind]) % SLOTS, when=when, landed=i * 32 + 16 * (n // SLOTS + 1))

                def rounds(par, i, first=False, last=False):
                    gate, value = 2 * par, 2 * par + 1
                    if not last:
                        act_free = i + (up0[gate] + 1)
                        ffn_high(0, par, i, panel_free[SPLIT_KEYS[q0 - 1]] if first and par == 0
                                 else (psum_full[gate], act_free))
                        ffn_high(1, par, i, (psum_full[0], up0[0] + 1) if first and par == 0
                                 else (psum_full[value], i + (up0[value] + 1)))
                    for b in (gate, value):
                        act.wait_ge(psum_full[b], i + (up0[b] + 1))
                    if not (first and l == 0):
                        act.wait_ge(gh_ready, 2 * i + (par - 1) + FF_ROUNDS * l if not first else FF_ROUNDS * l)
                    for half in range(2):
                        for j in range(2):
                            c = 2 * half + j
                            m = i * 4 + (2 * par + j + half * NFF)
                            ins = f(glu[par][:, c, :], ps[2 * par + half][:, j * T:(j + 1) * T], ACT.Identity,
                                    scale=VC[:, bass.ds(m + (w0 + 2 * 2 * NFF), 1)],
                                    bias=VC[:, bass.ds(m + b0, 1)])
                    ins.then_inc(taps_ready, 1)
                    if last:
                        n = LOAD_NO[("down", l, FF_ROUNDS - 1)]
                        high_part(n, (q0 + n - n0) % SLOTS, when=(psum_full[0], up0[0] + FF_ROUNDS // 2 + 1))
                    else:
                        ffn_high(2, par, i, (psum_full[1], up0[1] + 1) if first and par == 0
                                 else (down_done, 2 * i + (par + (FF_ROUNDS - 1) * l)))
                    act.wait_ge(psum_free[gate], i + (up0[gate] + 1))
                    f(glu[par][:, 0:2, :], glu[par][:, 0:2, :], ACT.Silu).then_inc(silu_ready, 1)
                    act.wait_ge(gf_ready, 2 * i + (par + 1 + FF_ROUNDS * l))
                    nc.scalar.copy(gh3[par], hidden[par]).then_inc(gh_ready, 1)

                rounds(0, 0, first=True)
                rounds(1, 0, first=True)
                with act.Fori(1, FF_ROUNDS // 2) as i:
                    rounds(0, i)
                    rounds(1, i)
                rounds(0, FF_ROUNDS // 2, last=True)
                next_high[0] = q0 + 3 * FF_ROUNDS
                split_after(f"ffn_up{l}")

            squares(nidx, lambda g: drained(act, f"down{g}_1"))
            norm(nidx)
            for n in range(NT):
                for g in range(2):
                    copy_out(f"out{2 * n + g}", FK[:, n * D + g * 512:n * D + (g + 1) * 512],
                             bank(f"out{2 * n + g}")[:, :])
                drained(act, f"out{2 * n + 1}")
                act.dma_start(out[0, n * P:(n + 1) * P, :], FK[:, n * D:(n + 1) * D]).then_inc(out_stored, 16)
            act.wait_ge(out_stored, 16 * NT)

        @block.vector
        def _(dve):
            steps = [0]
            V = nc.vector

            def step(ins):
                steps[0] += 1
                ins.then_inc(dve_step, 1)

            def settle():
                dve.wait_ge(dve_step, steps[0])

            def link(ins):
                step(ins)
                settle()

            def wide(col, shape):
                return col.to_broadcast(shape)

            def normed(nidx, gain, g0):
                dve.wait_ge(rinv_ready, nidx + 1)
                if nidx > 0:
                    full(dve, normed_last[nidx - 1])
                def chunk_low(c):
                    dve.wait_ge(xh_ready, 8 * nidx + c + 1)
                    V.tensor_tensor(xl3[:, c, :], xf3[:, c, :], xh3[:, c, :].bitcast(F32),
                                    ALU.subtract).then_inc(xn_ready, 1)

                for c in range(ND):
                    V.scalar_tensor_tensor(xf3[:, c, :], h3[:, c, :], vec(gain, g0 + c), RINV[:, :],
                                           ALU.mult, ALU.mult).then_inc(xf_ready, 1)
                    if nidx < 4 * DEPTH and c > 1:
                        chunk_low(c - 2)
                if nidx < 4 * DEPTH:
                    chunk_low(ND - 2)
                    chunk_low(ND - 1)

            def mixed_low(m, i):
                g = MIXED_ORDER[m][i]
                s = slice(g * 512, (g + 1) * 512)
                dve.wait_ge(yh_ready, 4 * m + i + 1)
                V.tensor_tensor(XL[:, s], Y[:, s], XH[:, s].bitcast(F32), ALU.subtract).then_inc(y_ready, 1)

            def low_part(n, slot, count, size=PANEL):
                dve.wait_ge(high_ready, count)
                V.tensor_tensor(low_slots[slot][:, 0:size], raw[n % SLOTS][:, 0:size], high_slots[slot][:, 0:size].bitcast(F32),
                                ALU.subtract).then_inc(low_ready, 1)

            next_low = [0]

            def split_low(place):
                while next_low[0] in high_from and high_from[next_low[0]] <= place:
                    q = next_low[0]
                    n = LOAD_NO[SPLIT_KEYS[q]]
                    low_part(n, q % SLOTS, q + 1, panel_size(n))
                    next_low[0] += 1

            def split_after(name):
                split_low(order_of[name])

            def row_max(tag, u, pidx):
                bb = pidx % 2
                for n, x in ((0, "Y"), (1, "X")):
                    full(dve, f"{tag}{x}{u}")
                    s3 = bank(f"{tag}{x}{u}")[:, 0:2 * (n + 1) * P].rearrange("p (r s) -> p r s", r=2)
                    ins = V.tensor_reduce(NM[:, 4 * bb + 2 * n:4 * bb + 2 * n + 2], s3, AX_X, ALU.max, negate=True)
                ins.then_inc(nmax_ready, 1)

            def normalise(tag, u, pidx, gate=None):
                bb = pidx % 2
                s4 = SM[:, 4 * bb:4 * bb + 4]
                drained(dve, f"{tag}X{u}")
                link(V.tensor_scalar(s4, s4, 1e-30, None, ALU.max))
                link(V.reciprocal(s4, s4))
                if gate is not None:
                    link(V.tensor_tensor(s4.rearrange("p (n r) -> p n r", n=NT),
                                         s4.rearrange("p (n r) -> p n r", n=NT), gate, ALU.mult))
                for n in range(NT):
                    w = (n + 1) * P
                    ins = V.tensor_tensor(probs[bb][n], probs[bb][n],
                                          s4[:, 2 * n:2 * n + 2].unsqueeze(2).to_broadcast([P, 2, w]), ALU.mult)
                ins.then_inc(p_ready, 1)

            def add_out(prefix, suffix=""):
                for g in range(4):
                    name = f"{prefix}{g}{suffix}"
                    full(dve, name)
                    s = slice(g * 512, (g + 1) * 512)
                    V.tensor_tensor(H[:, s], H[:, s], bank(name)[:, :], ALU.add).then_inc(free(name), 1)
                    if g < 3:
                        split_after(name)

            V.memset(EPSC[:, 0:1], EPS)
            V.memset(EPSC[:, 1:2], 1.0).then_inc(eps_ready, 1)
            for t in (AD, KZ, KCZ):
                V.memset(t[:, :], 0.0)
            step(V.memset(ZR[:, :], 0.0))
            dve.wait_ge(const_landed, 32)
            V.tensor_copy(IDB[:, :], ident)
            step(V.tensor_copy(NGB[:, :], const("causal_neg")))
            for g in range(4):
                full(dve, f"x{g}")
                V.tensor_copy(H[:, g * 512:(g + 1) * 512], bank(f"x{g}")[:, :]).then_inc(free(f"x{g}"), 1)
            settle()
            for g in range((NVT + 3) // 4):
                drained(dve, f"vec{g}")
            split_low(-1)
            lb = vec("hgrn_lb", 0, 8)
            mx, e = LB[:, 16:20], SPC[:, 8:16]
            link(V.tensor_tensor(mx, lb[:, 0:4], lb[:, 4:8], ALU.max))
            for l in range(DEPTH):
                V.tensor_tensor(e[:, 4 * l:4 * l + 4], lb[:, 4 * l:4 * l + 4], mx, ALU.subtract)
            lam = vec("lru_lambda_2", 0, 4)
            V.scalar_tensor_tensor(SPC[:, 16:20], lam, -1.0, lam, ALU.mult, ALU.min).then_inc(dve_part, 1)
            V.tensor_scalar(GQ[:, :], vec("nsa_qnorm_g", 0, 2), 0.125, None, ALU.mult)
            dve.wait_ge(act_part, 1)
            link(V.tensor_tensor(mx, e[:, 0:4], e[:, 4:8], ALU.add))
            link(V.reciprocal(mx, mx))
            for l in range(DEPTH):
                step(V.tensor_tensor(e[:, 4 * l:4 * l + 4], e[:, 4 * l:4 * l + 4], mx, ALU.mult))
            settle()
            V.tensor_tensor(LB[:, 0:4], e[:, 0:4], e[:, 0:4], ALU.subtract)
            link(V.tensor_tensor(LB[:, 4:8], e[:, 0:4], e[:, 4:8], ALU.add))
            link(V.tensor_tensor(LB[:, 4:8], LB[:, 4:8], e[:, 0:4], ALU.subtract))
            link(V.tensor_scalar(LB[:, 8:16], LB[:, 0:8], -1.0, 1.0, ALU.mult, ALU.add))

            for l in range(DEPTH):
                normed(2 * l, "norm_g", 8 * l)
                if l > 0:
                    split_after(f"pg3_{l - 1}")
                for g in range(2):
                    drained(dve, f"hf{g}_{l}")
                    split_after(f"hf{g}_{l}")
                for c in range(4):
                    low, rest = LB[:, 4 * l + c:4 * l + c + 1], LB[:, 8 + 4 * l + c:8 + 4 * l + c + 1]
                    s = slice(c * T, (c + 1) * T)
                    step(V.tensor_scalar(FG[:, s], FG[:, s], rest, low, ALU.mult, ALU.add))
                    ins = V.tensor_scalar(KQ[:, s], KQ[:, s], rest, None, ALU.mult)
                ins.then_inc(hg_ready, 1)

                def level(n, g):
                    name = f"lv{n}_{g}_{l}"
                    full(dve, name)
                    V.copy_predicated(AD[:, g * 512:(g + 1) * 512].rearrange("p (j t) -> p j t", j=4),
                                      v3(LM, NLVL)[:, n:n + 1, :].to_broadcast([P, 4, P]),
                                      v3(bank(name), 4)).then_inc(free(name), 1)
                    q, k = QP[:, g * 512:(g + 1) * 512], KQ[:, g * 512:(g + 1) * 512]
                    if n == 0:
                        settle()
                        V.tensor_tensor(q, q, FG[:, g * 512:(g + 1) * 512], ALU.mult).then_inc(level_ready, 1)
                        return
                    dve.wait_ge(level_ready, 16 * l + 2 * (n - 1) + g + 1)
                    h = 1 << (n - 1)
                    nb = 512 // (2 * h)
                    f_in = flevel[n - 1][:, g * (512 >> (n - 1)):(g + 1) * (512 >> (n - 1))]
                    f_in = f_in.rearrange("p (b e) -> p b e", e=2)
                    q = q.rearrange("p (b e t) -> p b e t", e=2, t=h)
                    k = k.rearrange("p (b e t) -> p b e t", e=2, t=h)
                    settle()
                    if n < NLVL - 1:
                        f_out = flevel[n][:, g * (512 >> n):(g + 1) * (512 >> n)]
                        step(V.tensor_tensor(f_out, f_in[:, :, 0], f_in[:, :, 1], ALU.mult))
                    V.tensor_tensor(q[:, :, 1, :], q[:, :, 1, :], f_in[:, :, 0:1].to_broadcast([P, nb, h]), ALU.mult)
                    V.tensor_tensor(k[:, :, 0, :], k[:, :, 0, :], f_in[:, :, 1:2].to_broadcast([P, nb, h]),
                                    ALU.mult).then_inc(level_ready, 1)

                for g in range(2):
                    split_after(f"hq{g}_{l}")
                split_after(f"hi{NT - 1}_{l}")
                for place, kind, *arg in agenda[l]:
                    if kind == "level":
                        level(*arg)
                    elif kind == "blocks":
                        drained(dve, f"kcvc_{l}")
                        pe3 = vec("cmp_pe", 32 * l, 32).rearrange("p (kv jj) -> p kv jj", kv=2)
                        V.memset(M2[:, :, :, :, NCMP:16], 0.0)
                        for kv in range(2):
                            for g in range(2):
                                src = K2[:, kv, g, 0:T].rearrange("p (c jj two) -> p jj c two", jj=8, two=2)
                                for hi in range(2):
                                    ins = V.tensor_tensor(
                                        M2[:, kv, 8 * hi:8 * hi + 8, g, 0:NCMP],
                                        src[:, :, hi:hi + NCMP, 0],
                                        pe3[:, kv, 8 * hi:8 * hi + 8].unsqueeze(2).to_broadcast([P, 8, NCMP]),
                                        ALU.add)
                        ins.then_inc(blocks_ready, 1)
                    elif kind == "gates":
                        drained(dve, f"vw_{l}")
                        link(V.tensor_scalar(GT[:, :], GT[:, :], 1.0, None, ALU.add))
                        V.reciprocal(GT[:, :], GT[:, :]).then_inc(gates_ready, 1)
                    elif kind == "q_norm":
                        dve.wait_ge(q_rinv_ready, l + 1)
                        link(V.scalar_tensor_tensor(QN[:, :], QN[:, :], GQ[:, l:l + 1], HZ[:, :],
                                                    ALU.mult, ALU.mult))
                        qn4 = v3(QN, 4)
                        for i, tab in enumerate(("cos", "sin")):
                            ins = V.tensor_tensor(UW[:, i * 1024:(i + 1) * 1024].rearrange("p (j t) -> p j t", j=4),
                                                  qn4, const(tab).unsqueeze(1).to_broadcast([P, 4, T]), ALU.mult)
                        ins.then_inc(rope_ready, 1)
                    elif kind == "k_norm":
                        dve.wait_ge(k_rinv_ready, l + 1)
                        for j in range(2):
                            s = slice(j * T, (j + 1) * T)
                            step(V.scalar_tensor_tensor(KN[:, s], KN[:, s], vec("nsa_knorm_g", 3 * l + 1 + j),
                                                        UK[:, 512 + j * T:512 + (j + 1) * T], ALU.mult, ALU.mult))
                        settle()
                        for i, tab in enumerate(("cos", "sin")):
                            ins = V.tensor_tensor(UK[:, i * 512:(i + 1) * 512].rearrange("p (j t) -> p j t", j=2),
                                                  v3(KN, 2), const(tab).unsqueeze(1).to_broadcast([P, 2, T]),
                                                  ALU.mult)
                        ins.then_inc(k_rope_ready, 1)
                    elif kind == "hidden":
                        dve.wait_ge(hid_exp_ready, l + 1)
                        link(V.tensor_scalar(SS[:, 0:64], SS[:, 0:64], 1.0, None, ALU.add))
                        link(V.reciprocal(SS[:, 0:64], SS[:, 0:64]))
                        V.tensor_tensor(HID[:, :], bank(f"hid_{l}")[:, 0:64], SS[:, 0:64],
                                        ALU.mult).then_inc(free(f"hid_{l}"), 1)
                        drained(dve, f"hid_{l}")
                        V.tensor_copy(HIDV[:, :].rearrange("p (g r c) -> p g r c", g=2, r=4),
                                      HID[:, 32:64].rearrange("p (g c) -> p g c", g=2).unsqueeze(2)
                                      .to_broadcast([P, 2, 4, 16])).then_inc(hidden_ready, 1)
                    elif kind == "cmp_kv":
                        full(dve, f"vc_{l}")
                        V.tensor_tensor(v3(VCB, 8), const("head16").unsqueeze(2).to_broadcast([P, 8, 64]),
                                        bank(f"vc_{l}")[:, 0:64].unsqueeze(1).to_broadcast([P, 8, 64]),
                                        ALU.mult).then_inc(free(f"vc_{l}"), 1)
                    elif kind == "kc_norm":
                        dve.wait_ge(kc_rinv_ready, l + 1)
                        for r in range(2):
                            h = slice(64 * r, 64 * r + 64)
                            ins = V.scalar_tensor_tensor(KCZ[h, 32 * r:32 * r + 32], KC[h, 0:32],
                                                         vec("nsa_knorm_g", 3 * l)[h, :], SS[h, 64:96],
                                                         ALU.mult, ALU.mult)
                        ins.then_inc(kc_ready, 1)
                    elif kind == "o_norm":
                        dve.wait_ge(o_rinv_ready, l + 1)
                        step(V.scalar_tensor_tensor(QP[:, :], QP[:, :], vec("hgrn_onorm_g", l), UK[:, :],
                                                    ALU.mult, ALU.mult))
                    elif kind == "cmp_softmax":
                        name = f"cs_{l}"
                        full(dve, name)
                        s4 = SC[:, :].rearrange("p (n h c) -> p n h c", n=NT, h=8)
                        s3 = SC[:, :].rearrange("p (q c) -> p q c", c=16)
                        r2 = SS[:, 96:112]

                        def by_tile(tab):
                            return const(tab).rearrange("p (n c) -> p n c", n=NT).unsqueeze(2) \
                                .to_broadcast([P, NT, 8, 16])

                        V.tensor_tensor(s4, by_tile("cmp_neg"),
                                        bank(name)[:, 0:256].rearrange("p (n h c) -> p n h c", n=NT, h=8),
                                        ALU.add).then_inc(free(name), 1)
                        drained(dve, name)
                        link(V.tensor_reduce(r2, s3, AX_X, ALU.max))
                        V.tensor_tensor(s3, s3, r2.unsqueeze(2).to_broadcast([P, 16, 16]),
                                        ALU.subtract).then_inc(cmp_shift_ready, 1)
                        dve.wait_ge(cmp_exp_ready, l + 1)
                        link(V.tensor_tensor(s4, s4, by_tile("cmp_seen"), ALU.mult))
                        link(V.tensor_reduce(r2, s3, AX_X, ALU.add))
                        link(V.tensor_scalar(r2, r2, 1e-30, None, ALU.max))
                        link(V.reciprocal(r2, r2))
                        link(V.tensor_tensor(r2.rearrange("p (n h) -> p n h", n=NT),
                                             r2.rearrange("p (n h) -> p n h", n=NT), gates[:, :, 0:8], ALU.mult))
                        V.tensor_tensor(s3, s3, r2.unsqueeze(2).to_broadcast([P, 16, 16]),
                                        ALU.mult).then_inc(cp_ready, 1)
                    elif kind == "scores":
                        row_max(f"n{l}", arg[0], 8 * l + arg[0])
                    elif kind == "values":
                        u = arg[0]
                        g0 = 8 * (u // 4 + 1) + 2 * (u % 4)
                        normalise(f"n{l}", u, 8 * l + u, gates[:, :, g0:g0 + 2])
                    elif kind == "mix":
                        dve.wait_ge(sig_ready, 3 * l + 1)
                        link(V.tensor_tensor(HZ[:, :], HZ[:, :], FG[:, :], ALU.mult))
                        dve.wait_ge(sig_ready, 3 * l + 2)
                        link(V.tensor_tensor(HZ[:, :], HZ[:, :], SG[:, :], ALU.mult))
                        for g in range(2):
                            s = slice(g * 512, (g + 1) * 512)
                            V.tensor_tensor(Y[:, s], QP[:, s], HZ[:, s], ALU.mult).then_inc(yf_ready, 1)
                        dve.wait_ge(sig_ready, 3 * l + 3)
                        link(V.tensor_tensor(NZ[:, :], NZ[:, :], VH[:, :], ALU.mult))
                        for g in range(2):
                            name = f"on{g}_{l}"
                            full(dve, name)
                            V.tensor_tensor(Y[:, 1024 + g * 512:1024 + (g + 1) * 512], bank(name)[:, :],
                                            NZ[:, g * 512:(g + 1) * 512], ALU.mult).then_inc(free(name), 1)
                            mixed_low(l, g)
                        for g in range(2, 4):
                            mixed_low(l, g)
                    split_low(place)
                add_out(f"wo_{l}_")
                normed(2 * l + 1, "ple_norm_g", 8 * l)
                split_after(f"wo_{l}_3")
                for g in range(4):
                    drained(dve, f"pg{g}_{l}")
                    drained(dve, f"pp{g}_{l}")
                    s = slice(g * 512, (g + 1) * 512)
                    link(V.tensor_tensor(Y[:, s], Y[:, s], PP[:, s], ALU.mult))
                    V.tensor_tensor(H[:, s], H[:, s], Y[:, s], ALU.add).then_inc(h_ready, 1)
                    if g < 3:
                        split_after(f"pg{g}_{l}")

            z, s, s2, q = SPC[:, 16:20], SPC[:, 20:24], SPC[:, 24:28], SPC[:, 28:32]
            link(V.tensor_scalar(s, z, 2.0, None, ALU.add))
            link(V.reciprocal(s, s))
            link(V.tensor_tensor(s, s, z, ALU.mult))
            link(V.tensor_tensor(s2, s, s, ALU.mult))
            link(V.tensor_scalar(q, s2, 1.0 / 19, None, ALU.mult))
            for k in range(17, 1, -2):
                link(V.scalar_tensor_tensor(q, q, 1.0 / k, s2, ALU.add, ALU.mult))
            link(V.tensor_scalar(q, q, 1.0, 2.0, ALU.add, ALU.mult))
            link(V.tensor_tensor(q, q, s, ALU.mult))
            link(V.tensor_scalar(s, vec("lru_lambda_2", 0, 4), -1.0, 0.0, ALU.mult, ALU.max))
            link(V.tensor_tensor(q, q, s, ALU.add))
            V.tensor_scalar(SPC[:, 0:4], q, -8.0, None, ALU.mult)
            V.tensor_scalar(SPC[:, 4:8], q, 8.0, None, ALU.mult).then_inc(small_ready, 1)

            nidx = 2 * DEPTH
            for l in range(DEPTH):
                if l == 0:
                    normed(nidx, "mix0_norm_2", 0)
                    split_after(f"pg3_{DEPTH - 1}")
                    V.memset(PB[:, 0:1024], 0.0).then_inc(bd_zeroed, 1)

                    def taps(name, g, src, dst, wname, n):
                        for back in range(1, n):
                            for j in range(2):
                                c = 2 * g + j
                                d = dst[:, c * T + back:(c + 1) * T]
                                ins = V.scalar_tensor_tensor(d, src(j)[:, 0:T - back],
                                                             vec(wname, 4 * (n - 1 - back) + c), d,
                                                             ALU.mult, ALU.add)
                                if back < n - 1 or j == 0:
                                    step(ins)
                            settle()
                        return ins

                    for g in range(2):
                        dve.wait_ge(conv_ready, g + 1)
                        src = bank(f"xa{g}")
                        taps(f"xa{g}", g, lambda j: src[:, j * T:(j + 1) * T], FG, "lru_conv_w_2",
                             4).then_inc(free(f"xa{g}"), 1)
                        split_after(f"xa{g}")
                    for g in range(2):
                        drained(dve, f"cp{g}")
                        full(dve, f"vb{g}")
                        V.tensor_tensor(QP[:, g * 512:(g + 1) * 512], bank(f"vb{g}")[:, :],
                                        KQ[:, g * 512:(g + 1) * 512], ALU.mult).then_inc(free(f"vb{g}"), 1)
                        split_after(f"vb{g}")
                    for g in range(2):
                        dve.wait_ge(conv_ready, 3 + g)
                        step(taps(None, g, lambda j: QP[:, (2 * g + j) * T:(2 * g + j + 1) * T], AD,
                                  "sconv_w_2", 3))
                    drained(dve, "li1")
                    link(V.tensor_tensor(NZ[:, :], NZ[:, :], FG, ALU.mult))
                    dve.wait_ge(act_part, 3)
                    link(V.tensor_tensor(UW[:, 0:1024], QN[:, :], QN[:, :], ALU.mult))
                    V.scalar_tensor_tensor(QR[:, :], UW[:, 0:1024], 1.0, QR[:, :], ALU.add,
                                           ALU.mult).then_inc(dve_part, 1)
                    dve.wait_ge(act_part, 4)
                    link(V.tensor_tensor(QR[:, :], QR[:, :], NZ[:, :], ALU.mult))
                    for c in range(4):
                        s = slice(c * T, (c + 1) * T)
                        step(V.tensor_tensor_scan(KQ[:, c * T:(c + 1) * T], QN[:, s], QR[:, s], 0.0,
                                                  ALU.mult, ALU.add))
                    for g in range(2):
                        drained(dve, f"ga{g}")
                        split_after(f"ga{g}")
                    for g in range(2):
                        full(dve, f"bp{g}")
                        V.tensor_tensor(Y[:, 1024 + g * 512:1024 + (g + 1) * 512], bank(f"bp{g}")[:, :],
                                        AD[:, g * 512:(g + 1) * 512], ALU.mult).then_inc(free(f"bp{g}"), 1)
                        split_after(f"bp{g}")
                    settle()
                    for g in range(2):
                        s = slice(g * 512, (g + 1) * 512)
                        V.tensor_tensor(Y[:, s], KQ[:, s], SG[:, s], ALU.mult).then_inc(yf_ready, 1)
                    for i in range(4):
                        mixed_low(DEPTH, i)
                else:
                    normed(nidx, "mix1_norm_2", 0)
                    split_after("down3_0")
                    for name in ("fq0", "fq1", "fk0", "fk1"):
                        split_after(name)
                    dve.wait_ge(bias_landed, 16)
                    full(dve, "fl")
                    V.tensor_scalar(SC[0:8, :], bank("fl")[0:8, 0:T], BF[0:8, 0:1], None,
                                    ALU.add).then_inc(free("fl"), 1)
                    drained(dve, "fl")
                    V.scalar_tensor_tensor(SS[0:8, :], SC[0:8, :], -1.0, SC[0:8, :], ALU.mult,
                                           ALU.min).then_inc(dve_part, 1)
                    link(V.tensor_scalar(SC[0:8, :], SC[0:8, :], 0.0, None, ALU.min))
                    dve.wait_ge(act_part, 5)
                    link(V.tensor_tensor(SC[0:8, :], SS[0:8, :], SC[0:8, :], ALU.subtract))
                    link(V.tensor_tensor_scan(PCT[0:8, :], ones[0:8, 0:1].to_broadcast([8, T]), SC[0:8, :], 0.0,
                                              ALU.mult, ALU.add))
                    V.tensor_tensor(UW[0:8, :].rearrange("p (h t) -> p h t", h=8),
                                    PCT[0:8, :].unsqueeze(1).to_broadcast([8, 8, T]),
                                    ident[0:8, 0:8].unsqueeze(2).to_broadcast([8, 8, T]),
                                    ALU.mult).then_inc(forget_ready, 1)
                    for name in ("fv0", "fv1", "zg0", "zg1"):
                        split_after(name)
                    for g in range(2):
                        full(dve, f"wt{g}")
                        V.tensor_tensor(AD[:, g * 512:(g + 1) * 512].rearrange("p (j t) -> p j t", j=4),
                                        v3(bank(f"wt{g}"), 4), const("upper").unsqueeze(1).to_broadcast([P, 4, P]),
                                        ALU.mult).then_inc(free(f"wt{g}"), 1)
                    dve.wait_ge(act_part, 6)
                    V.tensor_reduce(NT16[:, :], NZ[:, :].rearrange("p (q d) -> p q d", d=64), AX_X,
                                    ALU.add).then_inc(dve_part, 1)
                    todo = list(agenda[DEPTH + l])
                    for place, kind, *arg in todo:
                        if kind == "scores":
                            row_max("f", arg[0], 8 * DEPTH + arg[0])
                            if arg[0] == 0:
                                dve.wait_ge(act_part, 7)
                                V.tensor_tensor(QN[:, :].rearrange("p (q d) -> p q d", d=64),
                                                QN[:, :].rearrange("p (q d) -> p q d", d=64),
                                                NT16[:, :].unsqueeze(2).to_broadcast([P, 16, 64]),
                                                ALU.mult).then_inc(sgu_ready, 1)
                        elif kind == "values":
                            normalise("f", arg[0], 8 * DEPTH + arg[0])
                        elif kind in ("sg0", "sg1"):
                            g = int(kind[2])
                            full(dve, kind)
                            if g == 0:
                                dve.wait_ge(bt_landed, 16 * 8)
                            for j in range(2):
                                c = 2 * g + j
                                ins = V.scalar_tensor_tensor(
                                    v3(HZ, 4)[:, c, :].rearrange("p (n t) -> p n t", n=NT),
                                    bank(kind)[:, j * T:(j + 1) * T].rearrange("p (n t) -> p n t", n=NT),
                                    vec("sgu_norm_2", c), v3(AC, 4)[:, c:c + 1, :].to_broadcast([P, NT, P]),
                                    ALU.mult, ALU.add)
                            ins.then_inc(free(kind), 1)
                        split_low(place)
                    for g in range(2):
                        full(dve, f"fo{g}")
                        V.tensor_copy(Y[:, 1024 + g * 512:1024 + (g + 1) * 512],
                                      bank(f"fo{g}")[:, :]).then_inc(free(f"fo{g}"), 1)
                    drained(dve, "sg1")
                    dve.wait_ge(act_part, 8)
                    for g in range(2):
                        s = slice(g * 512, (g + 1) * 512)
                        V.tensor_tensor(Y[:, s], HZ[:, s], SG[:, s], ALU.mult).then_inc(yf_ready, 1)
                    for i in range(4):
                        mixed_low(DEPTH + l, i)
                nidx += 1
                add_out(f"wm_{l}_")

                normed(nidx, "ffn_norm_2", 8 * l)
                split_after(f"wm_{l}_3")
                nidx += 1
                w0 = VEC_AT["ffn_conv_w_2"] + l * 3 * 2 * NFF

                n0, q0, up0 = LOAD_NO[("gate", l, 0)], SPLIT_NO[("gate", l, 0)], ffn_base[l]

                def ffn_low(kind, par, i):
                    low_part(n0 + 3 * par + 2 + kind, (q0 + FFN_SLOT[kind]) % SLOTS, 6 * i + (q0 + 3 * par + 3 + kind))

                def rounds(par, i, last=False):
                    if not last:
                        ffn_low(0, par, i)
                        ffn_low(1, par, i)
                    dve.wait_ge(taps_ready, 2 * i + (par + 1 + FF_ROUNDS * l))
                    for back in (1, 2):
                        if back == 2:
                            dve.wait_ge(first_back_done, 2 * i + (par + 1 + FF_ROUNDS * l))
                        for half in range(2):
                            for j in range(2):
                                m = i * 4 + (2 * par + j + half * NFF)
                                d = glu[par][:, 2 * half + j, back:T]
                                ins = V.scalar_tensor_tensor(
                                    d, ps[2 * par + half][:, j * T:(j + 1) * T - back],
                                    VC[:, bass.ds(m + (w0 + (2 - back) * 2 * NFF), 1)], d, ALU.mult, ALU.add)
                            if back == 2:
                                ins.then_inc(psum_free[2 * par + half], 1)
                        if back == 1:
                            ins.then_inc(first_back_done, 1)
                    if last:
                        n = LOAD_NO[("down", l, FF_ROUNDS - 1)]
                        low_part(n, (q0 + n - n0) % SLOTS, q0 + 3 * FF_ROUNDS)
                    else:
                        ffn_low(2, par, i)
                    dve.wait_ge(psum_free[2 * par + 1], i + (up0[2 * par + 1] + 1))
                    dve.wait_ge(silu_ready, 2 * i + (par + 1 + FF_ROUNDS * l))
                    V.tensor_tensor(hidden[par], glu[par][:, 0:2, :], glu[par][:, 2:4, :],
                                    ALU.mult).then_inc(gf_ready, 1)
                    dve.wait_ge(gh_ready, 2 * i + (par + 1 + FF_ROUNDS * l))
                    V.tensor_tensor(gl3[par], hidden[par], gh3[par].bitcast(F32), ALU.subtract).then_inc(act_ready, 1)

                rounds(0, 0)
                rounds(1, 0)
                with dve.Fori(1, FF_ROUNDS // 2) as i:
                    rounds(0, i)
                    rounds(1, i)
                rounds(0, FF_ROUNDS // 2, last=True)
                next_low[0] = q0 + 3 * FF_ROUNDS
                split_after(f"ffn_up{l}")
                add_out(f"down", f"_{l}")

            normed(nidx, "final_norm_2", 0)

        @block.sync
        def _(sp):
            def slot_empty(n):
                if n >= SLOTS:
                    key = LOADS[n - SLOTS][0]
                    if key in SPLIT_NO:
                        sp.wait_ge(low_ready, SPLIT_NO[key] + 1)
                    else:
                        sp.wait_ge(*panel_free[key])

            def load_panel(n):
                (name, l, *r), src, c0, cols = LOADS[n]
                slot_empty(n)
                w = {"gate": "ffn_up_2", "value": "ffn_up_2", "down": "ffn_down_2"}.get(src, src)
                w = a[w][l % DEPTH if a[w].shape[0] == DEPTH else 0]
                if src == "cmp_w1":
                    w, c0 = w[c0], 0
                elif src in ("gate", "value"):
                    c0 = r[0] * T + (FF if src == "value" else 0)
                elif src == "down":
                    w, c0, cols = w[r[0] * T:(r[0] + 1) * T], 0, D
                nk = w.shape[0] // P
                sp.dma_start(raw[n % SLOTS][:, 0:nk * cols].rearrange("p (k n) -> p k n", k=nk),
                             w[:, c0:c0 + cols].rearrange("(k p) n -> p k n", p=P)).then_inc(panel_landed[n % SLOTS], 16)

            sp.dma_start(CN[:, :], a["const_table"]).then_inc(const_landed, 16)
            sp.dma_start(xt, a["x"][0].rearrange("(n p) d -> p n d", p=P)).then_inc(x_landed, 16)
            for tile, r, n, c0, c1, src in vec_dmas:
                sp.dma_start(vrows[r:r + n, tile, c0:c1], src).then_inc(vec_landed, 16)
            sp.dma_start(ptok.rearrange("p (l n) d -> p l n d", l=DEPTH),
                         a["p"][:, 0].rearrange("l (n p) d -> p l n d", p=P)).then_inc(p_landed, 16)
            sp.dma_start(LM[:, :], a["mask_table"]).then_inc(const_landed, 16)
            sp.dma_start(BF[0:8, 0:1], a["fox_bf_2"].rearrange("a h -> h a")).then_inc(bias_landed, 16)

            def ffn(l):
                n0, q0 = LOAD_NO[("gate", l, 0)], SPLIT_NO[("gate", l, 0)]

                def round_loads(par, i):
                    for kind in range(3):
                        n = n0 + 3 * par + 2 + kind
                        sp.wait_ge(low_ready, 6 * i + (q0 + 3 * par + kind))
                        if kind < 2:
                            w = a["ffn_up_2"][l].rearrange("(k p) n -> p k n", p=P)
                            src = w[:, :, bass.ds(i * 512 + ((par + 1) * T + kind * FF), T)]
                        else:
                            src = a["ffn_down_2"][l][bass.ds(i * 512 + par * T, T), :].rearrange(
                                "(k p) n -> p k n", p=P)
                        dst = raw[n % SLOTS].rearrange("p (k n) -> p k n", k=ND if kind < 2 else 2)
                        sp.dma_start(dst, src).then_inc(panel_landed[n % SLOTS], 16)

                for n in range(n0 + 2, n0 + 8):
                    load_panel(n)
                with sp.Fori(1, FF_ROUNDS // 2) as i:
                    round_loads(0, i)
                    round_loads(1, i)
                load_panel(n0 + 3 * FF_ROUNDS - 1)

            for n, (key, *_) in enumerate(LOADS):
                if len(key) == 2 or key[0] != "down" and key[2] == 0:
                    load_panel(n)
                name, l, *r = key
                if name == "cmp0":
                    if l > 0:
                        b, k = fills[f"vc_{l - 1}"]
                        sp.wait_ge(psum_full[b], k + 1)
                    for c0, kv in ((0, 0), (64, 0), (P, 1)):
                        sp.dma_start(W2[:, c0:c0 + 64], a["cmp_w2"][l, kv]).then_inc(w2_landed, 16)
                if name == "vb0":
                    sp.wait_ge(bd_zeroed, 1)
                    for at, w in ((0, "lru_wa_2"), (512, "lru_wx_2")):
                        src = a[w][0].rearrange("(c r) i j -> r i c j", r=2)
                        for r in range(2):
                            dst = PB[64 * r:64 * r + 64, at:at + 512].rearrange("p (c m) -> p c m", c=4)
                            sp.dma_start(dst[:, :, 64 * r:64 * r + 64], src[r]).then_inc(bd_landed, 16)
                if name == "fk0":
                    sp.dma_start(PT[:, 0:1024].rearrange("p (h s) -> p h s", h=8),
                                 a["sgu_w_2"][0].rearrange("h t s -> t h s")).then_inc(sgu_landed, 16)
                    for h in range(8):
                        r, c = h % 2, h // 2
                        sp.dma_start(AC[64 * r:64 * r + 64, c * P:(c + 1) * P],
                                     a["sgu_b_2"][0, h:h + 1, :].to_broadcast([64, P])).then_inc(bt_landed, 16)
                if name == "value" and r == [0]:
                    ffn(l)


_INS = ["x", "p", "norm_g", "w_in", "hgrn_lb", "hgrn_onorm_g", "nsa_qnorm_g", "nsa_knorm_g", "cmp_pe", "cmp_w1",
        "cmp_w2", "w_out", "ple_norm_g", "w_pg", "w_pp", "mix0_norm_2", "mix0_w_in_2", "lru_conv_w_2",
        "lru_conv_b_2", "lru_wa_2", "lru_ba_2", "lru_wx_2", "lru_bx_2", "lru_lambda_2", "sconv_w_2", "sconv_b_2",
        "mix0_w_out_2", "mix1_norm_2", "mix1_w_in_2", "sgu_norm_2", "sgu_w_2", "sgu_b_2", "fox_bf_2",
        "mix1_w_out_2", "ffn_norm_2", "ffn_up_2", "ffn_conv_w_2", "ffn_conv_b_2", "ffn_down_2", "final_norm_2"]


def kernel(**inputs):
    import concourse.bacc as bacc
    from concourse.bass_utils import run_bass_kernel_spmd

    nc = bacc.Bacc("TRN2", target_bir_lowering=False, num_devices=1)
    arrays, args = {}, {}
    table, masks = const_table()
    for name, value in [(n, inputs[n]) for n in _INS] + [("const_table", table), ("mask_table", masks)]:
        v = np.ascontiguousarray(value)
        arrays[f"in_{name}"] = v
        args[name] = nc.dram_tensor(f"in_{name}", v.shape, mybir.dt.from_np(v.dtype), kind="ExternalInput").ap()
    out = nc.dram_tensor("out", (1, T, D), F32, kind="ExternalOutput").ap()
    build(nc, args, out)
    r = run_bass_kernel_spmd(nc, [arrays], core_ids=[0])
    return r.results[0]["out"]
```

```python
from contextlib import ExitStack

import numpy as np

import concourse.bass as bass
from concourse import mybir

P = 128
T = 256
NT = T // P
D = 1024
ND = D // P
DEPTH = 2
HALF = 512
NH4 = HALF // P
IN1 = 4376
PLE = 256
FF = 2816
NFF = FF // P
FF_ROUNDS = NFF // 2
VG = 128 + 24
NCMP = 15
EPS = 1e-6
NEG = -1e30
SLOTS = 3
PANEL = 2048
NLVL = 8

ALU = mybir.AluOpType
ACT = mybir.ActivationFunctionType
F32 = mybir.dt.float32
F32R = mybir.dt.float32r
BF16 = mybir.dt.bfloat16
I32 = mybir.dt.int32
AX_X = mybir.AxisListType.X
LOG_EXP = "natural_log_exp_and_others"

CONST_COLS = {}


def const_table():
    p = np.arange(P)
    parts = [("ident", np.eye(P)), ("ones", np.ones((P, P))),
             ("head_ones", (p[:, None] // 64 == p[None, :] // 64).astype(float))]
    rot = np.zeros((P, P))
    for h in (0, 64):
        for d in range(8):
            rot[h + 8 + d, h + d] = -1.0
            rot[h + d, h + 8 + d] = 1.0
    parts.append(("rot", rot))
    inv = (np.float32(500000.0) ** (-np.arange(0, 16, 2, dtype=np.float32) / np.float32(16))).astype(np.float32)
    ang = np.arange(T, dtype=np.float32)[None, :] * inv[:, None]
    cos, sin = np.ones((P, T)), np.zeros((P, T))
    for h in (0, 8, 64, 72):
        cos[h:h + 8] = np.cos(ang.astype(np.float32))
        sin[h:h + 8] = np.sin(ang.astype(np.float32))
    parts += [("cos", cos), ("sin", sin)]
    t = p[:, None, None] + P * np.arange(NT)[None, :, None]
    seen = (16 * np.arange(16)[None, None, :] + 31 <= t).astype(float)
    parts += [("cmp_neg", ((1 - seen) * NEG).reshape(P, NT * 16)), ("cmp_seen", seen.reshape(P, NT * 16))]
    parts.append(("head16", (p[:, None] // 16 == np.arange(8)[None, :]).astype(float)))
    parts.append(("upper", (p[:, None] <= p[None, :]).astype(float)))
    parts.append(("causal_neg", np.where(p[None, :] > p[:, None], NEG, 0.0)))
    at = 0
    for name, a in parts:
        CONST_COLS[name] = (at, a.shape[1])
        at += a.shape[1]
    levels = [(p[:, None] == p[None, :])]
    for n in range(1, NLVL):
        h = 1 << (n - 1)
        levels.append((p[:, None] // (2 * h) == p[None, :] // (2 * h)) & (p[:, None] % (2 * h) < h)
                      & (p[None, :] % (2 * h) >= h))
    masks = np.stack(levels, axis=1).astype(np.int32).reshape(P, NLVL * P)
    return np.concatenate([a for _, a in parts], axis=1).astype(np.float32), masks


const_table()
NCONST = max(a + n for a, n in CONST_COLS.values())

VEC_ROWS = [("norm_g", 16), ("ple_norm_g", 16), ("hgrn_lb", 8), ("hgrn_onorm_g", 2), ("nsa_qnorm_g", 2),
            ("nsa_knorm_g", 6), ("cmp_pe", 64), ("mix0_norm_2", 8), ("lru_conv_w_2", 16), ("lru_conv_b_2", 4),
            ("lru_ba_2", 4), ("lru_bx_2", 4), ("lru_lambda_2", 4), ("sconv_w_2", 12), ("sconv_b_2", 4),
            ("mix1_norm_2", 8), ("sgu_norm_2", 4), ("ffn_norm_2", 16), ("final_norm_2", 8),
            ("ffn_conv_w_2", 264), ("ffn_conv_b_2", 88)]
VEC_AT, _n = {}, 0
for _name, _rows in VEC_ROWS:
    VEC_AT[_name] = _n
    _n += _rows
NVEC = _n
NVT = (NVEC + P - 1) // P
DUPLICATED = ("nsa_qnorm_g", "nsa_knorm_g")

FIRST_PANELS = [(f"{name}{h}", "w_in", c0 + 256 * h, 256) for name, c0 in
                (("hf", 512), ("hq", 0), ("hi", 1024), ("nq", 2560), ("kv", 3072)) for h in range(2)]
FIRST_PANELS += [("kw0", "w_in", 3584, P), ("kw1", "w_in", 3712, VG),
                 ("cmp0", "cmp_w1", 0, P), ("cmp1", "cmp_w1", 1, P)]
FIRST_PANELS += [(f"{name}{h}", "w_in", c0 + 256 * h, 256) for name, c0 in
                 (("hgo", 1536), ("hz", 2048), ("nz", IN1 - HALF)) for h in range(2)]
FIRST_PANELS += [(f"wo{g}", "w_out", 256 * g, 256) for g in range(4)]
FIRST_PANELS += [("pp", "w_pp", 0, D)] + [(f"pg{g}", "w_pg", 256 * g, 256) for g in range(4)]
EVEN_PANELS = [(f"{name}{h}", "mix0_w_in_2", c0 + 256 * h, 256) for name, c0 in
               (("xa", 0), ("ga", 512), ("cp", 1024), ("vb", 2048), ("bp", 1536)) for h in range(2)]
EVEN_PANELS += [(f"wo{g}", "mix0_w_out_2", 256 * g, 256) for g in range(4)]
ODD_PANELS = [(f"{name}{h}", "mix1_w_in_2", c0 + 256 * h, 256) for name, c0 in
              (("fq", 1024), ("fk", 1536)) for h in range(2)]
ODD_PANELS += [("ff", "mix1_w_in_2", 2560, 8)]
ODD_PANELS += [(f"{name}{h}", "mix1_w_in_2", c0 + 256 * h, 256) for name, c0 in
               (("fv", 2048), ("zg", 512), ("zu", 0)) for h in range(2)]
ODD_PANELS += [(f"wo{g}", "mix1_w_out_2", 256 * g, 256) for g in range(4)]
AS_THEY_ARE = ("cmp0", "cmp1", "pp", "ff")


def panel_plan():
    loads, load_no, split_no = [], {}, {}

    def put(key, src, c0, n, split=True):
        load_no[key] = len(load_no)
        if split:
            split_no[key] = len(split_no)
        loads.append((key, src, c0, n))

    for block in range(2):
        for l in range(DEPTH):
            for name, src, c0, n in FIRST_PANELS if block == 0 else (EVEN_PANELS, ODD_PANELS)[l]:
                put((name, DEPTH * block + l), src, c0, n, name not in AS_THEY_ARE)
            if block == 1:
                order = [("gate", 0), ("value", 0)]
                for r in range(FF_ROUNDS):
                    order += [("gate", r + 1), ("value", r + 1)] if r + 1 < FF_ROUNDS else []
                    order += [("down", r)]
                for kind, r in order:
                    put((kind, l, r), kind, r, T)
    return loads, load_no, split_no


LOADS, LOAD_NO, SPLIT_NO = panel_plan()
FFN_SLOT = (2, 0, 1)
SPLIT_KEYS = list(SPLIT_NO)


def build(nc, a, out):
    fills = {}
    bank_fills = [0] * 8

    with ExitStack() as ctx:
        def sb(name, cols, dt=F32):
            return ctx.enter_context(nc.sbuf_tensor(name, [P, cols], dt))

        sems = {}

        def sem(name):
            if name not in sems:
                sems[name] = ctx.enter_context(nc.semaphore(name))
            return sems[name]

        ps = [ctx.enter_context(nc.psum_tensor(f"ps{b}", [P, 512], F32)) for b in range(8)]
        psum_full = [sem(f"psum_full{b}") for b in range(8)]
        psum_free = [sem(f"psum_free{b}") for b in range(8)]
        panel_landed = [sem(f"panel_landed{s}") for s in range(SLOTS)]
        high_ready, low_ready = sem("panel_high_ready"), sem("panel_low_ready")
        panel_free = {}
        order_of = {}
        high_from = {}
        split_from = {}

        def v3(t, n, off=0):
            w = t.shape[1] - off
            return t[:, off:off + w].rearrange("p (n w) -> p n w", n=n)

        H = sb("residual", ND * T)
        XH, XL = sb("input_high", ND * T, F32R), sb("input_low", ND * T, F32R)
        SQ = sb("squares", ND * T)
        RAW = sb("panels", SLOTS * PANEL)
        HI, LO = sb("panels_high", SLOTS * PANEL, F32R), sb("panels_low", SLOTS * PANEL, F32R)
        Y = UW = XF = SQ
        RINV = sb("rinv", T)
        CN = sb("consts", NCONST)
        LM = sb("level_masks", NLVL * P, I32)
        VC = sb("vectors", NVT * P)
        IDB = sb("ident_bf16", P, BF16)
        NGB = sb("causal_neg_bf16", P, BF16)
        EPSC = sb("eps", 2)
        LB = sb("lower_bound", 32)
        GQ = sb("q_gain_scaled", 2)
        SPC = sb("lru_rate", 40)
        W2 = sb("cmp_w2", 256)
        FK = sb("forget_key", 2048)
        FG, KQ = FK[:, 0:1024], FK[:, 1024:2048]
        QP = sb("query", 1024)
        AD = sb("decay_diag", 1024)
        VH = sb("values_hg", 1024)
        SG = FLV = sb("gate_o", 1024)
        HZ = sb("gate_z", 1024)
        NZ = sb("nsa_z", 1024)
        QN = sb("q_nope", 1024)
        QR = sb("q_rope", 1024)
        AC = sb("decay_cross", 512)
        VT = sb("values_nsa", 512)
        GT = sb("nsa_gates", 48)
        KN = sb("k_normed", 512)
        UK = sb("k_rope_terms", 1024)
        KZ = sb("k_padded", 2048)
        PB = sb("probs", 2 * 768)
        PT = sb("probs_t", 2 * 768)
        SC = sb("cmp_scores", 256)
        SS = sb("small", 256)
        PCT = sb("cmp_probs_t", 256)
        VCB = sb("cmp_values", 512)
        HID = sb("cmp_hidden", 64)
        HIDV = sb("cmp_hidden_rep", P)
        KC = sb("cmp_k", 64)
        KCZ = sb("cmp_k_padded", 64)
        NM = sb("neg_max", 8)
        SM = sb("prob_sums", 8)
        PP = FK
        ZR = sb("zeros", P)
        NT16 = sb("head_stats", 16)

        raw, high_slots, low_slots = ([t[:, s * PANEL:(s + 1) * PANEL] for s in range(SLOTS)] for t in (RAW, HI, LO))

        def const(name):
            at, n = CONST_COLS[name]
            return CN[:, at:at + n]

        def vec(name, n=0, m=1):
            at = VEC_AT[name] + n
            return VC[:, at:at + m]

        h3, xf3, sq3, xh3, xl3 = (v3(t, ND) for t in (H, XF, SQ, XH, XL))
        ident = const("ident")
        K2 = PB[:, 0:1024].rearrange("p (kv g t) -> p kv g t", kv=2, g=2)
        M2 = PT[:, 0:1024].rearrange("p (kv jj g c) -> p kv jj g c", kv=2, jj=16, g=2)
        kz = KZ[:, :].rearrange("p (k par g t) -> p k par g t", k=2, par=2, g=2)
        ad = AD[:, :].rearrange("p (h n t) -> p h n t", h=4, n=NT)
        ac = v3(AC, 4)
        vh = v3(VH, NT)
        vt = VT[:, :].rearrange("p (k n d) -> p k n d", k=2, n=NT)
        gates = GT[:, :].rearrange("p (n a) -> p n a", n=NT)
        probs = [[PB[:, b * 768:b * 768 + 256].rearrange("p (r s) -> p r s", r=2),
                  PB[:, b * 768 + 256:b * 768 + 768].rearrange("p (r s) -> p r s", r=2)] for b in range(2)]
        pt_lo = [PT[:, b * 768:b * 768 + 512].rearrange("p (r t) -> p r t", r=2) for b in range(2)]
        pt_hi = [PT[:, b * 768 + 512:b * 768 + 768].rearrange("p (r t) -> p r t", r=2) for b in range(2)]
        flevel = {0: FG}
        at = 0
        for n in range(1, NLVL):
            w = 1024 >> n
            flevel[n] = FLV[:, at:at + w]
            at += w
        xt = FK[:, :].rearrange("p (n d) -> p n d", n=NT)
        ptok = QR[:, :].rearrange("p (l d) -> p l d", l=2 * NT)
        PTR = ctx.enter_context(nc.sbuf_tensor("p_transposed", [P, 1024], F32))
        ptr = PTR[:, :].rearrange("p (l k t) -> p l k t", l=DEPTH, k=2)
        vrows = v3(QN, 8)

        def panel_size(n):
            name, l, *r = LOADS[n][0]
            return {"kw0": ND * P, "kw1": ND * VG, "ff": ND * 8}.get(name, PANEL)

        def full(eng, name):
            b, k = fills[name]
            eng.wait_ge(psum_full[b], k + 1)

        def free(name):
            return psum_free[fills[name][0]]

        def drained(eng, name):
            b, k = fills[name]
            eng.wait_ge(psum_free[b], k + 1)

        def bank(name):
            return ps[fills[name][0]]

        agenda = {l: [] for l in range(2 * DEPTH)}
        normed_last = {}

        vec_dmas = []
        for name, rows in VEC_ROWS:
            src = a[name]
            wide64 = name in DUPLICATED
            src = src.rearrange(" ".join("abcd"[:len(src.shape)]) + " -> (" + " ".join("abcd"[:len(src.shape)]) + ")")
            src = src.rearrange("(r w) -> r w", w=64 if wide64 else P)
            done_rows = 0
            while done_rows < rows:
                at = VEC_AT[name] + done_rows
                n = min(rows - done_rows, P - at % P)
                for c0 in ((0, 64) if wide64 else (0,)):
                    vec_dmas.append((at // P, at % P, n, c0, c0 + (64 if wide64 else P),
                                     src[done_rows:done_rows + n, :]))
                done_rows += n
        N_VEC_DMAS = len(vec_dmas)

        pool_vec_landed = sem("vectors_landed_by_pool")
        const_landed, masks_landed = sem("const_landed"), sem("level_masks_landed")
        x_landed, p_landed, vec_landed = sem("x_landed"), sem("p_landed"), sem("vec_landed")
        w2_landed, bd_landed, sgu_landed = sem("cmp_w2_landed"), sem("lru_weights_landed"), sem("sgu_landed")
        bias_landed, bt_landed = sem("forget_bias_landed"), sem("sgu_bias_landed")
        eps_ready, bd_zeroed = sem("eps_ready"), sem("lru_weights_zeroed")
        sq_ready = sem("squares_ready")
        rinv_ready = sem("rinv_ready")
        xf_ready, xh_ready = sem("normed_f32_ready"), sem("normed_high_ready")
        xn_ready = sem("normed_ready")
        yf_ready, yh_ready = sem("mixed_f32_ready"), sem("mixed_high_ready")
        gf_ready, gh_ready = sem("ffn_hidden_f32_ready"), sem("ffn_hidden_high_ready")
        h_ready = sem("residual_ready")
        small_ready = sem("setup_vectors_ready")
        hg_ready = sem("hg_keys_ready")
        level_ready = sem("hg_level_ready")
        qsq_ready, ksq_ready = sem("q_squares_ready"), sem("k_squares_ready")
        kcsq_ready, osq_ready = sem("cmp_k_squares_ready"), sem("hg_o_squares_ready")
        q_rinv_ready, k_rinv_ready = sem("q_rinv_ready"), sem("k_rinv_ready")
        kc_rinv_ready, o_rinv_ready = sem("cmp_k_rinv_ready"), sem("hg_o_rinv_ready")
        rope_ready, k_rope_ready = sem("q_rope_terms_ready"), sem("k_rope_terms_ready")
        blocks_ready = sem("cmp_blocks_ready")
        gates_ready = sem("gates_ready")
        hid_exp_ready, hidden_ready = sem("cmp_hidden_exp_ready"), sem("cmp_hidden_ready")
        kc_ready = sem("cmp_k_ready")
        cmp_shift_ready, cmp_exp_ready, cp_ready = (sem("cmp_shifted_ready"), sem("cmp_exp_ready"),
                                                    sem("cmp_probs_ready"))
        nmax_ready = sem("neg_max_ready")
        p_ready = sem("probs_ready")
        sig_ready = sem("gate_sigmoids_ready")
        conv_ready = sem("conv_first_tap_ready")
        act_part = sem("scalar_part_ready")
        dve_part = sem("vector_part_ready")
        forget_ready, sgu_ready, y_ready = sem("forget_ready"), sem("sgu_ready"), sem("mixed_ready")
        taps_ready, first_back_done = sem("ffn_first_taps_ready"), sem("ffn_second_taps_done")
        silu_ready, act_ready = sem("ffn_silu_ready"), sem("ffn_hidden_ready")
        down_done, half_done = sem("ffn_down_done"), sem("half_by_token_done")
        out_stored = sem("out_stored")
        dve_step, act_step = sem("vector_step"), sem("scalar_step")
        BF = sb("forget_bias", 1)
        glu = [v3(t, 4) for t in (SG, HZ)]
        ones, head_ones = const("ones"), const("head_ones")
        ffn_base = {}
        GH, GL = sb("ffn_hidden_high", 1024, F32R), sb("ffn_hidden_low", 1024, F32R)
        hidden = [v3(VH[:, par * 512:(par + 1) * 512], 2) for par in range(2)]
        gh3, gl3 = ([v3(t[:, par * 512:(par + 1) * 512], 2) for par in range(2)] for t in (GH, GL))

        block = ctx.enter_context(nc.Block())

        @block.tensor
        def _(pe):
            last_done = [None]

            def begin(name, b):
                k = bank_fills[b]
                bank_fills[b] += 1
                fills[name] = (b, k)
                if k > 0:
                    pe.wait_ge(psum_free[b], k)
                return ps[b]

            def done(name, ins):
                order_of[name] = len(order_of)
                ins.then_inc(psum_full[fills[name][0]], 1)
                last_done[0] = name

            next_split = [SLOTS]

            def release(key):
                b, k = fills[last_done[0]]
                freed(key, (psum_full[b], k + 1), order_of[last_done[0]])

            def freed(key, when, place):
                panel_free[key] = when
                while next_split[0] < len(SPLIT_KEYS):
                    q = next_split[0]
                    n = LOAD_NO[SPLIT_KEYS[q]]
                    before, loaded_before = SPLIT_KEYS[q - SLOTS], LOADS[n - SLOTS][0]
                    if before not in panel_free:
                        break
                    if loaded_before not in SPLIT_NO and loaded_before not in panel_free:
                        break
                    split_from[q] = place
                    next_split[0] += 1

            def landed(key):
                n = LOAD_NO[key]
                pe.wait_ge(panel_landed[n % SLOTS], 16 * (n // SLOTS + 1))

            def split(key):
                pe.wait_ge(low_ready, SPLIT_NO[key] + 1)

            def raw_panel(key, nk=ND, n=512):
                return raw[LOAD_NO[key] % SLOTS][:, 0:nk * n].rearrange("p (k n) -> p k n", k=nk)

            def parts(key, nk=ND, n=256):
                s = SPLIT_NO[key] % SLOTS
                return [t[s][:, 0:nk * n].rearrange("p (k n) -> p k n", k=nk) for t in (high_slots, low_slots)]

            def product3(dst, w, x, start, stop, **kw):
                pe.matmul(dst, w[1], x[0], start=start, stop=False if not kw else True, **kw)
                pe.matmul(dst, w[0], x[1], start=False, stop=False if not kw else True, **kw)
                return pe.matmul(dst, w[0], x[0], start=False, stop=stop, **kw)

            def chunk(dst, w, col, mixed=None):
                for k in range(ND):
                    if mixed is not None:
                        pe.wait_ge(y_ready, 4 * mixed + k // 2 + 1)
                    ins = product3(dst, [t[:, k, col:col + P] for t in w], (xh3[:, k, :], xl3[:, k, :]),
                                   k == 0, k == ND - 1)
                return ins

            def small_chunk(dst, w3, col, x3, nk=ND, m=P):
                for k in range(nk):
                    ins = pe.matmul(dst, w3[:, k, col:col + m], x3[:, k, :], start=(k == 0), stop=(k == nk - 1))
                return ins

            def by_token(dst, w, col, n, tile):
                t = slice(tile * P, (tile + 1) * P)
                for k in range(ND):
                    ins = product3(dst, (xh3[:, k, t], xl3[:, k, t]), [part[:, k, col:col + n] for part in w],
                                   k == 0, k == ND - 1)
                return ins

            def two_chunks(name, b, key, mixed=None):
                begin(name, b)
                split(key)
                for j in range(2):
                    ins = chunk(ps[b][:, j * T:(j + 1) * T], parts(key), j * P, mixed if j == 0 else None)
                done(name, ins)
                release(key)

            def first_two(names, b, keys, nidx):
                for i in range(2):
                    if names:
                        begin(names[i], b[i])
                    split(keys[i])
                for k in range(ND):
                    pe.wait_ge(xn_ready, 8 * nidx + k + 1)
                    for i in range(2):
                        product3(ps[b[i]][:, 0:T], [t[:, k, 0:P] for t in parts(keys[i])],
                                 (xh3[:, k, :], xl3[:, k, :]), k == 0, k == ND - 1)
                for i in range(2):
                    ins = chunk(ps[b[i]][:, T:2 * T], parts(keys[i]), P)
                    if names:
                        done(names[i], ins)
                        release(keys[i])
                    else:
                        ins.then_inc(psum_full[b[i]], 1)

            def tokens(names, b, keys):
                for n in range(NT):
                    begin(names[n], b + n)
                for h, key in enumerate(keys):
                    split(key)
                    for n in range(NT):
                        ins = by_token(ps[b + n][:, h * T:(h + 1) * T], parts(key), 0, T, n)
                        if h == 1:
                            done(names[n], ins)
                    if h == 0:
                        ins.then_inc(half_done, 1)
                        halves[0] += 1
                        freed(key, (half_done, halves[0]), len(order_of) - 1)
                release(keys[1])

            halves = [0]

            def norm_sum(nidx, b=0, quarters=range(4)):
                for g in quarters:
                    if g == 0:
                        begin(f"ms{nidx}", b)
                    pe.wait_ge(sq_ready, 4 * nidx + g + 1)
                    for c in (2 * g, 2 * g + 1):
                        ins = pe.matmul(ps[b][:, 0:T], ones, sq3[:, c, :], start=(c == 0), stop=(c == ND - 1))
                    if g == 3:
                        done(f"ms{nidx}", ins)

            def product(name, b, n, lhs, rhs):
                begin(name, b)
                done(name, pe.matmul(ps[b][:, 0:n], lhs, rhs, start=True, stop=True))

            pe.wait_ge(const_landed, 16)
            pe.wait_ge(x_landed, 32)
            for g in range(4):
                begin(f"x{g}", g)
                for j in range(4):
                    c, n = 2 * g + j // 2, j % 2
                    ins = pe.transpose(ps[g][:, j * P:(j + 1) * P], xt[:, n, c * P:(c + 1) * P], ident)
                done(f"x{g}", ins)
            def scores(tag, u, q, keys, forget=None):
                begin(f"{tag}Y{u}", 5)
                begin(f"{tag}X{u}", 3 + u % 2)
                for n, b, x in ((0, 5, "Y"), (1, 3 + u % 2, "X")):
                    w = (n + 1) * P
                    o = ps[b][:, 0:2 * w].rearrange("p (r s) -> p r s", r=2)
                    pe.matmul(o, q[:, n * P:(n + 1) * P], keys[:, :, 0:w], start=True, stop=True)
                    if forget is not None:
                        pe.matmul(o, ones[0:8, :], forget[:, :, 0:w], start=False, stop=True,
                                  skip_group_check=True)
                    ins = pe.matmul(o[:, :, n * P:w], IDB[:, :], NGB[:, :].unsqueeze(1).to_broadcast([P, 2, P]),
                                    start=False, stop=True, skip_group_check=True)
                    done(f"{tag}{x}{u}", ins)

            def turn(tag, u, pidx):
                bb = pidx % 2
                pe.wait_ge(p_ready, pidx + 1)
                begin(f"{tag}A{u}", 6)
                for r in range(2):
                    pe.transpose(ps[6][:, r * T:r * T + P], probs[bb][0][:, r, :], ident)
                    ins = pe.transpose(ps[6][:, r * T + P:(r + 1) * T], probs[bb][1][:, r, 0:P], ident)
                done(f"{tag}A{u}", ins)
                begin(f"{tag}B{u}", 7)
                for r in range(2):
                    ins = pe.transpose(ps[7][:, r * P:(r + 1) * P], probs[bb][1][:, r, P:T], ident)
                done(f"{tag}B{u}", ins)

            def values(tag, u, pidx, vals, o, start, close=None):
                bb = pidx % 2
                drained(pe, f"{tag}A{u}")
                drained(pe, f"{tag}B{u}")
                for r in range(2):
                    pe.matmul(o[64 * r:64 * r + 64, :], vals(0, r), pt_lo[bb][:, r, :],
                              start=start, stop=True, skip_group_check=True)
                    ins = pe.matmul(o[64 * r:64 * r + 64, P:T], vals(1, r), pt_hi[bb][:, r, :],
                                    start=False, stop=True, skip_group_check=True)
                if close:
                    done(close, ins)

            def output(tag, l, b):
                for g in range(4):
                    two_chunks(f"{tag}{g}", 3 + g, (f"wo{g}", l), mixed=l if g == 0 else None)
                    if g > 0:
                        norm_sum(nidx, b, (g - 1,))

            norm_sum(0)
            by_pool = len(vec_dmas[2::3])
            pe.wait_ge(vec_landed, 16 * (N_VEC_DMAS - by_pool))
            pe.wait_ge(pool_vec_landed, 16 * by_pool)
            for g in range((NVT + 3) // 4):
                begin(f"vec{g}", 4 + g)
                for j in range(min(4, NVT - 4 * g)):
                    r = min(P, NVEC - (4 * g + j) * P)
                    ins = pe.transpose(ps[4 + g][:, j * P:j * P + r], vrows[0:r, 4 * g + j, :], ident[0:r, 0:r])
                done(f"vec{g}", ins)

            def noting(l):
                return lambda step: agenda[l].append((len(order_of) - 1, *step))

            nidx, pidx = 0, 0
            for l in range(DEPTH):
                todo = noting(l)
                if l > 0:
                    norm_sum(nidx)
                first_two([f"hf{g}_{l}" for g in range(2)], (1, 2), [(f"hf{g}", l) for g in range(2)], nidx)
                for g in range(2):
                    two_chunks(f"hq{g}_{l}", 3 + g, (f"hq{g}", l))
                tokens([f"hi{n}_{l}" for n in range(NT)], 5, [(f"hi{h}", l) for h in range(2)])
                if l == 0:
                    pe.wait_ge(p_landed, 16)
                    for m in range(DEPTH):
                        begin(f"p{m}", 1 + m)
                        for k in range(2):
                            for n in range(NT):
                                ins = pe.transpose(ps[1 + m][:, k * T + n * P:k * T + (n + 1) * P],
                                                   ptok[:, m * NT + n, k * P:(k + 1) * P], ident)
                        done(f"p{m}", ins)

                def level(n, g):
                    if n == 0:
                        pe.wait_ge(hg_ready, l + 1)
                        drained(pe, f"hq{g}_{l}")
                    else:
                        pe.wait_ge(level_ready, 16 * l + 2 * (n - 1) + g + 1)
                    b = (7, 0)[g]
                    begin(f"lv{n}_{g}_{l}", b)
                    for j in range(4):
                        s = (2 * g + j // 2) * T + (j % 2) * P
                        ins = pe.matmul(ps[b][:, j * P:(j + 1) * P], KQ[:, s:s + P], QP[:, s:s + P],
                                        start=True, stop=True)
                    done(f"lv{n}_{g}_{l}", ins)
                    todo(("level", n, g))

                gate_chunks = [(name, g, j) for name in ("hgo", "hz", "nz") for g in range(2) for j in range(2)]

                def gate_chunk():
                    if not gate_chunks:
                        return
                    name, g, j = gate_chunks.pop(0)
                    key = (f"{name}{g}", l)
                    b = 1 if key[0] == "hgo0" else 0
                    if j == 0:
                        begin(f"{name}{g}_{l}", b)
                        split(key)
                    ins = chunk(ps[b][:, j * T:(j + 1) * T], parts(key), j * P)
                    if j == 1:
                        done(f"{name}{g}_{l}", ins)
                        release(key)
                        todo(("copy", f"{name}{g}"))

                levels = [(n, g) for n in range(NLVL) for g in range(2)]

                def some(k):
                    for _ in range(min(k, len(levels))):
                        level(*levels.pop(0))

                some(2)
                for g in range(2):
                    key = (f"nq{g}", l)
                    begin(f"nq{g}_{l}", 1 + g)
                    split(key)
                    for j in range(2):
                        ins = chunk(ps[1 + g][:, j * T:(j + 1) * T], parts(key), j * P)
                        if j == 0:
                            some(1)
                    done(f"nq{g}_{l}", ins)
                    release(key)
                    todo(("copy", f"nq{g}"))
                    some(1)
                begin(f"kcvc_{l}", 3)
                split(("kv0", l))
                for j in range(2):
                    ins = chunk(ps[3][:, j * T:(j + 1) * T], parts(("kv0", l)), j * P)
                    if j == 0:
                        some(1)
                done(f"kcvc_{l}", ins)
                release(("kv0", l))
                todo(("blocks",))
                some(1)
                begin(f"ks_{l}", 4)
                split(("kv1", l))
                chunk(ps[4][:, 0:T], parts(("kv1", l)), 0)
                some(1)
                begin(f"vs_{l}", 5)
                for n in range(NT):
                    ins = by_token(ps[5][:, n * P:(n + 1) * P], parts(("kv1", l)), P, P, n)
                done(f"vs_{l}", ins)
                release(("kv1", l))
                todo(("copy", "vs"))
                some(1)
                split(("kw0", l))
                done(f"ks_{l}", chunk(ps[4][:, T:2 * T], parts(("kw0", l), n=P), 0))
                release(("kw0", l))
                todo(("k_square",))
                some(1)
                begin(f"vw_{l}", 6)
                split(("kw1", l))
                for n in range(NT):
                    ins = by_token(ps[6][:, n * VG:(n + 1) * VG], parts(("kw1", l), n=VG), 0, VG, n)
                done(f"vw_{l}", ins)
                release(("kw1", l))
                todo(("gates",))
                pe.wait_ge(qsq_ready, l + 1)
                for j in range(2):
                    product(f"qss{j}_{l}", 1 + j, 512, head_ones, SQ[:, j * 512:(j + 1) * 512])
                todo(("q_norm",))
                some(1)
                pe.wait_ge(ksq_ready, l + 1)
                product(f"kss_{l}", 4, 512, head_ones, UK[:, 0:512])
                todo(("k_norm",))
                some(1)
                pe.wait_ge(blocks_ready, l + 1)
                begin(f"hid_{l}", 3)
                for kv in range(2):
                    landed((f"cmp{kv}", l))
                    w1 = raw_panel((f"cmp{kv}", l), 16, P)
                    for jj in range(16):
                        ins = pe.matmul(ps[3][:, kv * 32:(kv + 1) * 32], w1[:, jj, :], M2[:, kv, jj, :, :],
                                        start=(jj == 0), stop=(jj == 15))
                done(f"hid_{l}", ins)
                release(("cmp0", l))
                release(("cmp1", l))
                todo(("hidden",))
                some(1)
                pe.wait_ge(rope_ready, l + 1)
                for j in range(2):
                    begin(f"qr{j}_{l}", 1 + j)
                    pe.matmul(ps[1 + j][:, :], ident, UW[:, j * 512:(j + 1) * 512], start=True, stop=False)
                    done(f"qr{j}_{l}", pe.matmul(ps[1 + j][:, :], const("rot"),
                                                 UW[:, 1024 + j * 512:1024 + (j + 1) * 512],
                                                 start=False, stop=True))
                    todo(("copy", f"qr{j}"))
                some(1)
                pe.wait_ge(k_rope_ready, l + 1)
                begin(f"kr_{l}", 4)
                pe.matmul(ps[4][:, :], ident, UK[:, 0:512], start=True, stop=False)
                done(f"kr_{l}", pe.matmul(ps[4][:, :], const("rot"), UK[:, 512:1024], start=False, stop=True))
                todo(("k_pad",))
                gate_chunk()
                some(16)
                gate_chunk()
                pe.wait_ge(level_ready, 16 * l + 16)
                begin(f"cross_{l}", 7)
                for hd in range(4):
                    ins = pe.matmul(ps[7][:, hd * P:(hd + 1) * P], KQ[:, hd * T:hd * T + P],
                                    QP[:, hd * T + P:(hd + 1) * T], start=True, stop=True)
                done(f"cross_{l}", ins)
                todo(("cross",))
                pe.wait_ge(w2_landed, 48 * (l + 1))
                pe.wait_ge(hidden_ready, l + 1)
                product(f"kc_{l}", 0, 32, W2[:, 0:P], HID[:, 0:32])
                product(f"vc_{l}", 3, 64, HIDV[:, :], W2[:, P:P + 64])
                todo(("cmp_kv",))
                drained(pe, f"hi1_{l}")
                drained(pe, f"cross_{l}")
                drained(pe, f"lv{NLVL - 1}_0_{l}")
                drained(pe, f"lv{NLVL - 1}_1_{l}")
                for g in range(2):
                    begin(f"o{g}_{l}", 5 + g)
                    for j in range(2):
                        hd = 2 * g + j
                        v = [vh[:, n, hd * P:(hd + 1) * P] for n in range(NT)]
                        pe.matmul(ps[5 + g][:, j * T:j * T + P], v[0], ad[:, hd, 0, :], start=True, stop=True)
                        pe.matmul(ps[5 + g][:, j * T + P:(j + 1) * T], v[0], ac[:, hd, :], start=True, stop=False)
                        ins = pe.matmul(ps[5 + g][:, j * T + P:(j + 1) * T], v[1], ad[:, hd, 1, :],
                                        start=False, stop=True)
                    done(f"o{g}_{l}", ins)
                todo(("o_square",))
                pe.wait_ge(kcsq_ready, l + 1)
                product(f"kcss_{l}", 0, 32, head_ones, KC[:, 32:64])
                todo(("kc_norm",))
                gate_chunk()
                pe.wait_ge(osq_ready, l + 1)
                for g in range(2):
                    product(f"oss{g}_{l}", 5 + g, 512, ones, SQ[:, g * 512:(g + 1) * 512])
                todo(("o_norm",))
                pe.wait_ge(kc_ready, l + 1)
                begin(f"cs_{l}", 3)
                for n in range(NT):
                    for j in range(4):
                        s = n * P + j * 32
                        ins = pe.matmul(ps[3][:, s:s + 32].rearrange("p (r c) -> p r c", r=2),
                                        QN[:, j * T + n * P:j * T + (n + 1) * P],
                                        v3(KCZ, 2)[:, :, (j // 2) * 16:(j // 2) * 16 + 16], start=True, stop=True)
                done(f"cs_{l}", ins)
                todo(("cmp_softmax",))
                gate_chunk()
                drained(pe, f"qr1_{l}")
                drained(pe, f"kr_{l}")
                drained(pe, f"vs_{l}")
                pe.wait_ge(gates_ready, l + 1)

                def unit(u):
                    kind, j = u // 4, u % 4
                    scores(f"n{l}", u, QR[:, j * T:(j + 1) * T], kz[:, kind, :, j // 2, :])
                    todo(("scores", u))

                unit(0)
                pe.wait_ge(cp_ready, l + 1)
                begin(f"ct_{l}", 7)
                for n in range(NT):
                    ins = pe.transpose(ps[7][:, n * P:(n + 1) * P], SC[:, n * P:(n + 1) * P], ident)
                done(f"ct_{l}", ins)
                todo(("copy", "ct"))
                gate_chunk()
                drained(pe, f"ct_{l}")
                drained(pe, f"vc_{l}")
                begin(f"on0_{l}", 1)
                begin(f"on1_{l}", 2)
                for j in range(4):
                    pe.matmul(ps[1 + j // 2][:, (j % 2) * T:(j % 2 + 1) * T], VCB[:, j * P:(j + 1) * P], PCT[:, :],
                              start=(j % 2 == 0), stop=True, skip_group_check=True)

                def weigh(u):
                    kind, j = u // 4, u % 4
                    values(f"n{l}", u, pidx + u, lambda n, r: vt[:, kind, n, (j // 2) * 64:(j // 2) * 64 + 64],
                           ps[1 + j // 2][:, (j % 2) * T:(j % 2 + 1) * T], False,
                           close={5: f"on0_{l}", 7: f"on1_{l}"}.get(u))

                for u in range(8):
                    todo(("normalise", u))
                    if u < 7:
                        unit(u + 1)
                    else:
                        todo(("mix",))
                    gate_chunk()
                    if u > 0:
                        weigh(u - 1)
                    turn(f"n{l}", u, pidx + u)
                    todo(("turned", u))
                    if u == 6:
                        todo(("sigmoids",))
                weigh(7)
                todo(("on",))
                pidx += 8
                normed_last[nidx] = f"nz1_{l}"
                nidx += 1
                output(f"wo_{l}_", l, 2)
                landed(("pp", l))
                for g in range(4):
                    b = (7, 0, 1, 3)[g]
                    if g == 2:
                        norm_sum(nidx, 2, (3,))
                    begin(f"pp{g}_{l}", b)
                    for j in range(2):
                        ins = small_chunk(ps[b][:, j * T:(j + 1) * T], raw_panel(("pp", l), 2, 1024),
                                          (2 * g + j) * P, ptr[:, l], nk=2)
                    done(f"pp{g}_{l}", ins)
                release(("pp", l))
                first_two([f"pg{g}_{l}" for g in range(2)], (4, 5), [(f"pg{g}", l) for g in range(2)], nidx)
                nidx += 1
                for g in (2, 3):
                    two_chunks(f"pg{g}_{l}", 4 + g, (f"pg{g}", l))
                normed_last[nidx - 1] = f"pg3_{l}"

            for l in range(DEPTH):
                L = DEPTH + l
                todo = noting(L)
                norm_sum(nidx, 0, (3,) if l > 0 else range(4))
                if l == 0:
                    def panels(*names):
                        for name, b in names:
                            for g in range(2):
                                two_chunks(f"{name}{g}", b + g, (f"{name}{g}", L))

                    first_two(["xa0", "xa1"], (1, 2), [("xa0", L), ("xa1", L)], nidx)
                    panels(("ga", 5))
                    pe.wait_ge(bd_landed, 64)
                    for name, w, b in (("lr", 0, (7, 0)), ("li", 512, (1, 2))):
                        for g in range(2):
                            drained(pe, f"xa{g}")
                            begin(f"{name}{g}", b[g])
                            for j in range(2):
                                c = 2 * g + j
                                ins = pe.matmul(ps[b[g]][:, j * T:(j + 1) * T], PB[:, w + c * P:w + (c + 1) * P],
                                                FG[:, c * T:(c + 1) * T], start=True, stop=True)
                            done(f"{name}{g}", ins)
                    panels(("cp", 3), ("vb", 5), ("bp", 1))
                    normed_last[nidx] = "bp1"
                else:
                    first_two(["fq0", "fq1"], (1, 2), [("fq0", L), ("fq1", L)], nidx)
                    for g in range(2):
                        two_chunks(f"fk{g}", 3 + g, (f"fk{g}", L))
                    landed(("ff", L))
                    begin("fl", 7)
                    done("fl", small_chunk(ps[7][0:8, 0:T], raw_panel(("ff", L), ND, 8), 0, xf3, m=8))
                    release(("ff", L))
                    tokens(["fv0", "fv1"], 5, [("fv0", L), ("fv1", L)])
                    pe.wait_ge(forget_ready, 1)
                    drained(pe, "fq1")
                    drained(pe, "fk1")
                    drained(pe, "fv1")

                    def unit(u):
                        scores("f", u, QR[:, u * T:(u + 1) * T], kz[:, u // 2, :, u % 2, :],
                               UW[0:8, :].rearrange("p (h t) -> p h t", h=8)[:, 2 * u:2 * u + 2, :])
                        todo(("scores", u))

                    def mix_tokens(g):
                        b = (0, 3)[g]
                        begin(f"sg{g}", b)
                        for j in range(2):
                            for n in range(NT):
                                for r in range(2):
                                    hd = 4 * g + 2 * j + r
                                    s = j * T + n * P
                                    ins = pe.matmul(ps[b][64 * r:64 * r + 64, s:s + P],
                                                    QN[:, n * 512 + hd * 64:n * 512 + (hd + 1) * 64],
                                                    AD[:, hd * P:(hd + 1) * P], start=True, stop=True)
                        done(f"sg{g}", ins)
                        todo((f"sg{g}",))

                    def weigh(u):
                        if u % 2 == 0:
                            begin(f"fo{u // 2}", 1 + u // 2)
                        values("f", u, pidx + u, lambda n, r: vh[:, n, (2 * u + r) * 64:(2 * u + r + 1) * 64],
                               ps[1 + u // 2][:, (u % 2) * T:(u % 2 + 1) * T], True,
                               close=f"fo{u // 2}" if u % 2 == 1 else None)

                    unit(0)
                    for u in range(4):
                        todo(("normalise", u))
                        if u < 3:
                            unit(u + 1)
                        if u == 0:
                            tokens(["zg0", "zg1"], 1, [("zg0", L), ("zg1", L)])
                            pe.wait_ge(sgu_landed, 16)
                            for g in range(2):
                                begin(f"wt{g}", (7, 0)[g])
                                for j in range(4):
                                    hd = 4 * g + j
                                    ins = pe.transpose(ps[(7, 0)[g]][:, j * P:(j + 1) * P],
                                                       PT[:, hd * P:(hd + 1) * P], ident)
                                done(f"wt{g}", ins)
                            todo(("wt",))
                            todo(("zg",))
                        elif u < 3:
                            two_chunks(f"zu{u - 1}", 0, (f"zu{u - 1}", L))
                            todo(("zu", u - 1))
                        else:
                            pe.wait_ge(sgu_ready, 1)
                            drained(pe, "wt1")
                            mix_tokens(0)
                            mix_tokens(1)
                        if u > 0:
                            weigh(u - 1)
                        turn("f", u, pidx + u)
                        todo(("turned", u))
                        if u == 0:
                            todo(("zg_norm",))
                    weigh(3)
                    normed_last[nidx] = "zu1"
                nidx += 1
                output(f"wm_{l}_", L, 0)

                norm_sum(nidx, 0, (3,))
                for g in range(4):
                    begin(f"down{g}_{l}", 4 + g)
                    pe.matmul(ps[4 + g][:, :], ZR[:, :], CN[:, 0:512], start=True, stop=True,
                              skip_group_check=True)
                ffn_base[l] = up0 = [bank_fills[b] for b in range(4)]
                q0 = SPLIT_NO[("gate", l, 0)]

                def up(par, i):
                    for half in range(2):
                        b = 2 * par + half
                        pe.wait_ge(psum_free[b], i + up0[b])
                        pe.wait_ge(low_ready, i * 6 + (q0 + 3 * par + half))
                        slot = (q0 + FFN_SLOT[half]) % SLOTS
                        w = [v3(t[slot], ND) for t in (high_slots, low_slots)]
                        for j in range(2):
                            ins = chunk(ps[b][:, j * T:(j + 1) * T], w, j * P)
                        ins.then_inc(psum_full[b], 1)

                def down(par, i, close=False):
                    slot = (q0 + FFN_SLOT[2]) % SLOTS
                    if close:
                        slot = (q0 + 2 + 3 * (FF_ROUNDS - 1)) % SLOTS
                        pe.wait_ge(low_ready, q0 + 3 * FF_ROUNDS)
                    else:
                        pe.wait_ge(low_ready, i * 6 + (q0 + 3 * par + 5))
                    pe.wait_ge(act_ready, 2 * i + (par + 1 + FF_ROUNDS * l))
                    w = [v3(t[slot], 2) for t in (high_slots, low_slots)]
                    for g in range(4):
                        for j in range(2):
                            c = slice((2 * g + j) * P, (2 * g + j + 1) * P)
                            for k in range(2):
                                ins = product3(ps[4 + g][:, j * T:(j + 1) * T], [w[i][:, k, c] for i in range(2)],
                                               (gh3[par][:, k, :], gl3[par][:, k, :]), False, True,
                                               skip_group_check=True)
                        if close:
                            done(f"down{g}_{l}", ins)
                            if g == 3:
                                release(("down", l, FF_ROUNDS - 1))
                            if g > 1:
                                norm_sum(nidx + 1, 0, (g - 2,))
                    if not close:
                        ins.then_inc(down_done, 1)

                for b in range(2):
                    pe.wait_ge(psum_free[b], up0[b])
                first_two(None, (0, 1), [("gate", l, 0), ("value", l, 0)], nidx)
                up(1, 0)
                down(0, 0)
                with pe.Fori(1, FF_ROUNDS // 2) as i:
                    up(0, i)
                    down(1, i - 1)
                    up(1, i)
                    down(0, i)
                up(0, FF_ROUNDS // 2)
                for b in range(4):
                    bank_fills[b] += FF_ROUNDS // 2 + (b < 2)
                last_up = f"ffn_up{l}"
                fills[last_up] = (1, bank_fills[1] - 1)
                order_of[last_up] = len(order_of)
                for r in range(FF_ROUNDS):
                    for b, kind in ((0, "gate"), (1, "value")):
                        freed((kind, l, r), (psum_full[b], bank_fills[b]), order_of[last_up])
                down(1, FF_ROUNDS // 2 - 1)
                for r in range(FF_ROUNDS - 1):
                    freed(("down", l, r), (down_done, (FF_ROUNDS - 1) * (l + 1)), order_of[last_up])
                down(0, FF_ROUNDS // 2, close=True)
                normed_last[nidx] = last_up
                nidx += 1
                norm_sum(nidx, 0, (2,))

            norm_sum(nidx, 0, (3,))
            for g in range(4):
                n, c0 = g % 2, 4 * (g // 2)
                begin(f"out{g}", 1 + g)
                for j in range(4):
                    if n == 0:
                        pe.wait_ge(xf_ready, 8 * nidx + c0 + j + 1)
                    ins = pe.transpose(ps[1 + g][:, j * P:(j + 1) * P], xf3[:, c0 + j, n * P:(n + 1) * P], ident)
                done(f"out{g}", ins)

        @block.scalar
        def _(act):
            steps = [0]

            def link(ins):
                steps[0] += 1
                ins.then_inc(act_step, 1)
                act.wait_ge(act_step, steps[0])

            def f(dst, src, func, **kw):
                return nc.scalar.activation(dst, src, func, **kw)

            def copy_out(name, dst, src):
                full(act, name)
                nc.scalar.copy(dst, src).then_inc(free(name), 1)

            def high_part(n, slot, size=PANEL, when=None, landed=None):
                if landed is None:
                    landed = 16 * (n // SLOTS + 1)
                act.wait_ge(panel_landed[n % SLOTS], landed)
                if when is not None:
                    act.wait_ge(*when)
                nc.scalar.copy(high_slots[slot][:, 0:size], raw[n % SLOTS][:, 0:size]).then_inc(high_ready, 1)

            next_high = [0]

            def split_high(place, most=len(SPLIT_KEYS)):
                while next_high[0] < most:
                    q = next_high[0]
                    key = SPLIT_KEYS[q]
                    if q >= SLOTS and split_from.get(q, 1 << 30) > place or len(key) == 3 and \
                            key not in (("gate", key[1], 0), ("value", key[1], 0)):
                        break
                    n = LOAD_NO[key]
                    high_part(n, q % SLOTS, panel_size(n), panel_free[SPLIT_KEYS[q - SLOTS]] if q >= SLOTS else None)
                    high_from[q] = place
                    next_high[0] += 1

            def split_after(name):
                split_high(order_of[name])

            def input_high(nidx):
                for c in range(ND):
                    act.wait_ge(xf_ready, 8 * nidx + c + 1)
                    nc.scalar.copy(xh3[:, c, :], xf3[:, c, :]).then_inc(xh_ready, 1)

            def mixed_high(m, names, quarters=range(4)):
                for g in quarters:
                    if g < 2:
                        act.wait_ge(yf_ready, 2 * m + g + 1)
                    else:
                        drained(act, names[g - 2])
                    nc.scalar.copy(XH[:, g * 512:(g + 1) * 512], Y[:, g * 512:(g + 1) * 512]).then_inc(yh_ready, 1)

            def log_exp():
                nc.scalar.preload_act_table_set(LOG_EXP)

            def squares(nidx, ready, between=None, quarters=range(4)):
                if 3 in quarters:
                    log_exp()
                for g in quarters:
                    ready(g)
                    f(sq3[:, 2 * g:2 * g + 2, :], h3[:, 2 * g:2 * g + 2, :], ACT.Square).then_inc(sq_ready, 1)
                    if between and g < 3:
                        between(g)

            def norm(nidx):
                full(act, f"ms{nidx}")
                f(RINV[:, :], bank(f"ms{nidx}")[:, 0:T], ACT.Ln, bias=EPSC[:, 0:1],
                  scale=1.0 / D).then_inc(free(f"ms{nidx}"), 1)
                drained(act, f"ms{nidx}")
                f(RINV[:, :], RINV[:, :], ACT.Exp, scale=-0.5).then_inc(rinv_ready, 1)
                if nidx < 4 * DEPTH:
                    input_high(nidx)

            def head_rinv(names, dst, width, n):
                for j, name in enumerate(names):
                    full(act, name)
                    w = n // len(names)
                    f(dst[:, j * w:(j + 1) * w], bank(name)[:, 0:w], ACT.Ln, bias=EPSC[:, 0:1],
                      scale=1.0 / width).then_inc(free(name), 1)
                drained(act, names[-1])
                return f(dst, dst, ACT.Exp, scale=-0.5)

            def exps(tag, u, pidx):
                bb = pidx % 2
                act.wait_ge(nmax_ready, pidx + 1)
                if pidx >= 2:
                    act.wait_ge(*turned[pidx - 2])
                for n, x in ((0, "Y"), (1, "X")):
                    s3 = bank(f"{tag}{x}{u}")[:, 0:2 * (n + 1) * P].rearrange("p (r s) -> p r s", r=2)
                    for r in range(2):
                        i = 2 * n + r
                        ins = f(probs[bb][n][:, r, :], s3[:, r, :], ACT.Exp, bias=NM[:, 4 * bb + i:4 * bb + i + 1],
                                accum_out=SM[:, 4 * bb + i:4 * bb + i + 1])
                    ins.then_inc(free(f"{tag}{x}{u}"), 1)

            def turned_copies(tag, u, pidx):
                bb = pidx % 2
                copy_out(f"{tag}A{u}", pt_lo[bb].rearrange("p r t -> p (r t)"), bank(f"{tag}A{u}")[:, :])
                copy_out(f"{tag}B{u}", pt_hi[bb].rearrange("p r t -> p (r t)"), bank(f"{tag}B{u}")[:, 0:T])
                b, k = fills[f"{tag}B{u}"]
                turned[pidx] = (psum_full[b], k + 1)

            act.dma_start(CN[:, :], a["const_table"]).then_inc(const_landed, 16)
            for tile, r, n, c0, c1, src in vec_dmas[0::3]:
                act.dma_start(vrows[r:r + n, tile, c0:c1], src).then_inc(vec_landed, 16)
            turned = {}
            act.wait_ge(eps_ready, 1)
            squares(0, lambda g: drained(act, f"x{g}"))
            split_high(-1, 2)
            for g in range((NVT + 3) // 4):
                n = min(512, NVEC - 512 * g)
                copy_out(f"vec{g}", VC[:, 512 * g:512 * g + n], bank(f"vec{g}")[:, 0:n])
            norm(0)
            split_high(-1)
            act.wait_ge(dve_part, 1)
            f(SPC[:, 8:20], SPC[:, 8:20], ACT.Exp).then_inc(act_part, 1)
            nidx, pidx = 0, 0
            for l in range(DEPTH):
                if l > 0:
                    squares(nidx, lambda g: act.wait_ge(h_ready, 4 * l + g - 3), quarters=(2, 3))
                    norm(nidx)
                    split_after(f"pg3_{l - 1}")
                nidx += 1
                for g in range(2):
                    full(act, f"hf{g}_{l}")
                    s = slice(g * 512, (g + 1) * 512)
                    f(FG[:, s], bank(f"hf{g}_{l}")[:, :], ACT.Sigmoid)
                    f(KQ[:, s], bank(f"hf{g}_{l}")[:, :], ACT.Sigmoid, scale=-1.0).then_inc(free(f"hf{g}_{l}"), 1)
                    split_after(f"hf{g}_{l}")
                for g in range(2):
                    copy_out(f"hq{g}_{l}", QP[:, g * 512:(g + 1) * 512], bank(f"hq{g}_{l}")[:, :])
                    split_after(f"hq{g}_{l}")
                for n in range(NT):
                    copy_out(f"hi{n}_{l}", vh[:, n, :], bank(f"hi{n}_{l}")[:, :])
                    split_after(f"hi{n}_{l}")
                if l == 0:
                    for m in range(DEPTH):
                        copy_out(f"p{m}", PTR[:, m * 512:(m + 1) * 512], bank(f"p{m}")[:, :])
                log_exp()
                dest = {"nq0": QN[:, 0:512], "nq1": QN[:, 512:1024], "qr0": QR[:, 0:512], "qr1": QR[:, 512:1024],
                        "vs": VT[:, 0:T], "ct": PCT[:, :], "hgo0": SG[:, 0:512], "hgo1": SG[:, 512:1024],
                        "hz0": HZ[:, 0:512], "hz1": HZ[:, 512:1024], "nz0": NZ[:, 0:512], "nz1": NZ[:, 512:1024]}
                held = False
                for place, step, *arg in agenda[l]:
                    if step == "copy":
                        name, dst = f"{arg[0]}_{l}", dest[arg[0]]
                        copy_out(name, dst, bank(name)[:, 0:dst.shape[1]])
                        if arg[0] == "nq1":
                            drained(act, name)
                            f(SQ[:, 0:1024], QN[:, :], ACT.Square).then_inc(qsq_ready, 1)
                    elif step == "blocks":
                        name = f"kcvc_{l}"
                        full(act, name)
                        src = v3(bank(name), 2)
                        for g in range(2):
                            s = src[64 * g:64 * g + 64]
                            nc.scalar.copy(K2[0:64, :, g, :], s)
                            ins = nc.scalar.copy(K2[64:128, :, g, 0:T - 1], s[:, :, 1:T])
                        ins.then_inc(free(name), 1)
                    elif step == "k_square":
                        name = f"ks_{l}"
                        copy_out(name, KN[:, :], bank(name)[:, :])
                        drained(act, name)
                        f(UK[:, 0:512], KN[:, :], ACT.Square).then_inc(ksq_ready, 1)
                    elif step == "gates":
                        name = f"vw_{l}"
                        full(act, name)
                        src = bank(name)[:, 0:NT * VG].rearrange("p (n w) -> p n w", n=NT)
                        nc.scalar.copy(vt[:, 1, :, :], src[:, :, 0:P])
                        f(gates, src[:, :, P:VG], ACT.Exp, scale=-1.0).then_inc(free(name), 1)
                    elif step == "q_norm":
                        head_rinv([f"qss{j}_{l}" for j in range(2)], HZ[:, :], 64, 1024).then_inc(q_rinv_ready, 1)
                    elif step == "k_norm":
                        head_rinv([f"kss_{l}"], UK[:, 512:1024], 64, 512).then_inc(k_rinv_ready, 1)
                    elif step == "hidden":
                        full(act, f"hid_{l}")
                        f(SS[:, 0:64], bank(f"hid_{l}")[:, 0:64], ACT.Exp, scale=-1.0).then_inc(hid_exp_ready, 1)
                    elif step == "k_pad":
                        name = f"kr_{l}"
                        full(act, name)
                        src = v3(bank(name), 2)
                        for g in range(2):
                            s = src[64 * g:64 * g + 64]
                            nc.scalar.copy(kz[0:64, :, 0, g, :], s)
                            ins = nc.scalar.copy(kz[64:128, :, 1, g, :], s)
                        ins.then_inc(free(name), 1)
                    elif step == "cross":
                        copy_out(f"cross_{l}", AC[:, :], bank(f"cross_{l}")[:, :])
                    elif step == "cmp_kv":
                        name = f"kc_{l}"
                        copy_out(name, KC[:, 0:32], bank(name)[:, 0:32])
                        drained(act, name)
                        f(KC[:, 32:64], KC[:, 0:32], ACT.Square).then_inc(kcsq_ready, 1)
                    elif step == "o_square":
                        for g in range(2):
                            copy_out(f"o{g}_{l}", QP[:, g * 512:(g + 1) * 512], bank(f"o{g}_{l}")[:, :])
                        drained(act, f"o1_{l}")
                        f(SQ[:, 0:1024], QP[:, :], ACT.Square).then_inc(osq_ready, 1)
                    elif step == "kc_norm":
                        head_rinv([f"kcss_{l}"], SS[:, 64:96], 64, 32).then_inc(kc_rinv_ready, 1)
                    elif step == "o_norm":
                        act.wait_ge(rope_ready, l + 1)
                        head_rinv([f"oss{g}_{l}" for g in range(2)], UK[:, :], P, 1024).then_inc(o_rinv_ready, 1)
                    elif step == "cmp_softmax":
                        act.wait_ge(cmp_shift_ready, l + 1)
                        f(SC[:, :], SC[:, :], ACT.Exp).then_inc(cmp_exp_ready, 1)
                    elif step == "scores":
                        exps(f"n{l}", arg[0], 8 * l + arg[0])
                    elif step == "turned":
                        turned_copies(f"n{l}", arg[0], 8 * l + arg[0])
                    elif step == "sigmoids":
                        drained(act, f"hz1_{l}")
                        for dst, src in ((FG, HZ), (SG, SG)):
                            f(dst[:, :], src[:, :], ACT.Sigmoid).then_inc(sig_ready, 1)
                    elif step == "on":
                        mixed_high(l, None, (0, 1))
                        drained(act, f"nz1_{l}")
                        f(VH[:, :], NZ[:, :], ACT.Sigmoid).then_inc(sig_ready, 1)
                        mixed_high(l, [f"on{g}_{l}" for g in range(2)], (2, 3))
                    held = (held or (step, *arg) == ("copy", "nz1")) and step != "on"
                    if not held:
                        split_high(place)
                squares(nidx, lambda g: drained(act, f"wo_{l}_{g}"), lambda g: split_after(f"wo_{l}_{g}"))

                def pp_out(g):
                    copy_out(f"pp{g}_{l}", PP[:, g * 512:(g + 1) * 512], bank(f"pp{g}_{l}")[:, :])

                pp_out(0)
                pp_out(1)
                norm(nidx)
                nidx += 1
                pp_out(2)
                pp_out(3)
                split_after(f"pp3_{l}")
                for g in range(4):
                    name = f"pg{g}_{l}"
                    full(act, name)
                    f(Y[:, g * 512:(g + 1) * 512], bank(name)[:, :], ACT.Sigmoid).then_inc(free(name), 1)
                    if g < 3:
                        split_after(name)
                    if g == 2:
                        squares(nidx, lambda g: act.wait_ge(h_ready, 4 * l + g + 1), quarters=(0, 1))

            pidx = 8 * DEPTH
            for l in range(DEPTH):
                if l == 0:
                    squares(nidx, lambda g: act.wait_ge(h_ready, 4 * DEPTH + g - 3), quarters=(2, 3))
                    norm(nidx)
                    split_after(f"pg3_{DEPTH - 1}")
                    nidx += 1

                    def first_tap(c, src, dst, w, bias):
                        return f(dst, src, ACT.Identity, scale=w, bias=bias)

                    for g in range(2):
                        full(act, f"xa{g}")
                        for j in range(2):
                            c = 2 * g + j
                            ins = first_tap(c, bank(f"xa{g}")[:, j * T:(j + 1) * T], FG[:, c * T:(c + 1) * T],
                                            vec("lru_conv_w_2", 12 + c), vec("lru_conv_b_2", c))
                        ins.then_inc(conv_ready, 1)
                        split_after(f"xa{g}")
                    for g in range(2):
                        full(act, f"ga{g}")
                        f(SG[:, g * 512:(g + 1) * 512], bank(f"ga{g}")[:, :],
                          ACT.Gelu_apprx_tanh).then_inc(free(f"ga{g}"), 1)
                        split_after(f"ga{g}")
                    for name, dst, bias in (("lr", HZ, "lru_ba_2"), ("li", NZ, "lru_bx_2")):
                        for g in range(2):
                            full(act, f"{name}{g}")
                            for j in range(2):
                                c = 2 * g + j
                                ins = f(dst[:, c * T:(c + 1) * T], bank(f"{name}{g}")[:, j * T:(j + 1) * T],
                                        ACT.Sigmoid, bias=vec(bias, c))
                            ins.then_inc(free(f"{name}{g}"), 1)
                    drained(act, "lr1")
                    act.wait_ge(small_ready, 1)
                    for c in range(4):
                        ins = f(QR[:, c * T:(c + 1) * T], HZ[:, c * T:(c + 1) * T], ACT.Tanh,
                                scale=SPC[:, 4 + c:5 + c])
                    ins.then_inc(act_part, 1)
                    for c in range(4):
                        ins = f(QN[:, c * T:(c + 1) * T], HZ[:, c * T:(c + 1) * T], ACT.Exp, scale=SPC[:, c:c + 1])
                    ins.then_inc(act_part, 1)
                    act.wait_ge(dve_part, 2)
                    f(QR[:, :], QR[:, :], ACT.Sqrt).then_inc(act_part, 1)
                    for g in range(2):
                        copy_out(f"cp{g}", KQ[:, g * 512:(g + 1) * 512], bank(f"cp{g}")[:, :])
                        split_after(f"cp{g}")
                    for g in range(2):
                        full(act, f"vb{g}")
                        split_after(f"vb{g}")
                        drained(act, f"vb{g}")
                        for j in range(2):
                            c = 2 * g + j
                            ins = first_tap(c, QP[:, c * T:(c + 1) * T], AD[:, c * T:(c + 1) * T],
                                            vec("sconv_w_2", 8 + c), vec("sconv_b_2", c))
                        ins.then_inc(conv_ready, 1)
                    full(act, "bp0")
                    split_after("bp0")
                    full(act, "bp1")
                    mixed_high(DEPTH, ["bp0", "bp1"])
                    split_after("bp1")
                else:
                    squares(nidx, lambda g: drained(act, f"down{g}_0"))
                    norm(nidx)
                    split_after("down3_0")
                    nidx += 1
                    for g in range(2):
                        full(act, f"fq{g}")
                        nc.scalar.mul(QR[:, g * 512:(g + 1) * 512], bank(f"fq{g}")[:, :],
                                      0.125).then_inc(free(f"fq{g}"), 1)
                        split_after(f"fq{g}")
                    for g in range(2):
                        full(act, f"fk{g}")
                        src = v3(bank(f"fk{g}"), 2)
                        nc.scalar.copy(kz[0:64, g, 0, :, :], src[0:64])
                        nc.scalar.copy(kz[64:128, g, 1, :, :], src[64:128]).then_inc(free(f"fk{g}"), 1)
                        split_after(f"fk{g}")
                    act.wait_ge(dve_part, 3)
                    link(f(SS[0:8, :], SS[0:8, :], ACT.Exp))
                    f(SS[0:8, :], SS[0:8, :], ACT.Ln, bias=EPSC[0:8, 1:2]).then_inc(act_part, 1)
                    for n in range(NT):
                        copy_out(f"fv{n}", vh[:, n, :], bank(f"fv{n}")[:, :])
                        split_after(f"fv{n}")
                    for place, step, *arg in agenda[DEPTH + l]:
                        if step == "scores":
                            exps("f", arg[0], pidx + arg[0])
                        elif step == "turned":
                            turned_copies("f", arg[0], pidx + arg[0])
                        elif step == "zg":
                            for n in range(NT):
                                full(act, f"zg{n}")
                                f(QN[:, n * 512:(n + 1) * 512], bank(f"zg{n}")[:, :],
                                  ACT.Gelu_apprx_tanh).then_inc(free(f"zg{n}"), 1)
                            drained(act, "zg1")
                            f(NZ[:, :], QN[:, :], ACT.Square).then_inc(act_part, 1)
                            log_exp()
                        elif step == "zg_norm":
                            act.wait_ge(dve_part, 4)
                            link(f(NT16[:, :], NT16[:, :], ACT.Ln, bias=EPSC[:, 0:1], scale=1.0 / 64))
                            f(NT16[:, :], NT16[:, :], ACT.Exp, scale=-0.5).then_inc(act_part, 1)
                        elif step == "zu":
                            g = arg[0]
                            copy_out(f"zu{g}", SG[:, g * 512:(g + 1) * 512], bank(f"zu{g}")[:, :])
                        elif step == "sg0":
                            drained(act, "zu1")
                            f(SG[:, :], SG[:, :], ACT.Gelu_apprx_tanh).then_inc(act_part, 1)
                        split_high(place)
                    mixed_high(DEPTH + l, ["fo0", "fo1"])

                squares(nidx, lambda g: drained(act, f"wm_{l}_{g}"), lambda g: split_after(f"wm_{l}_{g}"))
                norm(nidx)
                split_after(f"wm_{l}_3")
                nidx += 1
                up0 = ffn_base[l]
                w0, b0 = VEC_AT["ffn_conv_w_2"] + l * 3 * 2 * NFF, VEC_AT["ffn_conv_b_2"] + l * 2 * NFF
                n0, q0 = LOAD_NO[("gate", l, 0)], SPLIT_NO[("gate", l, 0)]

                def ffn_high(kind, par, i, when):
                    n = n0 + 3 * par + 2 + kind
                    high_part(n, (q0 + FFN_SLOT[kind]) % SLOTS, when=when, landed=i * 32 + 16 * (n // SLOTS + 1))

                def rounds(par, i, first=False, last=False):
                    gate, value = 2 * par, 2 * par + 1
                    if not last:
                        act_free = i + (up0[gate] + 1)
                        ffn_high(0, par, i, panel_free[SPLIT_KEYS[q0 - 1]] if first and par == 0
                                 else (psum_full[gate], act_free))
                        ffn_high(1, par, i, (psum_full[0], up0[0] + 1) if first and par == 0
                                 else (psum_full[value], i + (up0[value] + 1)))
                    else:
                        n = LOAD_NO[("down", l, FF_ROUNDS - 1)]
                        high_part(n, (q0 + n - n0) % SLOTS, when=(psum_full[0], up0[0] + FF_ROUNDS // 2 + 1))
                    for b in (gate, value):
                        act.wait_ge(psum_full[b], i + (up0[b] + 1))
                    if not (first and l == 0):
                        act.wait_ge(gh_ready, 2 * i + (par - 1) + FF_ROUNDS * l if not first else FF_ROUNDS * l)
                    for half in range(2):
                        for j in range(2):
                            c = 2 * half + j
                            m = i * 4 + (2 * par + j + half * NFF)
                            ins = f(glu[par][:, c, :], ps[2 * par + half][:, j * T:(j + 1) * T], ACT.Identity,
                                    scale=VC[:, bass.ds(m + (w0 + 2 * 2 * NFF), 1)],
                                    bias=VC[:, bass.ds(m + b0, 1)])
                    ins.then_inc(taps_ready, 1)
                    if not last:
                        ffn_high(2, par, i, (psum_full[1], up0[1] + 1) if first and par == 0
                                 else (down_done, 2 * i + (par + (FF_ROUNDS - 1) * l)))
                    act.wait_ge(psum_free[gate], i + (up0[gate] + 1))
                    f(glu[par][:, 0:2, :], glu[par][:, 0:2, :], ACT.Silu).then_inc(silu_ready, 1)
                    act.wait_ge(gf_ready, 2 * i + (par + 1 + FF_ROUNDS * l))
                    nc.scalar.copy(gh3[par], hidden[par]).then_inc(gh_ready, 1)

                rounds(0, 0, first=True)
                rounds(1, 0, first=True)
                with act.Fori(1, FF_ROUNDS // 2) as i:
                    rounds(0, i)
                    rounds(1, i)
                rounds(0, FF_ROUNDS // 2, last=True)
                next_high[0] = q0 + 3 * FF_ROUNDS
                split_after(f"ffn_up{l}")

            squares(nidx, lambda g: drained(act, f"down{g}_1"))
            norm(nidx)
            for g in range(4):
                if g % 2 == 0:
                    copy_out(f"out{g}", FK[:, g * 512:(g + 1) * 512], bank(f"out{g}")[:, :])
            for g in range(4):
                n, c0 = g % 2, 512 * (g // 2)
                if n == 0:
                    drained(act, f"out{g}")
                    act.dma_start(out[0, n * P:(n + 1) * P, c0:c0 + 512],
                                  FK[:, g * 512:(g + 1) * 512]).then_inc(out_stored, 16)
            act.wait_ge(out_stored, 16 * 4)

        @block.vector
        def _(dve):
            steps = [0]
            V = nc.vector

            def step(ins):
                steps[0] += 1
                ins.then_inc(dve_step, 1)

            def settle():
                dve.wait_ge(dve_step, steps[0])

            def link(ins):
                step(ins)
                settle()

            def wide(col, shape):
                return col.to_broadcast(shape)

            def normed(nidx, gain, g0):
                dve.wait_ge(rinv_ready, nidx + 1)
                if nidx > 0:
                    full(dve, normed_last[nidx - 1])
                def chunk_low(c):
                    dve.wait_ge(xh_ready, 8 * nidx + c + 1)
                    V.tensor_tensor(xl3[:, c, :], xf3[:, c, :], xh3[:, c, :].bitcast(F32),
                                    ALU.subtract).then_inc(xn_ready, 1)

                for c in range(ND):
                    V.scalar_tensor_tensor(xf3[:, c, :], h3[:, c, :], vec(gain, g0 + c), RINV[:, :],
                                           ALU.mult, ALU.mult).then_inc(xf_ready, 1)
                    if nidx < 4 * DEPTH and c > 0:
                        chunk_low(c - 1)
                if nidx < 4 * DEPTH:
                    chunk_low(ND - 1)

            def mixed_low(m, i):
                s = slice(i * 512, (i + 1) * 512)
                dve.wait_ge(yh_ready, 4 * m + i + 1)
                V.tensor_tensor(XL[:, s], Y[:, s], XH[:, s].bitcast(F32), ALU.subtract).then_inc(y_ready, 1)

            def low_part(n, slot, count, size=PANEL):
                dve.wait_ge(high_ready, count)
                V.tensor_tensor(low_slots[slot][:, 0:size], raw[n % SLOTS][:, 0:size], high_slots[slot][:, 0:size].bitcast(F32),
                                ALU.subtract).then_inc(low_ready, 1)

            next_low = [0]

            def split_low(place, most=len(SPLIT_KEYS)):
                while next_low[0] < most and next_low[0] in high_from and high_from[next_low[0]] <= place:
                    q = next_low[0]
                    n = LOAD_NO[SPLIT_KEYS[q]]
                    low_part(n, q % SLOTS, q + 1, panel_size(n))
                    next_low[0] += 1

            def split_after(name):
                split_low(order_of[name])

            def row_max(tag, u, pidx):
                bb = pidx % 2
                for n, x in ((0, "Y"), (1, "X")):
                    full(dve, f"{tag}{x}{u}")
                    s3 = bank(f"{tag}{x}{u}")[:, 0:2 * (n + 1) * P].rearrange("p (r s) -> p r s", r=2)
                    ins = V.tensor_reduce(NM[:, 4 * bb + 2 * n:4 * bb + 2 * n + 2], s3, AX_X, ALU.max, negate=True)
                ins.then_inc(nmax_ready, 1)

            def normalise(tag, u, pidx, gate=None):
                bb = pidx % 2
                s4 = SM[:, 4 * bb:4 * bb + 4]
                drained(dve, f"{tag}X{u}")
                link(V.tensor_scalar(s4, s4, 1e-30, None, ALU.max))
                link(V.reciprocal(s4, s4))
                if gate is not None:
                    link(V.tensor_tensor(s4.rearrange("p (n r) -> p n r", n=NT),
                                         s4.rearrange("p (n r) -> p n r", n=NT), gate, ALU.mult))
                for n in range(NT):
                    w = (n + 1) * P
                    ins = V.tensor_tensor(probs[bb][n], probs[bb][n],
                                          s4[:, 2 * n:2 * n + 2].unsqueeze(2).to_broadcast([P, 2, w]), ALU.mult)
                ins.then_inc(p_ready, 1)

            def add_out(prefix, suffix=""):
                for g in range(4):
                    name = f"{prefix}{g}{suffix}"
                    full(dve, name)
                    s = slice(g * 512, (g + 1) * 512)
                    V.tensor_tensor(H[:, s], H[:, s], bank(name)[:, :], ALU.add).then_inc(free(name), 1)
                    if g < 3:
                        split_after(name)

            V.memset(EPSC[:, 0:1], EPS)
            V.memset(EPSC[:, 1:2], 1.0).then_inc(eps_ready, 1)
            for t in (AD, KZ, KCZ):
                V.memset(t[:, :], 0.0)
            step(V.memset(ZR[:, :], 0.0))
            dve.wait_ge(const_landed, 16)
            V.tensor_copy(IDB[:, :], ident)
            step(V.tensor_copy(NGB[:, :], const("causal_neg")))
            for g in range(4):
                full(dve, f"x{g}")
                V.tensor_copy(H[:, g * 512:(g + 1) * 512], bank(f"x{g}")[:, :]).then_inc(free(f"x{g}"), 1)
            settle()
            for g in range((NVT + 3) // 4):
                drained(dve, f"vec{g}")
            split_low(-1, 2)
            normed(0, "norm_g", 0)
            split_low(-1)
            lb = vec("hgrn_lb", 0, 8)
            mx, e = LB[:, 16:20], SPC[:, 8:16]
            link(V.tensor_tensor(mx, lb[:, 0:4], lb[:, 4:8], ALU.max))
            for l in range(DEPTH):
                V.tensor_tensor(e[:, 4 * l:4 * l + 4], lb[:, 4 * l:4 * l + 4], mx, ALU.subtract)
            lam = vec("lru_lambda_2", 0, 4)
            V.scalar_tensor_tensor(SPC[:, 16:20], lam, -1.0, lam, ALU.mult, ALU.min).then_inc(dve_part, 1)
            V.tensor_scalar(GQ[:, :], vec("nsa_qnorm_g", 0, 2), 0.125, None, ALU.mult)
            dve.wait_ge(act_part, 1)
            link(V.tensor_tensor(mx, e[:, 0:4], e[:, 4:8], ALU.add))
            link(V.reciprocal(mx, mx))
            for l in range(DEPTH):
                step(V.tensor_tensor(e[:, 4 * l:4 * l + 4], e[:, 4 * l:4 * l + 4], mx, ALU.mult))
            settle()
            V.tensor_tensor(LB[:, 0:4], e[:, 0:4], e[:, 0:4], ALU.subtract)
            link(V.tensor_tensor(LB[:, 4:8], e[:, 0:4], e[:, 4:8], ALU.add))
            link(V.tensor_tensor(LB[:, 4:8], LB[:, 4:8], e[:, 0:4], ALU.subtract))
            link(V.tensor_scalar(LB[:, 8:16], LB[:, 0:8], -1.0, 1.0, ALU.mult, ALU.add))

            for l in range(DEPTH):
                if l > 0:
                    normed(2 * l, "norm_g", 8 * l)
                    split_after(f"pg3_{l - 1}")
                for g in range(2):
                    drained(dve, f"hf{g}_{l}")
                    split_after(f"hf{g}_{l}")
                for c in range(4):
                    low, rest = LB[:, 4 * l + c:4 * l + c + 1], LB[:, 8 + 4 * l + c:8 + 4 * l + c + 1]
                    s = slice(c * T, (c + 1) * T)
                    step(V.tensor_scalar(FG[:, s], FG[:, s], rest, low, ALU.mult, ALU.add))
                    ins = V.tensor_scalar(KQ[:, s], KQ[:, s], rest, None, ALU.mult)
                ins.then_inc(hg_ready, 1)

                def level(n, g):
                    name = f"lv{n}_{g}_{l}"
                    full(dve, name)
                    if n == 0:
                        dve.wait_ge(masks_landed, 16)
                    V.copy_predicated(AD[:, g * 512:(g + 1) * 512].rearrange("p (j t) -> p j t", j=4),
                                      v3(LM, NLVL)[:, n:n + 1, :].to_broadcast([P, 4, P]),
                                      v3(bank(name), 4)).then_inc(free(name), 1)
                    q, k = QP[:, g * 512:(g + 1) * 512], KQ[:, g * 512:(g + 1) * 512]
                    if n == 0:
                        settle()
                        V.tensor_tensor(q, q, FG[:, g * 512:(g + 1) * 512], ALU.mult).then_inc(level_ready, 1)
                        return
                    dve.wait_ge(level_ready, 16 * l + 2 * (n - 1) + g + 1)
                    h = 1 << (n - 1)
                    nb = 512 // (2 * h)
                    f_in = flevel[n - 1][:, g * (512 >> (n - 1)):(g + 1) * (512 >> (n - 1))]
                    f_in = f_in.rearrange("p (b e) -> p b e", e=2)
                    q = q.rearrange("p (b e t) -> p b e t", e=2, t=h)
                    k = k.rearrange("p (b e t) -> p b e t", e=2, t=h)
                    settle()
                    if n < NLVL - 1:
                        f_out = flevel[n][:, g * (512 >> n):(g + 1) * (512 >> n)]
                        step(V.tensor_tensor(f_out, f_in[:, :, 0], f_in[:, :, 1], ALU.mult))
                    V.tensor_tensor(q[:, :, 1, :], q[:, :, 1, :], f_in[:, :, 0:1].to_broadcast([P, nb, h]), ALU.mult)
                    V.tensor_tensor(k[:, :, 0, :], k[:, :, 0, :], f_in[:, :, 1:2].to_broadcast([P, nb, h]),
                                    ALU.mult).then_inc(level_ready, 1)

                for g in range(2):
                    split_after(f"hq{g}_{l}")
                split_after(f"hi{NT - 1}_{l}")
                for place, kind, *arg in agenda[l]:
                    if kind == "level":
                        level(*arg)
                    elif kind == "blocks":
                        drained(dve, f"kcvc_{l}")
                        pe3 = vec("cmp_pe", 32 * l, 32).rearrange("p (kv jj) -> p kv jj", kv=2)
                        V.memset(M2[:, :, :, :, NCMP:16], 0.0)
                        for kv in range(2):
                            for g in range(2):
                                src = K2[:, kv, g, 0:T].rearrange("p (c jj two) -> p jj c two", jj=8, two=2)
                                for hi in range(2):
                                    ins = V.tensor_tensor(
                                        M2[:, kv, 8 * hi:8 * hi + 8, g, 0:NCMP],
                                        src[:, :, hi:hi + NCMP, 0],
                                        pe3[:, kv, 8 * hi:8 * hi + 8].unsqueeze(2).to_broadcast([P, 8, NCMP]),
                                        ALU.add)
                        ins.then_inc(blocks_ready, 1)
                    elif kind == "gates":
                        drained(dve, f"vw_{l}")
                        link(V.tensor_scalar(GT[:, :], GT[:, :], 1.0, None, ALU.add))
                        V.reciprocal(GT[:, :], GT[:, :]).then_inc(gates_ready, 1)
                    elif kind == "q_norm":
                        dve.wait_ge(q_rinv_ready, l + 1)
                        link(V.scalar_tensor_tensor(QN[:, :], QN[:, :], GQ[:, l:l + 1], HZ[:, :],
                                                    ALU.mult, ALU.mult))
                        qn4 = v3(QN, 4)
                        for i, tab in enumerate(("cos", "sin")):
                            ins = V.tensor_tensor(UW[:, i * 1024:(i + 1) * 1024].rearrange("p (j t) -> p j t", j=4),
                                                  qn4, const(tab).unsqueeze(1).to_broadcast([P, 4, T]), ALU.mult)
                        ins.then_inc(rope_ready, 1)
                    elif kind == "k_norm":
                        dve.wait_ge(k_rinv_ready, l + 1)
                        for j in range(2):
                            s = slice(j * T, (j + 1) * T)
                            step(V.scalar_tensor_tensor(KN[:, s], KN[:, s], vec("nsa_knorm_g", 3 * l + 1 + j),
                                                        UK[:, 512 + j * T:512 + (j + 1) * T], ALU.mult, ALU.mult))
                        settle()
                        for i, tab in enumerate(("cos", "sin")):
                            ins = V.tensor_tensor(UK[:, i * 512:(i + 1) * 512].rearrange("p (j t) -> p j t", j=2),
                                                  v3(KN, 2), const(tab).unsqueeze(1).to_broadcast([P, 2, T]),
                                                  ALU.mult)
                        ins.then_inc(k_rope_ready, 1)
                    elif kind == "hidden":
                        dve.wait_ge(hid_exp_ready, l + 1)
                        link(V.tensor_scalar(SS[:, 0:64], SS[:, 0:64], 1.0, None, ALU.add))
                        link(V.reciprocal(SS[:, 0:64], SS[:, 0:64]))
                        V.tensor_tensor(HID[:, :], bank(f"hid_{l}")[:, 0:64], SS[:, 0:64],
                                        ALU.mult).then_inc(free(f"hid_{l}"), 1)
                        drained(dve, f"hid_{l}")
                        V.tensor_copy(HIDV[:, :].rearrange("p (g r c) -> p g r c", g=2, r=4),
                                      HID[:, 32:64].rearrange("p (g c) -> p g c", g=2).unsqueeze(2)
                                      .to_broadcast([P, 2, 4, 16])).then_inc(hidden_ready, 1)
                    elif kind == "cmp_kv":
                        full(dve, f"vc_{l}")
                        V.tensor_tensor(v3(VCB, 8), const("head16").unsqueeze(2).to_broadcast([P, 8, 64]),
                                        bank(f"vc_{l}")[:, 0:64].unsqueeze(1).to_broadcast([P, 8, 64]),
                                        ALU.mult).then_inc(free(f"vc_{l}"), 1)
                    elif kind == "kc_norm":
                        dve.wait_ge(kc_rinv_ready, l + 1)
                        for r in range(2):
                            h = slice(64 * r, 64 * r + 64)
                            ins = V.scalar_tensor_tensor(KCZ[h, 32 * r:32 * r + 32], KC[h, 0:32],
                                                         vec("nsa_knorm_g", 3 * l)[h, :], SS[h, 64:96],
                                                         ALU.mult, ALU.mult)
                        ins.then_inc(kc_ready, 1)
                    elif kind == "o_norm":
                        dve.wait_ge(o_rinv_ready, l + 1)
                        step(V.scalar_tensor_tensor(QP[:, :], QP[:, :], vec("hgrn_onorm_g", l), UK[:, :],
                                                    ALU.mult, ALU.mult))
                    elif kind == "cmp_softmax":
                        name = f"cs_{l}"
                        full(dve, name)
                        s4 = SC[:, :].rearrange("p (n h c) -> p n h c", n=NT, h=8)
                        s3 = SC[:, :].rearrange("p (q c) -> p q c", c=16)
                        r2 = SS[:, 96:112]

                        def by_tile(tab):
                            return const(tab).rearrange("p (n c) -> p n c", n=NT).unsqueeze(2) \
                                .to_broadcast([P, NT, 8, 16])

                        V.tensor_tensor(s4, by_tile("cmp_neg"),
                                        bank(name)[:, 0:256].rearrange("p (n h c) -> p n h c", n=NT, h=8),
                                        ALU.add).then_inc(free(name), 1)
                        drained(dve, name)
                        link(V.tensor_reduce(r2, s3, AX_X, ALU.max))
                        V.tensor_tensor(s3, s3, r2.unsqueeze(2).to_broadcast([P, 16, 16]),
                                        ALU.subtract).then_inc(cmp_shift_ready, 1)
                        dve.wait_ge(cmp_exp_ready, l + 1)
                        link(V.tensor_tensor(s4, s4, by_tile("cmp_seen"), ALU.mult))
                        link(V.tensor_reduce(r2, s3, AX_X, ALU.add))
                        link(V.tensor_scalar(r2, r2, 1e-30, None, ALU.max))
                        link(V.reciprocal(r2, r2))
                        link(V.tensor_tensor(r2.rearrange("p (n h) -> p n h", n=NT),
                                             r2.rearrange("p (n h) -> p n h", n=NT), gates[:, :, 0:8], ALU.mult))
                        V.tensor_tensor(s3, s3, r2.unsqueeze(2).to_broadcast([P, 16, 16]),
                                        ALU.mult).then_inc(cp_ready, 1)
                    elif kind == "scores":
                        row_max(f"n{l}", arg[0], 8 * l + arg[0])
                    elif kind == "normalise":
                        u = arg[0]
                        g0 = 8 * (u // 4 + 1) + 2 * (u % 4)
                        normalise(f"n{l}", u, 8 * l + u, gates[:, :, g0:g0 + 2])
                    elif kind == "mix":
                        for i, t in enumerate((FG, SG)):
                            dve.wait_ge(sig_ready, 3 * l + i + 1)
                            link(V.tensor_tensor(HZ[:, :], HZ[:, :], t[:, :], ALU.mult))
                        for g in range(2):
                            s = slice(g * 512, (g + 1) * 512)
                            V.tensor_tensor(Y[:, s], QP[:, s], HZ[:, s], ALU.mult).then_inc(yf_ready, 1)
                    elif kind == "on":
                        mixed_low(l, 0)
                        mixed_low(l, 1)
                        dve.wait_ge(sig_ready, 3 * l + 3)
                        link(V.tensor_tensor(NZ[:, :], NZ[:, :], VH[:, :], ALU.mult))
                        for g in range(2):
                            name = f"on{g}_{l}"
                            full(dve, name)
                            V.tensor_tensor(Y[:, 1024 + g * 512:1024 + (g + 1) * 512], bank(name)[:, :],
                                            NZ[:, g * 512:(g + 1) * 512], ALU.mult).then_inc(free(name), 1)
                            mixed_low(l, 2 + g)
                    if kind not in ("level", "k_pad"):
                        split_low(place)
                add_out(f"wo_{l}_")
                normed(2 * l + 1, "ple_norm_g", 8 * l)
                split_after(f"pp3_{l}")
                for g in range(4):
                    drained(dve, f"pg{g}_{l}")
                    drained(dve, f"pp{g}_{l}")
                    s = slice(g * 512, (g + 1) * 512)
                    link(V.tensor_tensor(Y[:, s], Y[:, s], PP[:, s], ALU.mult))
                    V.tensor_tensor(H[:, s], H[:, s], Y[:, s], ALU.add).then_inc(h_ready, 1)
                    if g < 3:
                        split_after(f"pg{g}_{l}")

            z, s, s2, q = SPC[:, 16:20], SPC[:, 20:24], SPC[:, 24:28], SPC[:, 28:32]
            link(V.tensor_scalar(s, z, 2.0, None, ALU.add))
            link(V.reciprocal(s, s))
            link(V.tensor_tensor(s, s, z, ALU.mult))
            link(V.tensor_tensor(s2, s, s, ALU.mult))
            link(V.tensor_scalar(q, s2, 1.0 / 19, None, ALU.mult))
            for k in range(17, 1, -2):
                link(V.scalar_tensor_tensor(q, q, 1.0 / k, s2, ALU.add, ALU.mult))
            link(V.tensor_scalar(q, q, 1.0, 2.0, ALU.add, ALU.mult))
            link(V.tensor_tensor(q, q, s, ALU.mult))
            link(V.tensor_scalar(s, vec("lru_lambda_2", 0, 4), -1.0, 0.0, ALU.mult, ALU.max))
            link(V.tensor_tensor(q, q, s, ALU.add))
            V.tensor_scalar(SPC[:, 0:4], q, -8.0, None, ALU.mult)
            V.tensor_scalar(SPC[:, 4:8], q, 8.0, None, ALU.mult).then_inc(small_ready, 1)

            nidx = 2 * DEPTH
            for l in range(DEPTH):
                if l == 0:
                    normed(nidx, "mix0_norm_2", 0)
                    split_after(f"pg3_{DEPTH - 1}")
                    V.memset(PB[:, 0:1024], 0.0).then_inc(bd_zeroed, 1)

                    def taps(name, g, src, dst, wname, n):
                        for back in range(1, n):
                            for j in range(2):
                                c = 2 * g + j
                                d = dst[:, c * T + back:(c + 1) * T]
                                ins = V.scalar_tensor_tensor(d, src(j)[:, 0:T - back],
                                                             vec(wname, 4 * (n - 1 - back) + c), d,
                                                             ALU.mult, ALU.add)
                                if back < n - 1 or j == 0:
                                    step(ins)
                            settle()
                        return ins

                    for g in range(2):
                        dve.wait_ge(conv_ready, g + 1)
                        src = bank(f"xa{g}")
                        taps(f"xa{g}", g, lambda j: src[:, j * T:(j + 1) * T], FG, "lru_conv_w_2",
                             4).then_inc(free(f"xa{g}"), 1)
                        split_after(f"xa{g}")
                    for g in range(2):
                        drained(dve, f"ga{g}")
                        split_after(f"ga{g}")
                    drained(dve, "li1")
                    link(V.tensor_tensor(NZ[:, :], NZ[:, :], FG, ALU.mult))
                    dve.wait_ge(act_part, 3)
                    link(V.tensor_tensor(UW[:, 0:1024], QN[:, :], QN[:, :], ALU.mult))
                    V.scalar_tensor_tensor(QR[:, :], UW[:, 0:1024], 1.0, QR[:, :], ALU.add,
                                           ALU.mult).then_inc(dve_part, 1)
                    dve.wait_ge(act_part, 4)
                    link(V.tensor_tensor(QR[:, :], QR[:, :], NZ[:, :], ALU.mult))
                    for c in range(4):
                        s = slice(c * T, (c + 1) * T)
                        step(V.tensor_tensor_scan(UW[:, 1024 + c * T:1024 + (c + 1) * T], QN[:, s], QR[:, s], 0.0,
                                                  ALU.mult, ALU.add))
                    settle()
                    for g in range(2):
                        s = slice(g * 512, (g + 1) * 512)
                        V.tensor_tensor(Y[:, s], UW[:, 1024 + g * 512:1024 + (g + 1) * 512], SG[:, s],
                                        ALU.mult).then_inc(yf_ready, 1)
                    for g in range(2):
                        full(dve, f"cp{g}")
                        split_after(f"cp{g}")
                    for g in range(2):
                        drained(dve, f"cp{g}")
                        full(dve, f"vb{g}")
                        V.tensor_tensor(QP[:, g * 512:(g + 1) * 512], bank(f"vb{g}")[:, :],
                                        KQ[:, g * 512:(g + 1) * 512], ALU.mult).then_inc(free(f"vb{g}"), 1)
                        split_after(f"vb{g}")
                    for g in range(2):
                        dve.wait_ge(conv_ready, 3 + g)
                        step(taps(None, g, lambda j: QP[:, (2 * g + j) * T:(2 * g + j + 1) * T], AD,
                                  "sconv_w_2", 3))
                    settle()
                    for g in range(2):
                        full(dve, f"bp{g}")
                        V.tensor_tensor(Y[:, 1024 + g * 512:1024 + (g + 1) * 512], bank(f"bp{g}")[:, :],
                                        AD[:, g * 512:(g + 1) * 512], ALU.mult).then_inc(free(f"bp{g}"), 1)
                        if g == 0:
                            split_after("bp0")
                    for i in range(4):
                        mixed_low(DEPTH, i)
                    split_after("bp1")
                else:
                    normed(nidx, "mix1_norm_2", 0)
                    split_after("down3_0")
                    for name in ("fq0", "fq1", "fk0", "fk1"):
                        split_after(name)
                    dve.wait_ge(bias_landed, 16)
                    full(dve, "fl")
                    V.tensor_scalar(SC[0:8, :], bank("fl")[0:8, 0:T], BF[0:8, 0:1], None,
                                    ALU.add).then_inc(free("fl"), 1)
                    drained(dve, "fl")
                    V.scalar_tensor_tensor(SS[0:8, :], SC[0:8, :], -1.0, SC[0:8, :], ALU.mult,
                                           ALU.min).then_inc(dve_part, 1)
                    link(V.tensor_scalar(SC[0:8, :], SC[0:8, :], 0.0, None, ALU.min))
                    dve.wait_ge(act_part, 5)
                    link(V.tensor_tensor(SC[0:8, :], SS[0:8, :], SC[0:8, :], ALU.subtract))
                    link(V.tensor_tensor_scan(PCT[0:8, :], ones[0:8, 0:1].to_broadcast([8, T]), SC[0:8, :], 0.0,
                                              ALU.mult, ALU.add))
                    V.tensor_tensor(UW[0:8, :].rearrange("p (h t) -> p h t", h=8),
                                    PCT[0:8, :].unsqueeze(1).to_broadcast([8, 8, T]),
                                    ident[0:8, 0:8].unsqueeze(2).to_broadcast([8, 8, T]),
                                    ALU.mult).then_inc(forget_ready, 1)
                    for name in ("fv0", "fv1"):
                        split_after(name)
                    for place, kind, *arg in agenda[DEPTH + l]:
                        if kind == "scores":
                            row_max("f", arg[0], 8 * DEPTH + arg[0])
                        elif kind == "normalise":
                            normalise("f", arg[0], 8 * DEPTH + arg[0])
                        elif kind == "zg":
                            dve.wait_ge(act_part, 6)
                            V.tensor_reduce(NT16[:, :], NZ[:, :].rearrange("p (q d) -> p q d", d=64), AX_X,
                                            ALU.add).then_inc(dve_part, 1)
                        elif kind == "zg_norm":
                            dve.wait_ge(act_part, 7)
                            V.tensor_tensor(QN[:, :].rearrange("p (q d) -> p q d", d=64),
                                            QN[:, :].rearrange("p (q d) -> p q d", d=64),
                                            NT16[:, :].unsqueeze(2).to_broadcast([P, 16, 64]),
                                            ALU.mult).then_inc(sgu_ready, 1)
                        elif kind == "wt":
                            for g in range(2):
                                full(dve, f"wt{g}")
                                V.tensor_tensor(AD[:, g * 512:(g + 1) * 512].rearrange("p (j t) -> p j t", j=4),
                                                v3(bank(f"wt{g}"), 4),
                                                const("upper").unsqueeze(1).to_broadcast([P, 4, P]),
                                                ALU.mult).then_inc(free(f"wt{g}"), 1)
                        elif kind in ("sg0", "sg1"):
                            g = int(kind[2])
                            full(dve, kind)
                            if g == 0:
                                dve.wait_ge(bt_landed, 16 * 8)
                            for j in range(2):
                                c = 2 * g + j
                                ins = V.scalar_tensor_tensor(
                                    v3(HZ, 4)[:, c, :].rearrange("p (n t) -> p n t", n=NT),
                                    bank(kind)[:, j * T:(j + 1) * T].rearrange("p (n t) -> p n t", n=NT),
                                    vec("sgu_norm_2", c), v3(AC, 4)[:, c:c + 1, :].to_broadcast([P, NT, P]),
                                    ALU.mult, ALU.add)
                            ins.then_inc(free(kind), 1)
                        split_low(place)
                    drained(dve, "sg1")
                    dve.wait_ge(act_part, 8)
                    for g in range(2):
                        s = slice(g * 512, (g + 1) * 512)
                        V.tensor_tensor(Y[:, s], HZ[:, s], SG[:, s], ALU.mult).then_inc(yf_ready, 1)
                    for g in range(2):
                        full(dve, f"fo{g}")
                        V.tensor_copy(Y[:, 1024 + g * 512:1024 + (g + 1) * 512],
                                      bank(f"fo{g}")[:, :]).then_inc(free(f"fo{g}"), 1)
                    for i in range(4):
                        mixed_low(DEPTH + l, i)
                nidx += 1
                add_out(f"wm_{l}_")

                normed(nidx, "ffn_norm_2", 8 * l)
                split_after(f"wm_{l}_3")
                nidx += 1
                w0 = VEC_AT["ffn_conv_w_2"] + l * 3 * 2 * NFF

                n0, q0, up0 = LOAD_NO[("gate", l, 0)], SPLIT_NO[("gate", l, 0)], ffn_base[l]

                def ffn_low(kind, par, i):
                    low_part(n0 + 3 * par + 2 + kind, (q0 + FFN_SLOT[kind]) % SLOTS, 6 * i + (q0 + 3 * par + 3 + kind))

                def rounds(par, i, last=False):
                    if not last:
                        ffn_low(0, par, i)
                        ffn_low(1, par, i)
                    else:
                        n = LOAD_NO[("down", l, FF_ROUNDS - 1)]
                        low_part(n, (q0 + n - n0) % SLOTS, q0 + 3 * FF_ROUNDS)
                    dve.wait_ge(taps_ready, 2 * i + (par + 1 + FF_ROUNDS * l))
                    for back in (1, 2):
                        if back == 2:
                            dve.wait_ge(first_back_done, 2 * i + (par + 1 + FF_ROUNDS * l))
                        for half in range(2):
                            for j in range(2):
                                m = i * 4 + (2 * par + j + half * NFF)
                                d = glu[par][:, 2 * half + j, back:T]
                                ins = V.scalar_tensor_tensor(
                                    d, ps[2 * par + half][:, j * T:(j + 1) * T - back],
                                    VC[:, bass.ds(m + (w0 + (2 - back) * 2 * NFF), 1)], d, ALU.mult, ALU.add)
                            if back == 2:
                                ins.then_inc(psum_free[2 * par + half], 1)
                        if back == 1:
                            ins.then_inc(first_back_done, 1)
                    if not last:
                        ffn_low(2, par, i)
                    dve.wait_ge(psum_free[2 * par + 1], i + (up0[2 * par + 1] + 1))
                    dve.wait_ge(silu_ready, 2 * i + (par + 1 + FF_ROUNDS * l))
                    V.tensor_tensor(hidden[par], glu[par][:, 0:2, :], glu[par][:, 2:4, :],
                                    ALU.mult).then_inc(gf_ready, 1)
                    dve.wait_ge(gh_ready, 2 * i + (par + 1 + FF_ROUNDS * l))
                    V.tensor_tensor(gl3[par], hidden[par], gh3[par].bitcast(F32), ALU.subtract).then_inc(act_ready, 1)

                rounds(0, 0)
                rounds(1, 0)
                with dve.Fori(1, FF_ROUNDS // 2) as i:
                    rounds(0, i)
                    rounds(1, i)
                rounds(0, FF_ROUNDS // 2, last=True)
                next_low[0] = q0 + 3 * FF_ROUNDS
                split_after(f"ffn_up{l}")
                add_out(f"down", f"_{l}")

            normed(nidx, "final_norm_2", 0)
            for g in (1, 3):
                full(dve, f"out{g}")
                V.tensor_copy(FK[:, g * 512:(g + 1) * 512], bank(f"out{g}")[:, :]).then_inc(free(f"out{g}"), 1)

        @block.gpsimd
        def _(pool):
            for tile, r, n, c0, c1, src in vec_dmas[2::3]:
                pool.dma_start(vrows[r:r + n, tile, c0:c1], src).then_inc(pool_vec_landed, 16)

        @block.sync
        def _(sp):
            def slot_empty(n):
                if n >= SLOTS:
                    key = LOADS[n - SLOTS][0]
                    if key in SPLIT_NO:
                        sp.wait_ge(low_ready, SPLIT_NO[key] + 1)
                    else:
                        sp.wait_ge(*panel_free[key])

            def load_panel(n):
                (name, l, *r), src, c0, cols = LOADS[n]
                slot_empty(n)
                w = {"gate": "ffn_up_2", "value": "ffn_up_2", "down": "ffn_down_2"}.get(src, src)
                w = a[w][l % DEPTH if a[w].shape[0] == DEPTH else 0]
                if src == "cmp_w1":
                    w, c0 = w[c0], 0
                elif src in ("gate", "value"):
                    c0 = r[0] * T + (FF if src == "value" else 0)
                elif src == "down":
                    w, c0, cols = w[r[0] * T:(r[0] + 1) * T], 0, D
                nk = w.shape[0] // P
                sp.dma_start(raw[n % SLOTS][:, 0:nk * cols].rearrange("p (k n) -> p k n", k=nk),
                             w[:, c0:c0 + cols].rearrange("(k p) n -> p k n", p=P)).then_inc(panel_landed[n % SLOTS], 16)

            xsrc = a["x"][0].rearrange("(n p) d -> p n d", p=P)
            for h in range(NT):
                sp.dma_start(xt[:, h, :], xsrc[:, h, :]).then_inc(x_landed, 16)
            load_panel(0)
            load_panel(1)
            for tile, r, n, c0, c1, src in vec_dmas[1::3]:
                sp.dma_start(vrows[r:r + n, tile, c0:c1], src).then_inc(vec_landed, 16)
            load_panel(2)
            sp.dma_start(ptok.rearrange("p (l n) d -> p l n d", l=DEPTH),
                         a["p"][:, 0].rearrange("l (n p) d -> p l n d", p=P)).then_inc(p_landed, 16)
            sp.dma_start(LM[:, :], a["mask_table"]).then_inc(masks_landed, 16)
            sp.dma_start(BF[0:8, 0:1], a["fox_bf_2"].rearrange("a h -> h a")).then_inc(bias_landed, 16)

            def ffn(l):
                n0, q0 = LOAD_NO[("gate", l, 0)], SPLIT_NO[("gate", l, 0)]

                def round_loads(par, i):
                    for kind in range(3):
                        n = n0 + 3 * par + 2 + kind
                        sp.wait_ge(low_ready, 6 * i + (q0 + 3 * par + kind))
                        if kind < 2:
                            w = a["ffn_up_2"][l].rearrange("(k p) n -> p k n", p=P)
                            src = w[:, :, bass.ds(i * 512 + ((par + 1) * T + kind * FF), T)]
                        else:
                            src = a["ffn_down_2"][l][bass.ds(i * 512 + par * T, T), :].rearrange(
                                "(k p) n -> p k n", p=P)
                        dst = raw[n % SLOTS].rearrange("p (k n) -> p k n", k=ND if kind < 2 else 2)
                        sp.dma_start(dst, src).then_inc(panel_landed[n % SLOTS], 16)

                for n in range(n0 + 2, n0 + 8):
                    load_panel(n)
                with sp.Fori(1, FF_ROUNDS // 2) as i:
                    round_loads(0, i)
                    round_loads(1, i)
                load_panel(n0 + 3 * FF_ROUNDS - 1)

            for n, (key, *_) in enumerate(LOADS):
                if n >= SLOTS and (len(key) == 2 or key[0] != "down" and key[2] == 0):
                    load_panel(n)
                name, l, *r = key
                if name == "cmp0":
                    if l > 0:
                        b, k = fills[f"vc_{l - 1}"]
                        sp.wait_ge(psum_full[b], k + 1)
                    for c0, kv in ((0, 0), (64, 0), (P, 1)):
                        sp.dma_start(W2[:, c0:c0 + 64], a["cmp_w2"][l, kv]).then_inc(w2_landed, 16)
                if name == "vb0":
                    sp.wait_ge(bd_zeroed, 1)
                    for at, w in ((0, "lru_wa_2"), (512, "lru_wx_2")):
                        src = a[w][0].rearrange("(c r) i j -> r i c j", r=2)
                        for r in range(2):
                            dst = PB[64 * r:64 * r + 64, at:at + 512].rearrange("p (c m) -> p c m", c=4)
                            sp.dma_start(dst[:, :, 64 * r:64 * r + 64], src[r]).then_inc(bd_landed, 16)
                if name == "fk0":
                    sp.dma_start(PT[:, 0:1024].rearrange("p (h s) -> p h s", h=8),
                                 a["sgu_w_2"][0].rearrange("h t s -> t h s")).then_inc(sgu_landed, 16)
                    for h in range(8):
                        r, c = h % 2, h // 2
                        sp.dma_start(AC[64 * r:64 * r + 64, c * P:(c + 1) * P],
                                     a["sgu_b_2"][0, h:h + 1, :].to_broadcast([64, P])).then_inc(bt_landed, 16)
                if name == "value" and r == [0]:
                    ffn(l)
            for g in (1, 3):
                drained(sp, f"out{g}")
                sp.dma_start(out[0, P:2 * P, 512 * (g // 2):512 * (g // 2) + 512],
                             FK[:, g * 512:(g + 1) * 512]).then_inc(out_stored, 16)


_INS = ["x", "p", "norm_g", "w_in", "hgrn_lb", "hgrn_onorm_g", "nsa_qnorm_g", "nsa_knorm_g", "cmp_pe", "cmp_w1",
        "cmp_w2", "w_out", "ple_norm_g", "w_pg", "w_pp", "mix0_norm_2", "mix0_w_in_2", "lru_conv_w_2",
        "lru_conv_b_2", "lru_wa_2", "lru_ba_2", "lru_wx_2", "lru_bx_2", "lru_lambda_2", "sconv_w_2", "sconv_b_2",
        "mix0_w_out_2", "mix1_norm_2", "mix1_w_in_2", "sgu_norm_2", "sgu_w_2", "sgu_b_2", "fox_bf_2",
        "mix1_w_out_2", "ffn_norm_2", "ffn_up_2", "ffn_conv_w_2", "ffn_conv_b_2", "ffn_down_2", "final_norm_2"]


def kernel(**inputs):
    import concourse.bacc as bacc
    from concourse.bass_utils import run_bass_kernel_spmd

    nc = bacc.Bacc("TRN2", target_bir_lowering=False, num_devices=1)
    arrays, args = {}, {}
    table, masks = const_table()
    for name, value in [(n, inputs[n]) for n in _INS] + [("const_table", table), ("mask_table", masks)]:
        v = np.ascontiguousarray(value)
        arrays[f"in_{name}"] = v
        args[name] = nc.dram_tensor(f"in_{name}", v.shape, mybir.dt.from_np(v.dtype), kind="ExternalInput").ap()
    out = nc.dram_tensor("out", (1, T, D), F32, kind="ExternalOutput").ap()
    build(nc, args, out)
    r = run_bass_kernel_spmd(nc, [arrays], core_ids=[0])
    return r.results[0]["out"]
```
